# Optimizing a Trainium2 kernel written in Bass

```python
import jax
import jax.numpy as jnp
from jax import lax
import numpy as np

D_MODEL = 1024
BATCH = 1
SEQ = 512
DEPTH = 2
DEC_BATCH = 8
DEC_SEQ = 4
PAST_LEN = 4096
PAGE_SIZE = 128

N_EVEN = (DEPTH + 1) // 2
N_ODD = DEPTH // 2
RMS_EPS = 1e-6
NEG_INF = -1e30
FORCE_SCORE = 1e30

POOL_WIDTH = D_MODEL // 2
POOL_WINDOWS = (2, 4, 8, 16)
N_POOL_GROUPS = len(POOL_WINDOWS)
POOL_GROUP = POOL_WIDTH // N_POOL_GROUPS
POOL_STATE = max(POOL_WINDOWS) - 1

HEAD_DIM = 64
NSA_HEADS = (D_MODEL - POOL_WIDTH) // HEAD_DIM
NSA_KV_HEADS = 2
NSA_WIDTH = NSA_HEADS * HEAD_DIM
KV_COLS = NSA_KV_HEADS * HEAD_DIM
CMP_BLOCK = 32
CMP_STRIDE = 16
CMP_RATIO = CMP_BLOCK // CMP_STRIDE
SEL_BLOCK = 64
SEL_PER_STRIDE = SEL_BLOCK // CMP_STRIDE
SEL_TOPK = 16
WINDOW = 512
Q_BLOCK = 128
SEL_Q_CHUNK = 32
EVEN_IN = POOL_WIDTH + NSA_WIDTH + 6 * KV_COLS + 3 * NSA_HEADS

LRU_WIDTH = D_MODEL
LRU_BLOCKS = 4
LRU_BLOCK = LRU_WIDTH // LRU_BLOCKS
CONV_WIDTH = 4
LRU_C = 8.0

N_MEM = 256
XATTN_HEADS = 4
XATTN_HEAD_DIM = D_MODEL // XATTN_HEADS

D_FF = -(-(8 * D_MODEL) // (3 * 256)) * 256

kernel_name = 'hybrid_pool_nsa_rglru_decoder_step'

def rmsnorm(x, g):
    xf = x.astype(jnp.float32)
    y = xf * lax.rsqrt(jnp.mean(xf * xf, axis=-1, keepdims=True) + RMS_EPS)
    return (y * g.astype(jnp.float32)).astype(x.dtype)

def cat_rows(past, new):
    return jnp.concatenate([past.astype(new.dtype), new], axis=1)

def gqa_attend(q, k, v, mask):
    b, tq, h, dh = q.shape
    g = k.shape[2]
    qg = q.reshape(b, tq, g, h // g, dh)
    s = jnp.einsum('btgod,bsgd->bgots', qg, k).astype(jnp.float32) * (dh ** -0.5)
    s = jnp.where(mask, s, NEG_INF)
    p = jnp.where(mask, jax.nn.softmax(s, axis=-1), 0.0)
    o = jnp.einsum('bgots,bsgd->btgod', p.astype(v.dtype), v)
    return o.reshape(b, tq, h, dh), p

def pool_mix(u_ext, n_new, start_pos, pool_w, pool_scale):
    b, l, c = u_ext.shape
    p = l - n_new
    off = POOL_STATE + 1
    uf = u_ext.astype(jnp.float32)
    cs = jnp.cumsum(jnp.pad(uf, ((0, 0), (off, 0), (0, 0))), axis=1)
    pos = start_pos + jnp.arange(n_new)
    means = []
    for gi, w in enumerate(POOL_WINDOWS):
        ch = slice(gi * POOL_GROUP, (gi + 1) * POOL_GROUP)
        win_sum = cs[:, off + p:off + p + n_new, ch] - cs[:, off + p - w:off + p + n_new - w, ch]
        cnt = jnp.minimum(pos + 1, w).astype(jnp.float32)[None, :, None]
        means.append(win_sum / cnt)
    d = (jnp.concatenate(means, axis=-1) - uf[:, p:]).reshape(b, n_new, N_POOL_GROUPS, POOL_GROUP)
    y = jnp.einsum('btgc,gcd->btgd', d, pool_w.astype(jnp.float32)).reshape(b, n_new, c)
    return (y * pool_scale.astype(jnp.float32)).astype(u_ext.dtype)

def split_even(z):
    b, t, _ = z.shape
    sizes = [POOL_WIDTH, NSA_WIDTH] + [KV_COLS] * 6 + [3 * NSA_HEADS]
    offsets = [int(o) for o in np.cumsum(sizes)[:-1]]
    parts = jnp.split(z, offsets, axis=-1)
    u = parts[0]
    q = parts[1].reshape(b, t, NSA_HEADS, HEAD_DIM)
    kvs = tuple(pp.reshape(b, t, NSA_KV_HEADS, HEAD_DIM) for pp in parts[2:8])
    gate = jax.nn.sigmoid(parts[8].astype(jnp.float32)).reshape(b, t, NSA_HEADS, 3)
    return u, q, kvs, gate

def compress_kv(k, v, w_ck, w_cv):
    b, l, g, dh = k.shape
    n_sub = -(-l // CMP_STRIDE)
    pad = n_sub * CMP_STRIDE - l
    n_cmp = n_sub - CMP_RATIO + 1

    def block_means(x):
        xs = jnp.pad(x.astype(jnp.float32), ((0, 0), (0, pad), (0, 0), (0, 0)))
        xs = xs.reshape(b, n_sub, CMP_STRIDE, g, dh).sum(axis=2)
        acc = xs[:, :n_cmp]
        for r in range(1, CMP_RATIO):
            acc = acc + xs[:, r:r + n_cmp]
        return acc / CMP_BLOCK

    kc = jnp.einsum('bngd,gde->bnge', block_means(k), w_ck.astype(jnp.float32))
    vc = jnp.einsum('bngd,gde->bnge', block_means(v), w_cv.astype(jnp.float32))
    return kc.astype(k.dtype), vc.astype(v.dtype)

def sel_importance(p, n_sel):
    lead = CMP_RATIO - 1
    span = SEL_PER_STRIDE + CMP_RATIO - 1
    total = SEL_PER_STRIDE * (n_sel - 1) + span
    right = max(total - lead - p.shape[-1], 0)
    pp = jnp.pad(p, [(0, 0)] * (p.ndim - 1) + [(lead, right)])
    stop = SEL_PER_STRIDE * (n_sel - 1) + 1
    out = pp[..., 0:stop:SEL_PER_STRIDE]
    for k in range(1, span):
        out = out + pp[..., k:k + stop:SEL_PER_STRIDE]
    return out

def select_blocks(imp, qpos, n_sel):
    j = jnp.arange(n_sel)[None, :]
    cur = (qpos // SEL_BLOCK)[:, None]
    valid = j * SEL_BLOCK <= qpos[:, None]
    forced = (j == 0) | (j == cur) | (j == cur - 1)
    score = jnp.where(forced, FORCE_SCORE, jnp.where(valid, imp, NEG_INF))
    _, idx = lax.top_k(score, min(SEL_TOPK, n_sel))
    return idx

def gather_blocks(blocks, idx):
    return jax.vmap(jax.vmap(lambda blk, ix: blk[ix]))(blocks, idx)

def selected_attend(q, qpos, kb, vb, idx):
    b, tq, h, dh = q.shape
    g = kb.shape[1]
    n_top = idx.shape[-1]
    kg = gather_blocks(kb, idx)
    vg = gather_blocks(vb, idx)
    qg = q.reshape(b, tq, g, h // g, dh)
    s = jnp.einsum('btgod,bgtksd->bgotks', qg, kg).astype(jnp.float32) * (dh ** -0.5)
    kpos = idx[..., None] * SEL_BLOCK + jnp.arange(SEL_BLOCK)
    mask = (kpos <= qpos[None, None, :, None, None])[:, :, None]
    s = jnp.where(mask, s, NEG_INF).reshape(b, g, h // g, tq, n_top * SEL_BLOCK)
    p = jax.nn.softmax(s, axis=-1).reshape(b, g, h // g, tq, n_top, SEL_BLOCK)
    p = jnp.where(mask, p, 0.0)
    o = jnp.einsum('bgotks,bgtksd->btgod', p.astype(vg.dtype), vg)
    return o.reshape(b, tq, h, dh)

def selected_attend_chunked(q, qpos, kb, vb, idx):
    b, t, h, dh = q.shape
    g, n_top = idx.shape[1], idx.shape[-1]
    n = t // SEL_Q_CHUNK
    qc = q.reshape(b, n, SEL_Q_CHUNK, h, dh).transpose(1, 0, 2, 3, 4)
    ic = idx.reshape(b, g, n, SEL_Q_CHUNK, n_top).transpose(2, 0, 1, 3, 4)
    pc = qpos.reshape(n, SEL_Q_CHUNK)
    out = lax.map(lambda a: selected_attend(a[0], a[2], kb, vb, a[1]), (qc, ic, pc))
    return out.transpose(1, 0, 2, 3, 4).reshape(b, t, h, dh)

def nsa_compressed_selected(q, qpos, kc, vc, ks, vs, w_ck, w_cv, chunked):
    b, l, g, dh = ks.shape
    kcmp, vcmp = compress_kv(kc, vc, w_ck, w_cv)
    cmp_end = jnp.arange(kcmp.shape[1]) * CMP_STRIDE + CMP_BLOCK - 1
    o_cmp, p_cmp = gqa_attend(q, kcmp, vcmp, cmp_end[None, :] <= qpos[:, None])
    n_sel = -(-l // SEL_BLOCK)
    idx = select_blocks(sel_importance(p_cmp.sum(axis=2), n_sel), qpos, n_sel)
    pad = ((0, 0), (0, n_sel * SEL_BLOCK - l), (0, 0), (0, 0))
    kb = jnp.pad(ks, pad).reshape(b, n_sel, SEL_BLOCK, g, dh).transpose(0, 3, 1, 2, 4)
    vb = jnp.pad(vs, pad).reshape(b, n_sel, SEL_BLOCK, g, dh).transpose(0, 3, 1, 2, 4)
    if chunked:
        o_slc = selected_attend_chunked(q, qpos, kb, vb, idx)
    else:
        o_slc = selected_attend(q, qpos, kb, vb, idx)
    return o_cmp, o_slc

def window_mask(qpos, kpos):
    d = qpos[:, None] - kpos[None, :]
    return (d >= 0) & (d < WINDOW) & (kpos[None, :] >= 0)

def window_attend_banded(q, kw, vw):
    b, t, h, dh = q.shape
    pad = ((0, 0), (WINDOW, 0), (0, 0), (0, 0))
    kp, vp = jnp.pad(kw, pad), jnp.pad(vw, pad)

    def one_block(i):
        q0 = i * Q_BLOCK
        qb = lax.dynamic_slice_in_dim(q, q0, Q_BLOCK, axis=1)
        kb = lax.dynamic_slice_in_dim(kp, q0, WINDOW + Q_BLOCK, axis=1)
        vb = lax.dynamic_slice_in_dim(vp, q0, WINDOW + Q_BLOCK, axis=1)
        qpos = q0 + jnp.arange(Q_BLOCK)
        kpos = q0 - WINDOW + jnp.arange(WINDOW + Q_BLOCK)
        return gqa_attend(qb, kb, vb, window_mask(qpos, kpos))[0]

    out = lax.map(one_block, jnp.arange(t // Q_BLOCK))
    return out.transpose(1, 0, 2, 3, 4).reshape(b, t, h, dh)

def even_mixer(h, past, start_pos, w_in, pool_w, pool_scale, w_ck, w_cv, w_out):
    b, t, _ = h.shape
    u, q, (kc, vc, ks, vs, kw, vw), gate = split_even(h @ w_in)
    qpos = start_pos + jnp.arange(t)
    if past is None:
        u_ext, kc_f, vc_f, ks_f, vs_f = u, kc, vc, ks, vs
    else:
        u_ext = cat_rows(past[0], u)
        kc_f, vc_f = cat_rows(past[1], kc), cat_rows(past[2], vc)
        ks_f, vs_f = cat_rows(past[3], ks), cat_rows(past[4], vs)
    a_out = pool_mix(u_ext, t, start_pos, pool_w, pool_scale)
    o_cmp, o_slc = nsa_compressed_selected(q, qpos, kc_f, vc_f, ks_f, vs_f, w_ck, w_cv, past is None)
    if past is None:
        n_keep = min(WINDOW, t)
        kw_ext, vw_ext = kw, vw
        o_win = window_attend_banded(q, kw, vw)
    else:
        n_keep = past[5].shape[1]
        kw_ext, vw_ext = cat_rows(past[5], kw), cat_rows(past[6], vw)
        kpos = start_pos - n_keep + jnp.arange(n_keep + t)
        o_win = gqa_attend(q, kw_ext, vw_ext, window_mask(qpos, kpos))[0]
    o_nsa = gate[..., 0:1] * o_cmp + gate[..., 1:2] * o_slc + gate[..., 2:3] * o_win
    mixed = jnp.concatenate([a_out, o_nsa.astype(h.dtype).reshape(b, t, NSA_WIDTH)], axis=-1) @ w_out
    new_state = (u_ext[:, -POOL_STATE:], kc, vc, ks, vs, kw_ext[:, -n_keep:], vw_ext[:, -n_keep:])
    return mixed, new_state

def odd_mixer(h, conv_past, h_past, start_pos, w_in, conv_w, conv_b, wa, ba, wx, bx, lam, w_out):
    b, t, _ = h.shape
    z = h @ w_in
    xb, yb = z[..., :LRU_WIDTH], z[..., LRU_WIDTH:]
    xe = cat_rows(conv_past, xb)
    xc = xe[:, 0:t] * conv_w[0]
    for k in range(1, CONV_WIDTH):
        xc = xc + xe[:, k:k + t] * conv_w[k]
    xf = (xc + conv_b).astype(jnp.float32)
    blocks = xf.reshape(b, t, LRU_BLOCKS, LRU_BLOCK)
    r = jax.nn.sigmoid(jnp.einsum('btnc,ncd->btnd', blocks, wa.astype(jnp.float32)).reshape(b, t, LRU_WIDTH) + ba.astype(jnp.float32))
    i = jax.nn.sigmoid(jnp.einsum('btnc,ncd->btnd', blocks, wx.astype(jnp.float32)).reshape(b, t, LRU_WIDTH) + bx.astype(jnp.float32))
    log_a = -LRU_C * r * jax.nn.softplus(-lam.astype(jnp.float32))
    a = jnp.exp(log_a)
    pos = start_pos + jnp.arange(t)
    mult = jnp.where((pos == 0)[None, :, None], 1.0, jnp.sqrt(-jnp.expm1(2.0 * log_a)))
    drive = mult * i * xf

    def step(carry, inp):
        a_t, d_t = inp
        carry = a_t * carry + d_t
        return carry, carry

    h_last, hs = lax.scan(step, h_past.astype(jnp.float32), (jnp.swapaxes(a, 0, 1), jnp.swapaxes(drive, 0, 1)))
    y = (jnp.swapaxes(hs, 0, 1) * jax.nn.gelu(yb.astype(jnp.float32))).astype(h.dtype) @ w_out
    return y, xe[:, -(CONV_WIDTH - 1):], h_last.astype(h.dtype)

def memory_kv(mem, g, wk, wv):
    b, m, _ = mem.shape
    mn = rmsnorm(mem, g)
    k = (mn @ wk).reshape(b, m, XATTN_HEADS, XATTN_HEAD_DIM)
    v = (mn @ wv).reshape(b, m, XATTN_HEADS, XATTN_HEAD_DIM)
    return k, v

def cross_attend(h, mk, mv, wq, wo):
    b, t, _ = h.shape
    q = (h @ wq).reshape(b, t, XATTN_HEADS, XATTN_HEAD_DIM)
    o, _ = gqa_attend(q, mk, mv, True)
    return o.reshape(b, t, D_MODEL) @ wo

def swiglu(h, wg, wu, wd):
    return (jax.nn.silu(h @ wg) * (h @ wu)) @ wd

def gather_pages(pool, page_table, layer):
    rows = pool[page_table, layer]
    b, n, p, g, dh = rows.shape
    return rows.reshape(b, n * p, g, dh)

def setup_inputs(seed: int = 0) -> dict:
    key = jax.random.key(seed)
    keys = iter(jax.random.split(key, 48))

    def nrm(shape, scale=1.0):
        return jax.random.normal(next(keys), shape, jnp.float32) * scale

    n_pages = PAST_LEN // PAGE_SIZE
    n_phys = (5 * DEC_BATCH * n_pages + 3) // 4
    n_win = min(WINDOW, PAST_LEN)
    perm = jax.random.permutation(next(keys), n_phys)
    page_table = perm[: DEC_BATCH * n_pages].reshape(DEC_BATCH, n_pages).astype(jnp.int32)
    paged = (n_phys, N_EVEN, PAGE_SIZE, NSA_KV_HEADS, HEAD_DIM)
    win = (N_EVEN, DEC_BATCH, n_win, NSA_KV_HEADS, HEAD_DIM)
    mem_shape = (DEPTH, DEC_BATCH, N_MEM, XATTN_HEADS, XATTN_HEAD_DIM)
    a0 = jax.random.uniform(next(keys), (N_ODD, LRU_WIDTH), jnp.float32, 0.9, 0.999) ** (1.0 / LRU_C)
    return {
        'x_prompt': nrm((BATCH, SEQ, D_MODEL)),
        'mem_prompt': nrm((BATCH, N_MEM, D_MODEL)),
        'x_sample': nrm((DEC_BATCH, DEC_SEQ, D_MODEL)),
        'state_pool': nrm((N_EVEN, DEC_BATCH, POOL_STATE, POOL_WIDTH)),
        'cache_cmp_k': nrm(paged),
        'cache_cmp_v': nrm(paged),
        'cache_slc_k': nrm(paged),
        'cache_slc_v': nrm(paged),
        'cache_win_k': nrm(win),
        'cache_win_v': nrm(win),
        'state_lru_h': nrm((N_ODD, DEC_BATCH, LRU_WIDTH), 0.5),
        'state_lru_conv': nrm((N_ODD, DEC_BATCH, CONV_WIDTH - 1, LRU_WIDTH)),
        'cache_mem_k': nrm(mem_shape),
        'cache_mem_v': nrm(mem_shape),
        'page_table': page_table,
        'norm_gain': 1.0 + nrm((DEPTH, 6, D_MODEL), 0.02),
        'mem_norm_gain': 1.0 + nrm((DEPTH, D_MODEL), 0.02),
        'w_in_even': nrm((N_EVEN, D_MODEL, EVEN_IN), D_MODEL ** -0.5),
        'pool_w': nrm((N_EVEN, N_POOL_GROUPS, POOL_GROUP, POOL_GROUP), POOL_GROUP ** -0.5),
        'pool_scale': 1.0 + nrm((N_EVEN, POOL_WIDTH), 0.1),
        'w_cmp_k': nrm((N_EVEN, NSA_KV_HEADS, HEAD_DIM, HEAD_DIM), HEAD_DIM ** -0.5),
        'w_cmp_v': nrm((N_EVEN, NSA_KV_HEADS, HEAD_DIM, HEAD_DIM), HEAD_DIM ** -0.5),
        'w_out_even': nrm((N_EVEN, POOL_WIDTH + NSA_WIDTH, D_MODEL), (POOL_WIDTH + NSA_WIDTH) ** -0.5),
        'w_in_odd': nrm((N_ODD, D_MODEL, 2 * LRU_WIDTH), D_MODEL ** -0.5),
        'conv_w': nrm((N_ODD, CONV_WIDTH, LRU_WIDTH), CONV_WIDTH ** -0.5),
        'conv_b': nrm((N_ODD, LRU_WIDTH), 0.01),
        'lru_wa': nrm((N_ODD, LRU_BLOCKS, LRU_BLOCK, LRU_BLOCK), LRU_BLOCK ** -0.5),
        'lru_ba': nrm((N_ODD, LRU_WIDTH), 0.01),
        'lru_wx': nrm((N_ODD, LRU_BLOCKS, LRU_BLOCK, LRU_BLOCK), LRU_BLOCK ** -0.5),
        'lru_bx': nrm((N_ODD, LRU_WIDTH), 0.01),
        'lru_lambda': jnp.log(a0) - jnp.log1p(-a0),
        'w_out_odd': nrm((N_ODD, LRU_WIDTH, D_MODEL), LRU_WIDTH ** -0.5),
        'w_xq': nrm((DEPTH, D_MODEL, D_MODEL), D_MODEL ** -0.5),
        'w_xk': nrm((DEPTH, D_MODEL, D_MODEL), D_MODEL ** -0.5),
        'w_xv': nrm((DEPTH, D_MODEL, D_MODEL), D_MODEL ** -0.5),
        'w_xo': nrm((DEPTH, D_MODEL, D_MODEL), D_MODEL ** -0.5),
        'w_ffn_gate': nrm((DEPTH, D_MODEL, D_FF), D_MODEL ** -0.5),
        'w_ffn_up': nrm((DEPTH, D_MODEL, D_FF), D_MODEL ** -0.5),
        'w_ffn_down': nrm((DEPTH, D_FF, D_MODEL), D_FF ** -0.5),
    }

def reference(x_prompt, mem_prompt, x_sample, state_pool, cache_cmp_k, cache_cmp_v, cache_slc_k,
              cache_slc_v, cache_win_k, cache_win_v, state_lru_h, state_lru_conv, cache_mem_k,
              cache_mem_v, page_table, norm_gain, mem_norm_gain, w_in_even, pool_w, pool_scale,
              w_cmp_k, w_cmp_v, w_out_even, w_in_odd, conv_w, conv_b, lru_wa, lru_ba, lru_wx,
              lru_bx, lru_lambda, w_out_odd, w_xq, w_xk, w_xv, w_xo, w_ffn_gate, w_ffn_up,
              w_ffn_down):
    past_len = page_table.shape[1] * PAGE_SIZE
    bp = x_prompt.shape[0]
    xp, xs = x_prompt, x_sample
    ev_p, ev_s = [], []
    lru_p, lru_s = [], []
    mem_k_p, mem_v_p = [], []
    for li in range(DEPTH):
        gn = norm_gain[li]
        hp = rmsnorm(xp, gn[0])
        hs = rmsnorm(xs, gn[0])
        if li % 2 == 0:
            e = li // 2
            wts = (w_in_even[e], pool_w[e], pool_scale[e], w_cmp_k[e], w_cmp_v[e], w_out_even[e])
            mix_p, st_p = even_mixer(hp, None, 0, *wts)
            past = (state_pool[e],
                    gather_pages(cache_cmp_k, page_table, e), gather_pages(cache_cmp_v, page_table, e),
                    gather_pages(cache_slc_k, page_table, e), gather_pages(cache_slc_v, page_table, e),
                    cache_win_k[e], cache_win_v[e])
            mix_s, st_s = even_mixer(hs, past, past_len, *wts)
            ev_p.append(st_p)
            ev_s.append(st_s)
        else:
            o = li // 2
            wts = (w_in_odd[o], conv_w[o], conv_b[o], lru_wa[o], lru_ba[o], lru_wx[o], lru_bx[o],
                   lru_lambda[o], w_out_odd[o])
            conv0 = jnp.zeros((bp, CONV_WIDTH - 1, LRU_WIDTH), hp.dtype)
            h0 = jnp.zeros((bp, LRU_WIDTH), jnp.float32)
            mix_p, conv_p, hl_p = odd_mixer(hp, conv0, h0, 0, *wts)
            mix_s, conv_s, hl_s = odd_mixer(hs, state_lru_conv[o], state_lru_h[o], past_len, *wts)
            lru_p.append((conv_p, hl_p))
            lru_s.append((conv_s, hl_s))
        xp = xp + rmsnorm(mix_p, gn[1])
        xs = xs + rmsnorm(mix_s, gn[1])
        mk, mv = memory_kv(mem_prompt, mem_norm_gain[li], w_xk[li], w_xv[li])
        mem_k_p.append(mk)
        mem_v_p.append(mv)
        xp = xp + rmsnorm(cross_attend(rmsnorm(xp, gn[2]), mk, mv, w_xq[li], w_xo[li]), gn[3])
        xs = xs + rmsnorm(cross_attend(rmsnorm(xs, gn[2]), cache_mem_k[li], cache_mem_v[li], w_xq[li], w_xo[li]), gn[3])
        xp = xp + rmsnorm(swiglu(rmsnorm(xp, gn[4]), w_ffn_gate[li], w_ffn_up[li], w_ffn_down[li]), gn[5])
        xs = xs + rmsnorm(swiglu(rmsnorm(xs, gn[4]), w_ffn_gate[li], w_ffn_up[li], w_ffn_down[li]), gn[5])
    return (xp, xs,
            jnp.stack([s[0] for s in ev_p]), jnp.stack([s[0] for s in ev_s]),
            jnp.stack([s[1] for s in ev_p], axis=1), jnp.stack([s[1] for s in ev_s], axis=1),
            jnp.stack([s[2] for s in ev_p], axis=1), jnp.stack([s[2] for s in ev_s], axis=1),
            jnp.stack([s[3] for s in ev_p], axis=1), jnp.stack([s[3] for s in ev_s], axis=1),
            jnp.stack([s[4] for s in ev_p], axis=1), jnp.stack([s[4] for s in ev_s], axis=1),
            jnp.stack([s[5] for s in ev_p]), jnp.stack([s[5] for s in ev_s]),
            jnp.stack([s[6] for s in ev_p]), jnp.stack([s[6] for s in ev_s]),
            jnp.stack([s[1] for s in lru_p]), jnp.stack([s[1] for s in lru_s]),
            jnp.stack([s[0] for s in lru_p]), jnp.stack([s[0] for s in lru_s]),
            jnp.stack(mem_k_p), jnp.stack(mem_v_p))


_drawn_inputs = setup_inputs


def setup_inputs(seed=0):
    import zlib

    import numpy as np

    out = dict(_drawn_inputs(seed))
    spreads = {}
    factors = {'cache_cmp_v': 7.146, 'lru_ba': 29.938, 'lru_bx': 8.0}
    for name, (base, spread) in spreads.items():
        noise = np.random.default_rng([zlib.crc32(name.encode()), seed]).standard_normal(out[name].shape)
        drawn = base * np.exp(spread * noise) if base else spread * noise
        out[name] = jnp.asarray(drawn.astype(out[name].dtype))
    for name, factor in factors.items():
        out[name] = (out[name] * factor).astype(out[name].dtype)
    return out
```

```python
from contextlib import ExitStack

import numpy as np

import concourse.bass as bass
from concourse import mybir

F32 = mybir.dt.float32
I32 = mybir.dt.int32
U32 = mybir.dt.uint32
ALU = mybir.AluOpType
ACT = mybir.ActivationFunctionType
AXX = mybir.AxisListType.X

P = 128
D = 1024
KC = D // P
TP = 512
NB, NT = 8, 4
TS = NB * NT
T = TP + TS
H = T // 2
DFF = 2816
FC = DFF // P
KD = FC // 2
NMEM = 256
PAST = 4096
PAGE = 128
NPAGE = PAST // PAGE
SUB = 16
NSUB = PAST // SUB
POOLW = (2, 4, 8, 16)
EPS = 1e-6
NEG = -1e30
FORCE = 1e30
SC = 64 ** -0.5
SX = 256 ** -0.5
NIN = 15
U, Q, KCM, VCM, KSL, VSL, KWI, VWI, GT = 0, 4, 8, 9, 10, 11, 12, 13, 14
NSLOT = 4
NC = 4
EXT = 16 + TP + NB * 19
CEX = 3 + TP + NB * 7

WSEG = {}


def _segments():
    at = 0
    for name, blocks, tiles in [
        ("w_in", NIN, 8), ("w_out0", 8, 8), ("mk0", 8, 8), ("mv0", 8, 8), ("xq0", 8, 8), ("xo0", 8, 8),
        ("ffn0", 2 * FC, 8), ("down0", 16, KD),
        ("w_in1", 16, 8), ("lru", 4, 8), ("w_out1", 8, 8), ("mk1", 8, 8), ("mv1", 8, 8), ("xq1", 8, 8),
        ("xo1", 8, 8), ("ffn1", 2 * FC, 8), ("down1", 16, KD),
    ]:
        WSEG[name] = (at, blocks, tiles)
        at += blocks
    return at


NBLK = _segments()

ACC = {}
NORMS = ["mix0", "pmix0", "mem0", "xat0", "pxat0", "ffn_0", "pffn0",
         "mix1", "pmix1", "mem1", "xat1", "pxat1", "ffn_1", "pffn1"]
NORM = {n: i for i, n in enumerate(NORMS)}
FIRST = []


def _accumulators():
    n = 1
    ACC["s_mix0"] = 0
    for m in range(NIN):
        FIRST.append(("in", m))
        if m % 2 == 1:
            FIRST.append(("mean", m // 2))
        elif m >= 2:
            FIRST.append(("cmp", m // 2 - 1))
    FIRST.append(("mean", 7))
    for c in range(4):
        FIRST.append(("pool", c))
    FIRST.append(("cmp", 7))
    for i, (kind, k) in enumerate(FIRST):
        ACC[kind, k] = n + i
    n += len(FIRST)
    for l in range(2):
        if l == 1:
            ACC["s_mix1"] = n
            ACC["w_in1"] = n + 1
            ACC["lru"] = n + 17
            n += 33
        for name, k in [(f"w_out{l}", 8), (f"s_pmix{l}", 1), (f"s_mem{l}", 1), (f"mk{l}", 8), (f"s_xat{l}", 1),
                        (f"mv{l}", 8), (f"xq{l}", 8), (f"xo{l}", 8), (f"s_pxat{l}", 1), (f"s_ffn_{l}", 1),
                        (f"ffn{l}", 2 * FC), (f"down{l}", 8), (f"s_pffn{l}", 1)]:
            ACC[name] = n
            n += k
    return n


NACC = _accumulators()


def _consumer(b):
    for name, (b0, k, _) in WSEG.items():
        if b0 <= b < b0 + k:
            i = b - b0
            if name == "w_in":
                return ACC["in", i]
            if name == "lru":
                return ACC["lru"] + 4 * i + 3
            if name.startswith("down"):
                return ACC[name] + i // 2
            return ACC[name] + i
    raise ValueError(b)


TILES = [("cmp", b, kv, h) for b in range(NB) for kv in "kv" for h in range(2)]
for _hb in range(2):
    TILES += [("win", _hb, kv, 0) for kv in "kv"]
    TILES += [("slc", 4 * _hb + j, "k", h) for j in range(4) for h in range(2)]
    TILES += [("slc", 4 * _hb + j, "v", h) for j in range(4) for h in range(2)]
TILES += [("mem0", b, kv, 0) for kv in "kv" for b in range(NB)]
TILES += [("mem1", b, kv, 0) for kv in "kv" for b in range(NB)]
TILE = {t: i for i, t in enumerate(TILES)}

CONST = {}


def _constants():
    parts = []
    at = 0

    def put(name, a):
        nonlocal at
        a = np.asarray(a, np.float32).reshape(P, -1)
        CONST[name] = (at, a.shape[1])
        parts.append(a)
        at += a.shape[1]

    p = np.arange(P)
    put("ident", np.eye(P))
    put("ones", np.ones((P, P)))
    put("causal", np.where(p[None, :] > p[:, None], NEG, 0.0))
    a = np.zeros((2, P, NSUB))
    for s in range(NSUB):
        for i in (s, s - 1):
            if 0 <= i < NSUB - 1:
                a[s // P, s % P, i] = 1.0 / 32.0
    put("pair", a.transpose(1, 0, 2))
    t = (np.arange(4)[None, :] * P + p[:, None])[:, :, None]
    i = np.arange(32)[None, None, :]
    put("cmpbias", np.where((i * 16 + 31 <= t) & (i < 31), 0.0, NEG))
    put("anyblock", (p >= 31).astype(np.float32))
    j, g, c, tt = p // 32, p // 16 % 2, p // 4 % 4, p % 4
    key = np.arange(TS)
    for hb in range(2):
        own = (key[None, :] // 4 == 4 * hb + j[:, None]) & (key[None, :] % 4 <= tt[:, None])
        put(f"newbias{hb}", np.where(own, 0.0, NEG))
        put(f"rep{hb}", np.pad((key[:, None] == (16 * hb + 4 * j + tt)[None, :]).astype(np.float32), ((0, 96), (0, 0))))
    put("oldbias", np.where(np.arange(4)[None, :] <= tt[:, None], NEG, 0.0))
    put("headmask", np.repeat(np.arange(8)[None, :] == (4 * g + c)[:, None], 3, axis=1))
    same = (j[:, None] == j[None, :]) & (g[:, None] == g[None, :]) & (tt[:, None] == tt[None, :])
    put("heads", same)
    fix = np.ones((4, 16))
    for k, w in enumerate(POOLW):
        fix[k, :w] = w / np.minimum(np.arange(w) + 1.0, w)
    put("poolfix", np.broadcast_to(fix.reshape(1, -1), (P, 64)))
    put("subrow", (p % 8))
    return np.concatenate(parts, axis=1)


CONSTANTS = _constants()

PARAM = {"gain": 0, "memgain": 96, "poolscale": 112, "convw": 116, "convb": 148, "ba": 156, "bx": 164, "lam": 172}
NPARAM = 180


def decoder_step(nc, a, w, o):
    with ExitStack() as ctx:
        def sb(name, shape, dt=F32):
            return ctx.enter_context(nc.sbuf_tensor(name, shape, dt))

        sems = {}

        def S(name):
            if name not in sems:
                sems[name] = ctx.enter_context(nc.semaphore(name))
            return sems[name]

        x = sb("x", [P, KC, T])
        work = sb("work", [P, 2 * KC, T])
        h = work[:, 0:KC, :]
        y = work[:, KC:2 * KC, :]
        mix = sb("mix", [P, KC, T])
        big = sb("big", [P, FC, T])
        wring = sb("wring", [P, NSLOT, KD * P])
        cring = sb("cring", [P, NC, 2048])
        kstore = sb("kstore", [P, 8, 256])
        vstore = sb("vstore", [P, 8, 256])
        cst = sb("cst", [P, CONSTANTS.shape[1]])
        par = sb("par", [P, NPARAM])
        sq = sb("sq", [P, 2, T])
        ssum = sb("ssum", [P, T])
        rms = sb("rms", [P, T])
        rinv = sb("rinv", [P, T])
        idx = sb("idx", [P, 16], I32)
        small = sb("small", [P, 640])
        epsc = sb("epsc", [P, 1])
        spb = sb("spb", [P, 64])
        lh0 = sb("lh0", [P, 8, 8])
        lh = sb("lh", [P, 8, 9])
        ps = ctx.enter_context(nc.psum_tensor("ps", [P, 8, 512], F32))

        def C(name):
            at, n = CONST[name]
            return cst[:, at:at + n]

        def G(name, k):
            return par[:, PARAM[name] + k:PARAM[name] + k + 1]

        def halves(ap):
            return ap.rearrange("p (a n) -> p a n", a=2)

        swork = work[:, :, :].rearrange("p c t -> p (c t)")
        ybase = KC * T
        ext = swork[:, ybase:ybase + 4 * EXT].rearrange("p (g n) -> p g n", g=4)
        poolw_sb = swork[:, ybase + 4 * EXT:ybase + 4 * EXT + 512].rearrange("p (g n) -> p g n", g=4)
        wcmp_sb = swork[:, ybase + 4 * EXT + 512:ybase + 4 * EXT + 768].rearrange("p (g n) -> p g n", g=2)
        bufs = [mix[:, 0:2, :].rearrange("p c t -> p (c t)")[:, 0:EXT],
                mix[:, 2:4, :].rearrange("p c t -> p (c t)")[:, 0:EXT]]
        flat = big[:, 15:22, :].rearrange("p c t -> p (c t)")
        ktb = flat[:, 0:1024].rearrange("p (b n) -> p b n", b=2)
        meant = flat[:, 1024:1536].rearrange("p (k n) -> p k n", k=2)
        vcp4 = flat[:, 1024:1536].rearrange("p (q n) -> p q n", q=4)
        subs = flat[:, 1536:2560].rearrange("p (b n) -> p b n", b=8)
        mv4 = flat[:, 1536:2048].rearrange("p (q n) -> p q n", q=4)
        vnew = flat[:, 2048:2304]
        grw = flat[:, 2304:2328]
        pcs = flat[:, 2352:2448].rearrange("p (k n) -> p k n", k=3)
        s32 = flat[:, 2448:2512].rearrange("p (k n) -> p k n", k=2)
        vnat = flat[:, 2560:3584].rearrange("p (v k n) -> p v k n", v=2, k=4)
        pp = swork[:, 0:2048].rearrange("p (u r n) -> p u r n", u=2, r=2)
        ppt = swork[:, 2048:4096].rearrange("p (u r n) -> p u r n", u=2, r=2)
        pcm = swork[:, 4096:5120]
        pct = swork[:, 5120:6144].rearrange("p (k n) -> p k n", k=2)
        sslc = swork[:, 0:PAST + TS]
        spt = swork[:, ybase:ybase + PAST]
        uflat = big[:, 0:4, :].rearrange("p c t -> p (c t)")
        pce = uflat[:, 0:264]
        swin = uflat[:, 264:808]
        pwt = uflat[:, 808:1320]
        pst2 = uflat[:, 1320:1576]
        orow = pst2[:, 0:P]
        pwn = uflat[:, 1576:1704]
        spn = uflat[:, 1704:1832]
        maskb = uflat[:, 1832:1904]
        sel = uflat[:, 1904:1976]
        m8 = uflat[:, 1976:1984]
        qbd = small[:, 0:256]
        kcp = small[:, 256:288]
        gpr = small[:, 288:384].rearrange("p (q n) -> p q n", q=4)
        gtok = small[:, 384:408]
        mp = small[:, 408:440]
        grow = small[:, 440:446].rearrange("p (k n) -> p k n", k=2)
        sst = small[:, 448:472].rearrange("p (k n) -> p k n", k=6)
        pst = small[:, 472:488].rearrange("p (u r n) -> p u r n", u=2, r=2)
        xsm = small[:, 488:492]
        xpm = small[:, 492:508]
        tmp8 = small[:, 512:576].rearrange("p (c b) -> p c b", c=8)
        flatx = big[:, 8:22, :].rearrange("p c t -> p (c t)")
        xpp = flatx[:, 0:1024].rearrange("p (h n) -> p h n", h=4)
        xpt = flatx[:, 1024:2048].rearrange("p (k n) -> p k n", k=2)
        xst = flatx[:, 2048:2304]
        xsp = flatx[:, 2304:2560]
        xqd = flatx[:, 2560:4608].rearrange("p (b c n) -> p b c n", b=NB, c=8)
        xvr = flatx[:, 2560:4608].rearrange("p (b n) -> p b n", b=2)
        memn = flatx[:, 5568:7616].rearrange("p (c n) -> p c n", c=8)
        vst2 = vstore[:, :, :].rearrange("p b n -> p (b n)").rearrange("p (k n) -> p k n", k=2)
        cext = big[:, 13:22, :].rearrange("p c t -> p (c t)")[:, 0:8 * CEX].rearrange("p (c n) -> p c n", c=8)
        cv = [big[:, 8:10, :].rearrange("p c t -> p (c t)")[:, 0:571], big[:, 10:12, :].rearrange("p c t -> p (c t)")[:, 0:571]]
        lsp = spb[:, 0:8]
        lsn = spb[:, 8:16]
        ident = C("ident")

        accp = [ps[:, 2 * q:2 * q + 2, 0:H] for q in range(4)]
        ready = [S(f"acc_ready{q}") for q in range(4)]
        drained = [S(f"acc_drained{q}") for q in range(4)]
        wfull = [S(f"weights_full{s}") for s in range(NSLOT)]
        cfull = [S(f"cache_full{s}") for s in range(NC)]

        def acc_free(e, g, i=0):
            if g >= 4:
                e.wait_ge(drained[g % 4], i + g // 4)

        def acc_done(e, g, i=0):
            e.wait_ge(ready[g % 4], i + (g // 4 + 1))

        def acc_emptied(e, g):
            e.wait_ge(drained[g % 4], g // 4 + 1)

        def weights_in(e, b, i=0):
            e.wait_ge(wfull[b % NSLOT], 16 * i + 16 * (b // NSLOT + 1))

        def tile_in(e, *t):
            n = TILE[t]
            e.wait_ge(cfull[n % NC], 16 * (n // NC + 1))
            return cring[:, n % NC, :]

        def s_places(hb, hd, q):
            src = ps[:, 2 * hb + hd // 2, (hd % 2) * 256:(hd % 2) * 256 + 256].rearrange("p (d j r) -> p d j r", d=2, j=2)
            dst = mix[:, 2 * hd:2 * hd + 2, TP + 16 * hb:TP + 16 * hb + 16].rearrange("p d (j r) -> p d j r", j=2)
            return dst[:, :, :, 4 * q:4 * q + 4], src[:, :, :, 48 * q + 4 * hd:48 * q + 4 * hd + 4]

        def sample(ap):
            return ap.rearrange("p (b t) -> p b t", b=NB)

        block = ctx.enter_context(nc.Block())

        @block.sync
        def _(sp):
            sp.dma_start(x[:, :, 0:TP], a["xp"]).then_inc(S("x_loaded"), 16)
            sp.dma_start(x[:, :, TP:T], a["xs"]).then_inc(S("x_loaded"), 16)
            sp.dma_start(cst[:, :], a["const"]).then_inc(S("const_loaded"), 16)
            sp.dma_start(par[:, :], a["param"]).then_inc(S("const_loaded"), 16)
            sp.dma_start(poolw_sb, a["poolw"]).then_inc(S("small_loaded"), 16)
            sp.dma_start(wcmp_sb, a["wcmp"]).then_inc(S("small_loaded"), 16)
            sp.dma_start(lh0[:, :, :], a["lruh"]).then_inc(S("h0_loaded"), 16)

            def load(name):
                b0, k, tiles = WSEG[name]
                dst = [wring[:, s, 0:tiles * P] for s in range(NSLOT)]
                looped = tiles == 8 and k % 4 == 0 and k >= 8
                for i in range(4 if looped else k):
                    b = b0 + i
                    if b >= NSLOT:
                        acc_done(sp, _consumer(b - NSLOT))
                    sp.dma_start(dst[b % NSLOT], w[name][i]).then_inc(wfull[b % NSLOT], 16)
                if looped:
                    g0 = _consumer(b0)
                    with sp.Fori(0, k // 4 - 1) as i:
                        for j in range(4):
                            acc_done(sp, g0 + j, i)
                            s = (b0 + j) % NSLOT
                            sp.dma_start(dst[s], w[name][4 * i + (4 + j)]).then_inc(wfull[s], 16)

            for name in WSEG:
                if name.startswith("mk"):
                    acc_done(sp, ACC["w_out" + name[2]])
                    sp.dma_start(memn, a["mem"]).then_inc(S("mem_loaded"), 16)
                if name == "w_in1":
                    acc_done(sp, ACC["down0"] + 7)
                    sp.wait_ge(S("conv_zero"), 1)
                    sp.dma_start(cext[:, :, 3 + TP:CEX], a["lruconv"]).then_inc(S("conv_past"), 16)
                load(name)
            for name, n in (("out_pool", 1), ("out_kv", 6), ("win_copied", 3), ("out_mem", 4), ("out_conv", 9),
                            ("out_y", 2), ("out_lru", 1)):
                sp.wait_ge(S(name), 16 * n)

        @block.gpsimd
        def _(pool):
            pool.dma_start(idx[:, :], a["pages"]).then_inc(S("pages_loaded"), 16)
            pool.memset(epsc[:, :], EPS).then_inc(S("eps_set"), 1)
            pool.memset(ext, 0.0).then_inc(S("ext_zero"), 1)
            pool.memset(qbd, 0.0).then_inc(S("qbd_zero"), 1)
            pool.wait_ge(S("ext_zero"), 1)
            pool.dma_start(ext[:, :, 16 + TP:EXT], a["poolpast"]).then_inc(S("pool_past"), 16)
            pool.dma_start(o["wink_s"], a["winold_k"]).then_inc(S("win_copied"), 16)
            pool.dma_start(o["winv_s"], a["winold_v"]).then_inc(S("win_copied"), 16)
            pool.dma_start(o["poolold"], a["poolold"]).then_inc(S("win_copied"), 16)

            def tile_used(n):
                kind, b, kv, hh = TILES[n]
                if kind == "cmp":
                    pool.wait_ge(S("sub_ready"), n + 1)
                elif kind == "win":
                    pool.wait_ge(S("sw_sc" if kv == "k" else "sw_pv"), b + 1)
                elif kind == "slc" and kv == "k":
                    pool.wait_ge(S("kt_tr"), 4 * (2 * b + hh + 1))
                elif kind == "slc":
                    pool.wait_ge(S("sv_used"), 2 * b + hh + 1)
                else:
                    pool.wait_ge(S("mk_used" if kv == "k" else "mv_used"), 8 * int(kind[3]) + b + 1)

            def tile(n):
                kind, b, kv, hh = TILES[n]
                s = n % NC
                if n >= NC:
                    tile_used(n - NC)
                dst = cring[:, s, :]
                if kind == "cmp" or kind == "slc":
                    pool.indirect_dma_start(dst, None, a[kind + kv], bass.IndirectOffsetOnAxis(
                        ap=idx[:, 2 * b + hh:2 * b + hh + 1].bitcast(U32), axis=0)).then_inc(cfull[s], 16)
                elif kind == "win":
                    pool.dma_start(dst, a["win" + kv][b]).then_inc(cfull[s], 16)
                else:
                    pool.dma_start(dst, a["mem" + kv][int(kind[3]), b]).then_inc(cfull[s], 16)

            def sums(name):
                n = 8 * NORM[name]
                wd = NMEM if name.startswith("mem") else T
                for c in range(8):
                    pool.wait_ge(S("sq_ready"), n + c + 1)
                    if c == 0:
                        if n:
                            pool.wait_ge(S("rms_ready"), NORM[name])
                        pool.tensor_copy(ssum[:, 0:wd], sq[:, 0, 0:wd]).then_inc(S("sq_summed"), 1)
                    else:
                        pool.wait_ge(S("sq_summed"), n + c)
                        pool.tensor_tensor(ssum[:, 0:wd], ssum[:, 0:wd], sq[:, c % 2, 0:wd],
                                           ALU.add).then_inc(S("sq_summed"), 1)

            pool.wait_ge(S("idx_ready"), 1)
            for n in range(NC):
                tile(n)
            sums("mix0")
            k = 0
            at = NC
            for g in range(4):
                pool.wait_ge(S("ext_ready"), g + 1)
                if g:
                    pool.wait_ge(S("pool_d"), g)
                src, lo = ext[:, g, :], 0
                for lev in range(g + 1):
                    dst = bufs[lev % 2]
                    sh = 1 << lev
                    if lev:
                        pool.wait_ge(S("win_step"), k)
                    lo += sh
                    pool.tensor_tensor(dst[:, lo:EXT], src[:, lo:EXT], src[:, lo - sh:EXT - sh],
                                       ALU.add).then_inc(S("win_step"), 1)
                    k += 1
                    src = dst
                pool.wait_ge(S("win_step"), k)
                pool.tensor_tensor(src[:, 16:32], src[:, 16:32], C("poolfix")[:, 16 * g:16 * g + 16],
                                   ALU.mult).then_inc(S("win_step"), 1)
                k += 1
                for _ in range(6):
                    tile(at)
                    at += 1
            for n in range(at, TILE["mem0", 0, "k", 0]):
                tile(n)
            for l in range(2):
                if l:
                    sums("mix1")
                acc_done(pool, ACC[f"w_out{l}"])
                if l == 0:
                    pool.wait_ge(S("out_kv"), 16 * 6)
                pool.memset(xqd, 0.0).then_inc(S("xq_zero"), 1)
                sums(f"pmix{l}")
                n0 = TILE[f"mem{l}", 0, "k", 0]
                for n in range(n0, n0 + NC):
                    tile(n)
                sums(f"mem{l}")
                sums(f"xat{l}")
                for n in range(n0 + NC, n0 + 16):
                    tile(n)
                sums(f"pxat{l}")
                sums(f"ffn_{l}")
                sums(f"pffn{l}")

        @block.scalar
        def _(act):
            act.wait_ge(S("const_loaded"), 32)
            act.wait_ge(S("eps_set"), 1)
            act.wait_ge(S("sp_abs"), 1)
            act.activation(spb[:, 16:24], spb[:, 24:32], ACT.Exp, scale=-1.0).then_inc(S("sp_exp"), 1)

            def square(name, c, src):
                n = 8 * NORM[name] + c
                wd = NMEM if name.startswith("mem") else T
                if n >= 2:
                    act.wait_ge(S("sq_summed"), n - 1)
                dst = sq[:, c % 2, 0:wd]
                if len(src.shape) == 3:
                    dst = halves(dst)
                act.activation(dst, src, ACT.Square).then_inc(S("sq_ready"), 1)

            def root(name):
                g = ACC["s_" + name]
                acc_done(act, g)
                if NORM[name]:
                    act.wait_ge(S("rinv_ready"), NORM[name])
                if name.startswith("mem"):
                    src, dst = ps[:, 2 * (g % 4), 0:NMEM], rms[:, 0:NMEM]
                else:
                    src, dst = accp[g % 4], halves(rms[:, :])
                act.activation(dst, src, ACT.Sqrt, bias=epsc[:, 0:1], scale=1.0 / D).then_inc(S("rms_ready"), 1)
                act.wait_ge(S("rms_ready"), NORM[name] + 1)
                act.sem_inc(drained[g % 4], 1)

            def norm_in(name):
                r = ["mix0", "xat0", "ffn_0", "mix1", "xat1", "ffn_1"].index(name)
                if not r:
                    act.wait_ge(S("x_loaded"), 32)
                for c in range(8):
                    if r:
                        act.wait_ge(S("x_ready"), 8 * (r - 1) + c + 1)
                    square(name, c, x[:, c, :])
                root(name)

            def evict_y(name, norm):
                for m in range(8):
                    g = ACC[name] + m
                    acc_done(act, g)
                    act.activation(halves(y[:, m, :]), accp[g % 4], ACT.Copy).then_inc(S("y_ready"), 1)
                    square(norm, m, accp[g % 4])
                    act.wait_ge(S("sq_ready"), 8 * NORM[norm] + m + 1)
                    act.sem_inc(drained[g % 4], 1)
                root(norm)

            def evict(g, out, src):
                acc_done(act, g)
                act.activation(out, src, ACT.Copy).then_inc(drained[g % 4], 1)

            norm_in("mix0")
            for kind, k in FIRST:
                g = ACC[kind, k]
                pa, pb = 2 * (g % 4), 2 * (g % 4) + 1
                if kind == "in":
                    evict(g, halves(big[:, k, :]), accp[g % 4])
                    if k == 3:
                        for q in range(4):
                            acc_emptied(act, ACC["in", q])
                        act.dma_start(o["pool"], big[:, U:U + 4, TP - 15:T]).then_inc(S("out_pool"), 16)
                    if KCM <= k <= VWI:
                        acc_emptied(act, g)
                        act.dma_start(o["kv"][k - KCM], big[:, k, :]).then_inc(S("out_kv"), 16)
                elif kind == "mean":
                    evict(g, meant, ps[:, pa:pa + 2, 0:NSUB])
                elif kind == "cmp":
                    acc_done(act, g)
                    act.activation(kstore[:, k, :], ps[:, pa, 0:NSUB], ACT.Copy)
                    act.activation(vstore[:, k, :], ps[:, pb, 0:NSUB], ACT.Copy).then_inc(drained[g % 4], 1)
                else:
                    acc_done(act, g)
                    if k == 0:
                        act.wait_ge(S("pool_d"), 4)
                    act.activation(halves(mix[:, k, :]), accp[g % 4], ACT.Copy,
                                   scale=G("poolscale", k)).then_inc(drained[g % 4], 1)

            act.wait_ge(S("zeroed"), 1)
            act.wait_ge(S("prep_small"), 1)
            act.activation(kcp, ps[:, 0, 0:32], ACT.Copy).then_inc(S("prep_ready"), 1)
            act.wait_ge(S("prep_small"), 2)
            act.activation(vcp4, ps[:, 5, :].rearrange("p (q n) -> p q n", q=4), ACT.Copy).then_inc(S("prep_ready"), 1)
            for v in range(2):
                act.wait_ge(S("prep_v"), v + 1)
                act.activation(vnat[:, v, :, :].rearrange("p k n -> p (k n)"), ps[:, 1 + v, :],
                               ACT.Copy).then_inc(S("prep_ready"), 1)
            act.wait_ge(S("prep_new"), 1)
            act.activation(vnew[0:TS, :], ps[0:TS, 3, 0:256], ACT.Copy).then_inc(S("prep_ready"), 1)
            act.activation(gtok[0:TS, :], ps[0:TS, 3, 256:280], ACT.Sigmoid).then_inc(S("gates_ready"), 1)
            act.activation(gpr, ps[:, 4, :].rearrange("p (k n) -> p k n", k=4)[:, :, 0:24],
                           ACT.Sigmoid).then_inc(S("gates_ready"), 1)
            act.wait_ge(S("pc_sub"), 1)
            act.activation(pcm, pcm, ACT.Exp, scale=SC).then_inc(S("pc_exp"), 1)
            for k in range(2):
                act.wait_ge(S("pc_tr"), k + 1)
                act.activation(pct[:, k, :], ps[:, k, :], ACT.Copy).then_inc(S("pc_trc"), 1)

            def p_exp(u):
                n = (u % 4 + 1) * P
                for br in range(2):
                    act.wait_ge(S("pa_max"), 2 * u + br + 1)
                    if u >= 2:
                        act.wait_ge(S("pa_tr"), 2 * (u - 2) + br + 1)
                    act.activation(pp[:, u % 2, br, 0:n], ps[:, 2 * (u % 2) + br, 0:n], ACT.Exp,
                                   bias=pst[:, u % 2, br, 1:2], scale=SC,
                                   accum_out=pst[:, u % 2, br, 2:3]).then_inc(S("pa_exp"), 1)

            def p_evac(u):
                n = (u % 4 + 1) * P
                for br in range(2):
                    act.wait_ge(S("pa_tr"), 2 * u + br + 1)
                    if u >= 2:
                        act.wait_ge(S("pa_pv"), u - 1)
                    act.activation(ppt[:, u % 2, br, 0:n], ps[:, 4 + br, 0:n], ACT.Copy).then_inc(S("pa_trc"), 1)

            def p_out(c):
                act.wait_ge(S("pa_pv"), 8 * c + 8)
                act.activation(mix[:, 4 + c, 0:TP], ps[:, 6 + c % 2, :], ACT.Copy).then_inc(S("pa_out"), 1)

            for u in range(34):
                if 1 <= u <= 32:
                    p_evac(u - 1)
                if u < 32:
                    p_exp(u)
                if u >= 2 and (u - 2) % 8 == 7:
                    p_out((u - 2) // 8)

            def soft(sbuf, k):
                act.wait_ge(S("sm_max"), k + 1)
                act.activation(sbuf, sbuf, ACT.Exp, bias=sst[:, k, 1:2], scale=SC,
                               accum_out=sst[:, k, 2:3]).then_inc(S("sm_exp"), 1)

            for hb in range(2):
                soft(pce[:, 1:256], 3 * hb)
                act.wait_ge(S("sc_tr"), hb + 1)
                act.activation(pst2, ps[:, 6, 0:256], ACT.Copy).then_inc(S("sc_trc"), 1)
                act.wait_ge(S("sw_sc"), hb + 1)
                act.activation(swin[:, 0:512], ps[:, 2, :], ACT.Copy).then_inc(S("sw_cp"), 1)
                soft(swin, 3 * hb + 1)
                act.wait_ge(S("sw_tr"), hb + 1)
                act.activation(pwt, ps[:, 0, :], ACT.Copy).then_inc(S("sw_trc"), 1)
                act.activation(pwn[0:TS, :], ps[0:TS, 1, 0:P], ACT.Copy).then_inc(S("sw_trc"), 1)
                for k in range(32):
                    n = 32 * hb + k
                    act.wait_ge(S("kt_tr"), n + 1)
                    if n >= 2:
                        act.wait_ge(S("kt_sc"), n - 1)
                    act.activation(ktb[:, n % 2, :], ps[:, n % 2, :], ACT.Copy).then_inc(S("kt_trc"), 1)
                soft(sslc, 3 * hb + 2)
                for k in range(8):
                    act.wait_ge(S("sp_tr"), 8 * hb + k + 1)
                    act.activation(spt[:, k * 512:(k + 1) * 512], ps[:, k % 2, :], ACT.Copy).then_inc(S("sp_trc"), 1)
                act.wait_ge(S("spn_tr"), hb + 1)
                act.activation(spn[0:TS, :], ps[0:TS, 5, 0:P], ACT.Copy).then_inc(S("spn_trc"), 1)
                act.wait_ge(S("so_rows"), hb + 1)
                act.activation(orow, ps[:, 7, 256 + P * hb:384 + P * hb], ACT.Copy).then_inc(S("so_copied"), 1)
            act.wait_ge(S("so_done"), 2)
            for g in range(2):
                rows = slice(64 * g, 64 * g + 64)
                for c in range(4):
                    act.activation(
                        sample(mix[rows, 4 + c, TP:T]),
                        ps[rows, 7, 0:256].rearrange("p (b g c t) -> p b g c t", g=2, c=4, t=4)[:, :, g, c, :],
                        ACT.Copy).then_inc(S("so_out"), 1)

            def cross(l):
                for i in range(8):
                    g = ACC[f"xq{l}"] + i
                    evict(g, halves(big[:, i, :]), accp[g % 4])

                def x_exp(qt):
                    n = 4 * l + qt
                    act.wait_ge(S("xp_max"), n + 1)
                    if n:
                        act.wait_ge(S("xp_tr"), 2 * n)
                    for hd in range(4):
                        act.activation(xpp[:, hd, :], ps[:, 2 + hd // 2, (hd % 2) * 256:(hd % 2) * 256 + 256],
                                       ACT.Exp, bias=xpm[:, 4 + hd:5 + hd], scale=SX,
                                       accum_out=xpm[:, 8 + hd:9 + hd]).then_inc(S("xp_exp"), 1)

                def x_evac(qt):
                    n = 4 * l + qt
                    if n:
                        act.wait_ge(S("xp_pv"), n)
                    for k in range(2):
                        act.wait_ge(S("xp_tr"), 2 * n + k + 1)
                        act.activation(xpt[:, k, :], ps[:, 4 + k, :], ACT.Copy).then_inc(S("xp_trc"), 1)

                def x_out(qt):
                    act.wait_ge(S("xp_pv"), 4 * l + qt + 1)
                    act.activation(mix[:, :, qt * P:qt * P + P],
                                   ps[:, 6:8, :].rearrange("p a (c t) -> p (a c) t", c=4), ACT.Copy).then_inc(S("xo_in"), 1)

                def s_copy(hb):
                    act.wait_ge(S("mv_used"), 8 * l + 4 * (hb + 1))
                    act.activation(xvr[:, hb, 0:512], ps[:, 2 * hb, :], ACT.Copy).then_inc(S("xv_copied_a"), 1)

                def s_out(hb):
                    act.wait_ge(S("xv_tr"), 2 * l + hb + 1)
                    for hd in (0, 1):
                        for q in range(2):
                            dst, src = s_places(hb, hd, q)
                            act.activation(dst, src, ACT.Copy).then_inc(S("xv_out_a"), 1)

                x_exp(0)
                act.wait_ge(S("xs_max"), l + 1)
                act.activation(xsp, ps[:, 1, 0:256], ACT.Exp, bias=xsm[:, 1:2], scale=SX,
                               accum_out=xsm[:, 2:3]).then_inc(S("xs_exp"), 1)
                x_evac(0)
                x_exp(1)
                x_out(0)
                act.wait_ge(S("xs_tr"), l + 1)
                act.activation(xst, ps[:, 0, 256:512], ACT.Copy).then_inc(S("xs_trc"), 1)
                x_evac(1)
                x_exp(2)
                x_out(1)
                s_copy(0)
                x_evac(2)
                x_exp(3)
                x_out(2)
                s_out(0)
                s_copy(1)
                x_evac(3)
                x_out(3)
                s_out(1)

            def layer_end(l):
                evict_y(f"w_out{l}", f"pmix{l}")
                act.wait_ge(S("mem_loaded"), 16 * (l + 1))
                for c in range(8):
                    square(f"mem{l}", c, memn[:, c, :])
                root(f"mem{l}")
                if l:
                    act.wait_ge(S("out_mem"), 32)
                for m in range(8):
                    g = ACC[f"mk{l}"] + m
                    evict(g, kstore[:, m, :], ps[:, 2 * (g % 4), 0:NMEM])
                for m in range(4, 8):
                    acc_emptied(act, ACC[f"mk{l}"] + m)
                act.dma_start(o["memk"][l], kstore[:, :, :]).then_inc(S("out_mem"), 16)
                norm_in(f"xat{l}")
                for m in range(8):
                    g = ACC[f"mv{l}"] + m
                    evict(g, vst2[:, :, m * P:m * P + P], ps[:, 2 * (g % 4):2 * (g % 4) + 2, 0:P])
                for m in range(4, 8):
                    acc_emptied(act, ACC[f"mv{l}"] + m)
                act.dma_start(o["memv"][l], vstore[:, :, :]).then_inc(S("out_mem"), 16)
                if l == 0:
                    act.wait_ge(S("out_kv"), 16 * 6)
                cross(l)
                evict_y(f"xo{l}", f"pxat{l}")
                norm_in(f"ffn_{l}")
                g0 = ACC[f"ffn{l}"]
                with act.Fori(0, FC // 2) as i:
                    for j in range(2):
                        g = g0 + 2 * j
                        acc_done(act, g, i)
                        act.activation(halves(big[:, 2 * i + j, :]), accp[g % 4], ACT.Silu).then_inc(drained[g % 4], 1)
                evict_y(f"down{l}", f"pffn{l}")

            layer_end(0)

            norm_in("mix1")
            act.wait_ge(S("conv_past"), 16)
            for m in range(16):
                g = ACC["w_in1"] + m
                acc_done(act, g)
                if m < 8:
                    pa = 2 * (g % 4)
                    act.activation(cext[:, m, 3:3 + H], ps[:, pa, 0:H], ACT.Copy)
                    act.activation(cext[:, m, 3 + H:3 + TP], ps[:, pa + 1, 0:TP - H], ACT.Copy)
                    act.activation(sample(cext[:, m, 3 + TP:CEX])[:, :, 3:7], sample(ps[:, pa + 1, TP - H:H]),
                                   ACT.Copy).then_inc(drained[g % 4], 1)
                else:
                    act.activation(halves(y[:, m - 8, :]), accp[g % 4], ACT.Gelu_apprx_tanh).then_inc(drained[g % 4], 1)
            act.dma_start(o["conv_p"], cext[:, :, TP:TP + 3]).then_inc(S("out_conv"), 16)
            for c in range(8):
                act.dma_start(o["conv_s"][:, c, :, :], sample(cext[:, c, 3 + TP:CEX])[:, :, 4:7]).then_inc(S("out_conv"), 16)
            for m in range(8):
                for k in range(2):
                    g = ACC["lru"] + 2 * m + k
                    acc_done(act, g)
                    dst = (big[:, m, :], h[:, m, :])[k]
                    act.activation(halves(dst), accp[g % 4], ACT.Sigmoid,
                                   bias=G("ba" if k == 0 else "bx", m)).then_inc(drained[g % 4], 1)
            act.wait_ge(S("out_conv"), 16 * 9)
            act.wait_ge(S("sp_ready"), 1)
            for m in range(12, 16):
                acc_emptied(act, ACC["lru"] + m)
            for m in range(8):
                act.activation(big[:, 8 + m, :], big[:, m, :], ACT.Tanh, scale=lsp[:, m:m + 1]).then_inc(S("th_ready"), 1)
                act.wait_ge(S("th_ready"), m + 1)
                act.activation(big[:, m, :], big[:, m, :], ACT.Exp, scale=lsn[:, m:m + 1]).then_inc(S("a_ready"), 1)
            for m in range(8):
                act.wait_ge(S("m2_ready"), m + 1)
                act.activation(big[:, 8 + m, :], big[:, 8 + m, :], ACT.Sqrt).then_inc(S("mult_ready"), 1)
            act.wait_ge(S("lru_done"), 1)
            act.dma_start(o["lru_h"], lh[:, :, :]).then_inc(S("out_lru"), 16)
            layer_end(1)
            act.wait_ge(S("x_ready"), 48)
            act.dma_start(o["yp"], x[:, :, 0:TP]).then_inc(S("out_y"), 16)
            act.dma_start(o["ys"], x[:, :, TP:T]).then_inc(S("out_y"), 16)

        @block.vector
        def _(dve):
            steps = [0]

            def link(ins):
                steps[0] += 1
                ins.then_inc(S("dve_step"), 1)
                dve.wait_ge(S("dve_step"), steps[0])

            dve.wait_ge(S("const_loaded"), 32)
            dve.wait_ge(S("pages_loaded"), 16)
            dve.tensor_scalar(idx[:, :], idx[:, :], 8.0, C("subrow"), ALU.mult, ALU.add).then_inc(S("idx_ready"), 1)
            lam = par[:, PARAM["lam"]:PARAM["lam"] + 8]
            link(dve.tensor_scalar(spb[:, 32:40], lam, -1.0, None, ALU.mult))
            dve.tensor_tensor(spb[:, 24:32], lam, spb[:, 32:40], ALU.max).then_inc(S("sp_abs"), 1)
            dve.wait_ge(S("sp_exp"), 1)
            e, z, s1, s2, acc = spb[:, 16:24], spb[:, 32:40], spb[:, 40:48], spb[:, 48:56], spb[:, 56:64]
            link(dve.tensor_scalar(s1, e, 2.0, None, ALU.add))
            link(dve.reciprocal(s1, s1))
            link(dve.tensor_tensor(s1, s1, e, ALU.mult))
            link(dve.tensor_tensor(s2, s1, s1, ALU.mult))
            link(dve.tensor_scalar(acc, s2, 1.0 / 17, None, ALU.mult))
            for k in (15, 13, 11, 9, 7, 5, 3):
                link(dve.scalar_tensor_tensor(out=acc, in0=acc, scalar=1.0 / k, in1=s2, op0=ALU.add, op1=ALU.mult))
            link(dve.scalar_tensor_tensor(out=acc, in0=acc, scalar=1.0, in1=s1, op0=ALU.add, op1=ALU.mult))
            link(dve.tensor_scalar(z, z, 0.0, None, ALU.max))
            link(dve.scalar_tensor_tensor(out=acc, in0=acc, scalar=2.0, in1=z, op0=ALU.mult, op1=ALU.add))
            dve.tensor_scalar(lsp, acc, 8.0, None, ALU.mult)
            dve.tensor_scalar(lsn, acc, -8.0, None, ALU.mult).then_inc(S("sp_ready"), 1)

            def inverse(name):
                wd = NMEM if name.startswith("mem") else T
                dve.wait_ge(S("rms_ready"), NORM[name] + 1)
                dve.reciprocal(rinv[:, 0:wd], rms[:, 0:wd]).then_inc(S("rinv_ready"), 1)
                dve.wait_ge(S("rinv_ready"), NORM[name] + 1)

            def norm_apply(name, gain):
                inverse(name)
                for c in range(8):
                    dve.scalar_tensor_tensor(out=h[:, c, :], in0=x[:, c, :], scalar=G("gain", 8 * gain + c),
                                             in1=rinv[:, :], op0=ALU.mult, op1=ALU.mult).then_inc(S("h_ready"), 1)

            def residual(name, gain, r):
                inverse(name)
                dve.wait_ge(S("y_ready"), 8 * (r + 1))
                for c in range(9):
                    if c < 8:
                        dve.scalar_tensor_tensor(out=y[:, c, :], in0=y[:, c, :], scalar=G("gain", 8 * gain + c),
                                                 in1=rinv[:, :], op0=ALU.mult, op1=ALU.mult).then_inc(S("y_scaled"), 1)
                    if c:
                        dve.wait_ge(S("y_scaled"), 8 * r + c)
                        dve.tensor_tensor(x[:, c - 1, :], x[:, c - 1, :], y[:, c - 1, :], ALU.add).then_inc(S("x_ready"), 1)

            norm_apply("mix0", 0)
            dve.wait_ge(S("ext_zero"), 1)
            dve.wait_ge(S("pool_past"), 16)
            wsteps = 0
            for b in range(NB):
                for kv in range(2):
                    for hh in range(2):
                        n = 4 * b + 2 * kv + hh
                        src = tile_in(dve, "cmp", b, "kv"[kv], hh)
                        if b >= 2:
                            acc_done(dve, ACC["mean", b - 2])
                        dve.tensor_reduce(subs[:, n % 8, :], src.rearrange("p (r c) -> p c r", r=SUB), AXX,
                                          ALU.add).then_inc(S("sub_ready"), 1)
                if b < 4:
                    acc_emptied(dve, ACC["in", b])
                    dve.tensor_copy(ext[:, b, 16:16 + TP], big[:, b, 0:TP])
                    dve.tensor_copy(sample(ext[:, b, 16 + TP:EXT])[:, :, 15:19],
                                    sample(big[:, b, TP:T])).then_inc(S("ext_ready"), 1)
                if 1 <= b <= 4:
                    g = b - 1
                    wsteps += g + 2
                    dve.wait_ge(S("win_step"), wsteps)
                    dve.scalar_tensor_tensor(out=mix[:, 4 + g, 0:TP], in0=bufs[g % 2][:, 16:16 + TP],
                                             scalar=1.0 / POOLW[g], in1=big[:, g, 0:TP], op0=ALU.mult, op1=ALU.subtract)
                    dve.scalar_tensor_tensor(out=sample(mix[:, 4 + g, TP:T]),
                                             in0=sample(bufs[g % 2][:, 16 + TP:EXT])[:, :, 15:19],
                                             scalar=1.0 / POOLW[g], in1=sample(big[:, g, TP:T]),
                                             op0=ALU.mult, op1=ALU.subtract).then_inc(S("pool_d"), 1)

            for k in (VCM, VWI, GT):
                acc_emptied(dve, ACC["in", k])
            for g in range(2):
                rows = slice(64 * g, 64 * g + 64)
                if not g:
                    dve.wait_ge(S("qbd_zero"), 1)
                for c in range(4):
                    last = dve.tensor_copy(qbd[rows, :].rearrange("p (b g c t) -> p b g c t", g=2, c=4, t=4)[:, :, g, c, :],
                                           sample(big[rows, Q + c, TP:T]))
            last.then_inc(S("qbd_ready"), 1)
            acc_done(dve, ACC["cmp", 7])
            dve.memset(mv4, 0.0)
            dve.memset(vnew, 0.0)
            dve.memset(mp, 0.0)
            for k in range(2):
                last = dve.tensor_reduce(s32[:, k, :], big[:, KCM + k, 0:TP].rearrange("p (s r) -> p s r", r=SUB),
                                         AXX, ALU.add)
            link(last)
            link(dve.tensor_tensor(mp[:, 0:31], s32[:, 0, 0:31], s32[:, 0, 1:32], ALU.add))
            dve.tensor_scalar(mp[:, 0:31], mp[:, 0:31], 1.0 / 32, None, ALU.mult)
            link(dve.tensor_tensor(s32[:, 1, 0:31], s32[:, 1, 0:31], s32[:, 1, 1:32], ALU.add))
            for q in range(4):
                last = dve.tensor_scalar(mv4[:, q, 32 * q:32 * q + 31], s32[:, 1, 0:31], 1.0 / 32, None, ALU.mult)
            last.then_inc(S("means_ready"), 1)
            dve.wait_ge(S("out_pool"), 16)
            dve.memset(pwn, 0.0)
            dve.memset(spn, 0.0)
            dve.memset(pce, 0.0).then_inc(S("zeroed"), 1)
            for hb in range(2):
                dve.wait_ge(S("grow_mm"), 1)
                link(dve.tensor_tensor(grw, ps[:, 0, 64 + 32 * hb:88 + 32 * hb], C("headmask"), ALU.mult))
                link(dve.tensor_reduce(grow[:, hb, :], grw.rearrange("p (h r) -> p r h", r=3), AXX, ALU.add))
            dve.wait_ge(S("pc_sc"), 1)
            for k in range(2):
                last = dve.tensor_tensor(pcm[:, 512 * k:512 * k + 512].rearrange("p (h n) -> p h n", h=4),
                                         ps[:, 6 + k, :].rearrange("p (h n) -> p h n", h=4),
                                         C("cmpbias").unsqueeze(1).to_broadcast([P, 4, P]), ALU.add)
            link(last)
            pc3 = pcm.rearrange("p (u n) -> p u n", n=32)

            def over(col):
                return col.unsqueeze(2).to_broadcast([P, 32, 32])

            link(dve.tensor_reduce(pcs[:, 0, :], pc3, AXX, ALU.max))
            dve.tensor_tensor(pc3, pc3, over(pcs[:, 0, :]), ALU.subtract).then_inc(S("pc_sub"), 1)
            dve.wait_ge(S("pc_exp"), 1)
            link(dve.tensor_reduce(pcs[:, 1, :], pc3, AXX, ALU.add))
            link(dve.reciprocal(pcs[:, 2, :], pcs[:, 1, :]))
            dve.wait_ge(S("gates_ready"), 2)
            r4 = pcs[:, 2, :].rearrange("p (h q) -> p h q", q=4)
            gv = gpr.rearrange("p q (g c r) -> p g c r q", g=2, c=4)
            for c in range(4):
                for g in range(2):
                    last = dve.tensor_tensor(r4[:, 4 * g + c, :], r4[:, 4 * g + c, :], gv[:, g, c, 0, :], ALU.mult)
            link(last)
            link(dve.tensor_scalar(r4[:, :, 0], r4[:, :, 0], C("anyblock"), None, ALU.mult))
            dve.tensor_tensor(pc3, pc3, over(pcs[:, 2, :]), ALU.mult).then_inc(S("pc_norm"), 1)

            def p_max(u):
                qt = u % 4
                n = (qt + 1) * P
                for br in range(2):
                    dve.wait_ge(S("pa_sc"), 2 * u + br + 1)
                    bank = 2 * (u % 2) + br
                    diag = ps[:, bank, qt * P:n]
                    link(dve.tensor_tensor(diag, diag, C("causal"), ALU.add))
                    link(dve.tensor_reduce(pst[:, u % 2, br, 0:1], ps[:, bank, 0:n], AXX, ALU.max))
                    dve.tensor_scalar(pst[:, u % 2, br, 1:2], pst[:, u % 2, br, 0:1], -SC, None,
                                      ALU.mult).then_inc(S("pa_max"), 1)

            def p_norm(u):
                c, g, qt = u // 8, u // 4 % 2, u % 4
                n = (qt + 1) * P
                for br in range(2):
                    dve.wait_ge(S("pa_exp"), 2 * u + br + 1)
                    link(dve.reciprocal(pst[:, u % 2, br, 3:4], pst[:, u % 2, br, 2:3]))
                    gate = gpr[:, qt, 3 * (4 * g + c) + 1 + br:3 * (4 * g + c) + 2 + br]
                    dve.tensor_scalar(pp[:, u % 2, br, 0:n], pp[:, u % 2, br, 0:n], pst[:, u % 2, br, 3:4], gate,
                                      ALU.mult, ALU.mult).then_inc(S("pa_norm"), 1)

            for u in range(33):
                if u:
                    p_norm(u - 1)
                if u < 32:
                    p_max(u)

            def s_max(sbuf, k):
                link(dve.tensor_reduce(sst[:, k, 0:1], sbuf, AXX, ALU.max))
                dve.tensor_scalar(sst[:, k, 1:2], sst[:, k, 0:1], -SC, None, ALU.mult).then_inc(S("sm_max"), 1)
                dve.wait_ge(S("sm_exp"), k + 1)
                link(dve.reciprocal(sst[:, k, 3:4], sst[:, k, 2:3]))

            dve.wait_ge(S("pa_pv"), 32)
            for hb in range(2):
                dve.wait_ge(S("sc_sc"), hb + 1)
                if hb:
                    dve.wait_ge(S("sc_tr"), 1)
                link(dve.tensor_copy(pce[:, 1:256], ps[:, 4, 0:255]))
                s_max(pce[:, 1:256], 3 * hb)
                dve.tensor_scalar(pce[:, 1:256], pce[:, 1:256], sst[:, 3 * hb, 3:4], None,
                                  ALU.mult).then_inc(S("sc_norm"), 1)
                dve.wait_ge(S("sc_imp"), hb + 1)
                imp = sel[:, 0:65]
                link(dve.tensor_copy(imp, ps[:, 5, 0:257:4]))
                for k in range(1, 5):
                    link(dve.tensor_tensor(imp, imp, ps[:, 5, k:k + 257:4], ALU.add))
                dve.memset(sel[:, 0:1], FORCE)
                link(dve.memset(sel[:, 63:65], FORCE))
                for _ in range(2):
                    link(dve.max(m8, imp))
                    link(dve.match_replace(imp, m8, imp, -2.0))
                dve.tensor_scalar(maskb[:, 0:65], imp, -1.0, NEG, ALU.is_gt, ALU.mult)
                dve.tensor_scalar(pce[:, 1:256], pce[:, 1:256], grow[:, hb, 0:1], None,
                                  ALU.mult).then_inc(S("sc_gate"), 1)
                dve.wait_ge(S("sw_cp"), hb + 1)
                dve.tensor_tensor(swin[:, 0:4], swin[:, 0:4], C("oldbias"), ALU.add)
                if hb:
                    dve.wait_ge(S("sw_tr"), 1)
                link(dve.tensor_tensor(swin[:, 512:544], ps[:, 3, 0:TS], C(f"newbias{hb}"), ALU.add))
                s_max(swin, 3 * hb + 1)
                dve.tensor_scalar(swin, swin, sst[:, 3 * hb + 1, 3:4], grow[:, hb, 2:3], ALU.mult,
                                  ALU.mult).then_inc(S("sw_norm"), 1)
                if hb:
                    dve.wait_ge(S("sp_tr"), 8)
                    dve.wait_ge(S("spn_tr"), 1)
                for k in range(32):
                    n = 32 * hb + k
                    j, hh, q = k // 8, k // 4 % 2, k % 4
                    rows = slice(32 * j, 32 * j + 32)
                    at = (16 * hh + 4 * q) * P
                    dve.wait_ge(S("kt_sc"), n + 1)
                    dve.tensor_tensor(
                        sslc[rows, at:at + 512].rearrange("p (r b s) -> p r b s", r=4, s=4),
                        ps[rows, 2 + n % 2, :].rearrange("p (r b s) -> p r b s", r=4, s=4),
                        maskb[rows, 32 * hh:32 * hh + 32].unsqueeze(1).unsqueeze(3).to_broadcast([32, 4, 32, 4]),
                        ALU.add).then_inc(S("sl_ev"), 1)
                dve.wait_ge(S("sl_new"), hb + 1)
                dve.wait_ge(S("sl_ev"), 32 * (hb + 1))
                link(dve.tensor_tensor(sslc[:, PAST:PAST + TS], ps[:, 4, 0:TS], C(f"newbias{hb}"), ALU.add))
                s_max(sslc, 3 * hb + 2)
                dve.tensor_scalar(sslc, sslc, sst[:, 3 * hb + 2, 3:4], grow[:, hb, 1:2], ALU.mult,
                                  ALU.mult).then_inc(S("sl_norm"), 1)

            def layer_end(l):
                residual(f"pmix{l}", 6 * l + 1, 3 * l)
                inverse(f"mem{l}")
                for c in range(8):
                    dve.scalar_tensor_tensor(out=memn[:, c, :], in0=memn[:, c, :], scalar=G("memgain", 8 * l + c),
                                             in1=rinv[:, 0:NMEM], op0=ALU.mult, op1=ALU.mult).then_inc(S("memn_ready"), 1)
                norm_apply(f"xat{l}", 6 * l + 2)
                dve.wait_ge(S("xq_zero"), l + 1)
                for c in range(8):
                    acc_emptied(dve, ACC[f"xq{l}"] + c)
                    for q in range(2):
                        last = dve.tensor_copy(xqd[:, q::2, c, 16 * q + 4 * (c // 2):16 * q + 4 * (c // 2) + 4],
                                               sample(big[:, c, TP:T])[:, q::2, :])
                last.then_inc(S("xq_apart"), 1)

                def x_soft(qt):
                    n = 4 * l + qt
                    dve.wait_ge(S("xp_sc"), n + 1)
                    link(dve.tensor_reduce(xpm[:, 0:4], ps[:, 2:4, :].rearrange("p a (h n) -> p (a h) n", h=2), AXX, ALU.max))
                    dve.tensor_scalar(xpm[:, 4:8], xpm[:, 0:4], -SX, None, ALU.mult).then_inc(S("xp_max"), 1)
                    dve.wait_ge(S("xp_exp"), 4 * (n + 1))
                    link(dve.reciprocal(xpm[:, 12:16], xpm[:, 8:12]))
                    dve.tensor_tensor(xpp, xpp, xpm[:, 12:16].unsqueeze(2).to_broadcast([P, 4, 256]),
                                      ALU.mult).then_inc(S("xp_norm"), 1)

                def s_copy(hb):
                    dve.wait_ge(S("mv_used"), 8 * l + 4 * (hb + 1))
                    dve.tensor_copy(xvr[:, hb, 512:1024], ps[:, 2 * hb + 1, :]).then_inc(S("xv_copied_v"), 1)

                def s_out(hb):
                    dve.wait_ge(S("xv_tr"), 2 * l + hb + 1)
                    for hd in (2, 3):
                        for q in range(2):
                            dst, src = s_places(hb, hd, q)
                            dve.tensor_copy(dst, src).then_inc(S("xv_out_v"), 1)

                x_soft(0)
                dve.wait_ge(S("mk_used"), 8 * (l + 1))
                link(dve.tensor_reduce(xsm[:, 0:1], ps[:, 1, 0:256], AXX, ALU.max))
                dve.tensor_scalar(xsm[:, 1:2], xsm[:, 0:1], -SX, None, ALU.mult).then_inc(S("xs_max"), 1)
                dve.wait_ge(S("xs_exp"), l + 1)
                link(dve.reciprocal(xsm[:, 3:4], xsm[:, 2:3]))
                dve.tensor_scalar(xsp, xsp, xsm[:, 3:4], None, ALU.mult).then_inc(S("xs_norm"), 1)
                x_soft(1)
                x_soft(2)
                s_copy(0)
                x_soft(3)
                s_out(0)
                s_copy(1)
                s_out(1)
                residual(f"pxat{l}", 6 * l + 3, 3 * l + 1)
                norm_apply(f"ffn_{l}", 6 * l + 4)
                g0 = ACC[f"ffn{l}"]
                with dve.Fori(0, FC // 2) as i:
                    for j in range(2):
                        g = g0 + 2 * j + 1
                        acc_done(dve, g, i)
                        dve.wait_ge(drained[(g - 1) % 4], i + ((g - 1) // 4 + 1))
                        hid = halves(big[:, 2 * i + j, :])
                        dve.tensor_tensor(hid, hid, accp[g % 4], ALU.mult).then_inc(drained[g % 4], 1)
                residual(f"pffn{l}", 6 * l + 5, 3 * l + 2)

            layer_end(0)

            acc_done(dve, ACC["down0"] + 7)
            dve.memset(cext[:, :, 0:3], 0.0).then_inc(S("conv_zero"), 1)
            norm_apply("mix1", 6)
            n = CEX - 3
            for m in range(8):
                acc_emptied(dve, ACC["w_in1"] + m)
                link(dve.tensor_scalar(cv[m % 2][:, 0:n], cext[:, m, 0:n], G("convw", m), G("convb", m), ALU.mult, ALU.add))
                for k in (1, 2):
                    link(dve.scalar_tensor_tensor(out=cv[m % 2][:, 0:n], in0=cext[:, m, k:k + n], scalar=G("convw", 8 * k + m),
                                                  in1=cv[m % 2][:, 0:n], op0=ALU.mult, op1=ALU.add))
                dve.scalar_tensor_tensor(out=mix[:, m, 0:TP], in0=cext[:, m, 3:3 + TP], scalar=G("convw", 24 + m),
                                         in1=cv[m % 2][:, 0:TP], op0=ALU.mult, op1=ALU.add)
                dve.scalar_tensor_tensor(out=sample(mix[:, m, TP:T]), in0=sample(cext[:, m, 3 + TP:CEX])[:, :, 3:7],
                                         scalar=G("convw", 24 + m), in1=sample(cv[m % 2][:, 3 + TP:CEX])[:, :, 0:4],
                                         op0=ALU.mult, op1=ALU.add).then_inc(S("xf_ready"), 1)
            for m in range(8):
                dve.wait_ge(S("th_ready"), m + 1)
                if m:
                    dve.wait_ge(S("m2_ready"), m)
                t = rinv[:, :]
                link(dve.tensor_scalar(t, big[:, 8 + m, :], 1.0, None, ALU.add))
                link(dve.reciprocal(t, t))
                dve.scalar_tensor_tensor(out=big[:, 8 + m, :], in0=big[:, 8 + m, :], scalar=2.0, in1=t,
                                         op0=ALU.mult, op1=ALU.mult).then_inc(S("m2_ready"), 1)
            for m in range(8):
                dve.wait_ge(S("mult_ready"), m + 1)
                dve.wait_ge(S("a_ready"), m + 1)
                link(dve.memset(big[:, 8 + m, 0:1], 1.0))
                link(dve.tensor_tensor(h[:, m, :], h[:, m, :], big[:, 8 + m, :], ALU.mult))
                link(dve.tensor_tensor(h[:, m, :], h[:, m, :], mix[:, m, :], ALU.mult))
                link(dve.tensor_tensor_scan(mix[:, m, 0:TP], big[:, m, 0:TP], h[:, m, 0:TP], 0.0, ALU.mult, ALU.add))

            def col(ap, t):
                return ap[:, 0:8, TP:T].rearrange("p c (b t) -> p c b t", t=NT)[:, :, :, t]

            dve.wait_ge(S("h0_loaded"), 16)
            for t in range(NT):
                prev = lh0[:, :, :] if t == 0 else col(mix, t - 1)
                link(dve.tensor_tensor(tmp8, col(big, t), prev, ALU.mult))
                link(dve.tensor_tensor(col(mix, t), tmp8, col(h, t), ALU.add))
            dve.tensor_copy(lh[:, :, 0:1], mix[:, :, TP - 1:TP])
            dve.tensor_copy(lh[:, :, 1:9], col(mix, NT - 1)).then_inc(S("lru_done"), 1)
            dve.wait_ge(S("lru_done"), 1)
            for m in range(8):
                acc_emptied(dve, ACC["w_in1"] + 8 + m)
                dve.tensor_tensor(mix[:, m, :], mix[:, m, :], y[:, m, :], ALU.mult).then_inc(S("lmix_ready"), 1)
            layer_end(1)

        @block.tensor
        def _(pe):
            pe.wait_ge(S("const_loaded"), 32)

            def mm(out, lhsT, rhs, start, stop, **kw):
                return pe.matmul(out, lhsT, rhs, start=start, stop=stop, **kw)

            def stats(name):
                g = ACC["s_" + name]
                acc_free(pe, g)
                pe.wait_ge(S("sq_summed"), 8 * (NORM[name] + 1))
                if name.startswith("mem"):
                    mm(ps[:, 2 * (g % 4), 0:NMEM], C("ones"), ssum[:, 0:NMEM], True, True).then_inc(ready[g % 4], 1)
                    return
                for a_ in range(2):
                    last = mm(accp[g % 4][:, a_, :], C("ones"), ssum[:, a_ * H:a_ * H + H], True, True)
                last.then_inc(ready[g % 4], 1)

            def chunk(g, b, src, i=0, tiles=8, k0=0, kn=8):
                weights_in(pe, b, i)
                last = None
                for k in range(tiles):
                    for a_ in range(2):
                        last = mm(accp[g % 4][:, a_, :], wring[:, b % NSLOT, k * P:k * P + P],
                                  src[:, k0 + k, a_ * H:a_ * H + H], k0 + k == 0, k0 + k == kn - 1,
                                  skip_group_check=True)
                return last

            def linear(name, src):
                b0, k, _ = WSEG[name]
                g0 = ACC[name]
                with pe.Fori(0, k // 4) as i:
                    for j in range(4):
                        acc_free(pe, g0 + j, i)
                        chunk(g0 + j, b0 + j, src, i).then_inc(ready[(g0 + j) % 4], 1)

            stats("mix0")
            pe.wait_ge(S("h_ready"), 8)
            for kind, k in FIRST:
                g = ACC[kind, k]
                pa, pb = 2 * (g % 4), 2 * (g % 4) + 1
                acc_free(pe, g)
                if kind == "in":
                    last = chunk(g, WSEG["w_in"][0] + k, h)
                elif kind == "mean":
                    for kv in range(2):
                        for hh in range(2):
                            n = 4 * k + 2 * kv + hh
                            pe.wait_ge(S("sub_ready"), n + 1)
                            last = mm(ps[:, pa + kv, 0:NSUB], subs[:, n % 8, :], C("pair")[:, hh * NSUB:hh * NSUB + NSUB],
                                      hh == 0, hh == 1)
                elif kind == "cmp":
                    if k == 0:
                        pe.wait_ge(S("small_loaded"), 32)
                    acc_emptied(pe, ACC["mean", k])
                    mm(ps[:, pa, 0:NSUB], wcmp_sb[:, 0, :], meant[:, 0, :], True, True)
                    for kt in range(2):
                        last = mm(ps[:, pb, kt * P:kt * P + P], meant[:, 1, kt * P:kt * P + P], wcmp_sb[:, 1, :], True, True)
                else:
                    pe.wait_ge(S("pool_d"), k + 1)
                    for a_ in range(2):
                        last = mm(accp[g % 4][:, a_, :], poolw_sb[:, k, :], mix[:, 4 + k, a_ * H:a_ * H + H], True, True)
                last.then_inc(ready[g % 4], 1)

            for kind, k in FIRST[-4:]:
                acc_emptied(pe, ACC[kind, k])
            pe.wait_ge(S("means_ready"), 1)
            mm(ps[:, 0, 0:32], wcmp_sb[:, 0, :], mp, True, True).then_inc(S("prep_small"), 1)
            for q in range(4):
                last = mm(ps[:, 5, q * P:q * P + P], mv4[:, q, :], wcmp_sb[:, 1, :], True, True)
            last.then_inc(S("prep_small"), 1)
            for v, chunk_ in enumerate((VSL, VWI)):
                for k in range(4):
                    last = pe.transpose(ps[:, 1 + v, k * P:k * P + P], big[:, chunk_, k * P:k * P + P], ident)
                last.then_inc(S("prep_v"), 1)
            for k in range(4):
                pe.transpose(ps[:, 4, k * P:k * P + P], big[:, GT, k * P:k * P + P], ident)
            for v, chunk_ in enumerate((VSL, VWI, GT)):
                last = pe.transpose(ps[0:TS, 3, v * P:v * P + P], big[:, chunk_, TP:T], ident)
            last.then_inc(S("prep_new"), 1)
            pe.wait_ge(S("prep_ready"), 1)
            for u in range(32):
                c, g, qt = u // 8, u // 4 % 2, u % 4
                rows = slice(64 * g, 64 * g + 64)
                at = (4 * c + qt) * 32
                last = mm(ps[:, 6 + g, at:at + 32], big[rows, Q + c, qt * P:qt * P + P],
                          kcp[rows, :], True, True)
            last.then_inc(S("pc_sc"), 1)
            pe.wait_ge(S("gates_ready"), 1)
            for hb in range(2):
                last = mm(ps[:, 0, 64 + 32 * hb:88 + 32 * hb], C(f"rep{hb}")[0:TS, :], gtok[0:TS, :], True, True)
            last.then_inc(S("grow_mm"), 1)
            pe.wait_ge(S("prep_ready"), 5)
            pe.wait_ge(S("pc_norm"), 1)
            for hd in range(8):
                last = pe.transpose(ps[:, hd // 4, (hd % 4) * P:(hd % 4) * P + P], pcm[:, hd * P:hd * P + P], ident)
                if hd % 4 == 3:
                    last.then_inc(S("pc_tr"), 1)

            pe.wait_ge(S("pc_trc"), 2)
            pe.wait_ge(S("gates_ready"), 2)

            def p_scores(u):
                c, g, qt = u // 8, u // 4 % 2, u % 4
                n = (qt + 1) * P
                rows = slice(64 * g, 64 * g + 64)
                if u >= 2:
                    pe.wait_ge(S("pa_exp"), 2 * (u - 1))
                for br, kc in enumerate((KSL, KWI)):
                    mm(ps[:, 2 * (u % 2) + br, 0:n], big[rows, Q + c, qt * P:qt * P + P], big[rows, kc, 0:n],
                       True, True).then_inc(S("pa_sc"), 1)

            def p_turn(u):
                for br in range(2):
                    pe.wait_ge(S("pa_norm"), 2 * u + br + 1)
                    if u:
                        pe.wait_ge(S("pa_trc"), 2 * (u - 1) + br + 1)
                    for k in range(u % 4 + 1):
                        last = pe.transpose(ps[:, 4 + br, k * P:k * P + P], pp[:, u % 2, br, k * P:k * P + P], ident)
                    last.then_inc(S("pa_tr"), 1)

            def p_values(u):
                c, g, qt = u // 8, u // 4 % 2, u % 4
                hd = 4 * g + c
                if u % 8 == 0 and c >= 2:
                    pe.wait_ge(S("pa_out"), c - 1)
                pe.wait_ge(S("pa_trc"), 2 * u + 2)
                out = ps[64 * g:64 * g + 64, 6 + c % 2, qt * P:qt * P + P]
                cols = slice(64 * g, 64 * g + 64)
                mm(out, vcp4[:, qt, cols], pct[:, hd // 4, (hd % 4) * P:(hd % 4) * P + P], True, False)
                for br in range(2):
                    for k in range(qt + 1):
                        last = mm(out, vnat[:, br, k, cols], ppt[:, u % 2, br, k * P:k * P + P], False,
                                  br == 1 and k == qt)
                last.then_inc(S("pa_pv"), 1)

            for u in range(34):
                if u < 32:
                    p_scores(u)
                if 1 <= u <= 32:
                    p_turn(u - 1)
                if u >= 2:
                    p_values(u - 2)

            pe.wait_ge(S("pa_out"), 4)
            pe.wait_ge(S("qbd_ready"), 1)
            opened = [False] * NB

            def to_rows(b, probs, values, stop=False):
                at = 256 + P * (b // 4)
                ins = mm(ps[32 * (b % 4):32 * (b % 4) + 32, 7, at:at + P], probs, values, not opened[b], stop,
                         skip_group_check=True)
                opened[b] = True
                return ins

            for hb in range(2):
                if hb:
                    pe.wait_ge(S("sw_cp"), 1)
                for j in range(4):
                    b = 4 * hb + j
                    last = mm(ps[32 * j:32 * j + 32, 4, 0:NSUB], qbd[:, 32 * b:32 * b + 32], kstore[:, b, :], True, True)
                last.then_inc(S("sc_sc"), 1)
                pe.wait_ge(S("sc_norm"), hb + 1)
                if hb:
                    pe.wait_ge(S("spn_trc"), 1)
                mm(ps[:, 5, 0:264], C("heads"), pce, True, True).then_inc(S("sc_imp"), 1)
                wk = tile_in(pe, "win", hb, "k", 0)
                for j in range(4):
                    b = 4 * hb + j
                    mm(ps[32 * j:32 * j + 32, 2, :], qbd[:, 32 * b:32 * b + 32], wk[:, j * 512:j * 512 + 512], True, True)
                rows4 = qbd[:, 128 * hb:128 * hb + 128]
                mm(ps[:, 3, 0:TS], rows4, big[:, KWI, TP:T], True, True).then_inc(S("sw_sc"), 1)
                pe.wait_ge(S("sc_gate"), hb + 1)
                if hb:
                    pe.wait_ge(S("sw_trc"), 2)
                for kt in range(2):
                    last = pe.transpose(ps[:, 6, kt * P:kt * P + P], pce[:, 1 + kt * P:1 + kt * P + P], ident)
                last.then_inc(S("sc_tr"), 1)
                pe.wait_ge(S("sc_trc"), hb + 1)
                if hb:
                    pe.wait_ge(S("so_copied"), 1)
                for j in range(4):
                    b = 4 * hb + j
                    for kt in range(2):
                        to_rows(b, pst2[:, kt * P + 32 * j:kt * P + 32 * j + 32], vstore[:, b, kt * P:kt * P + P])
                pe.wait_ge(S("sw_norm"), hb + 1)
                for kt in range(4):
                    pe.transpose(ps[:, 0, kt * P:kt * P + P], swin[:, kt * P:kt * P + P], ident)
                pe.transpose(ps[0:TS, 1, 0:P], swin[:, 512:544], ident).then_inc(S("sw_tr"), 1)
                wv = tile_in(pe, "win", hb, "v", 0)
                pe.wait_ge(S("sw_trc"), 2 * (hb + 1))
                for j in range(4):
                    b = 4 * hb + j
                    to_rows(b, pwn[:, 32 * j:32 * j + 32], vnew[:, P:2 * P])
                    for kt in range(4):
                        last = to_rows(b, pwt[:, kt * P + 32 * j:kt * P + 32 * j + 32],
                                       wv[:, j * 512 + kt * P:j * 512 + kt * P + P])
                last.then_inc(S("sw_pv"), 1)
                if hb:
                    pe.wait_ge(S("sp_trc"), 8)
                for k in range(33):
                    n = 32 * hb + k
                    if k < 32:
                        if k % 4 == 0:
                            kt_ = tile_in(pe, "slc", 4 * hb + k // 8, "k", k // 4 % 2)
                        if n >= 2:
                            pe.wait_ge(S("kt_trc"), n - 1)
                        for r in range(4):
                            at = (4 * (k % 4) + r) * P
                            last = pe.transpose(ps[:, n % 2, r * P:r * P + P], kt_[:, at:at + P], ident)
                        last.then_inc(S("kt_tr"), 1)
                    if k:
                        n -= 1
                        j = (k - 1) // 8
                        pe.wait_ge(S("kt_trc"), n + 1)
                        if n >= 2:
                            pe.wait_ge(S("sl_ev"), n - 1)
                        b = 4 * hb + j
                        mm(ps[32 * j:32 * j + 32, 2 + n % 2, :], qbd[:, 32 * b:32 * b + 32], ktb[:, n % 2, :],
                           True, True).then_inc(S("kt_sc"), 1)
                mm(ps[:, 4, 0:TS], rows4, big[:, KSL, TP:T], True, True).then_inc(S("sl_new"), 1)
                pe.wait_ge(S("sl_norm"), hb + 1)
                for k in range(8):
                    if k >= 2:
                        pe.wait_ge(S("sp_trc"), 8 * hb + k - 1)
                    for r in range(4):
                        at = (4 * k + r) * P
                        last = pe.transpose(ps[:, k % 2, r * P:r * P + P], sslc[:, at:at + P], ident)
                    last.then_inc(S("sp_tr"), 1)
                pe.transpose(ps[0:TS, 5, 0:P], sslc[:, PAST:PAST + TS], ident).then_inc(S("spn_tr"), 1)
                pe.wait_ge(S("sp_trc"), 8 * (hb + 1))
                pe.wait_ge(S("spn_trc"), hb + 1)
                for j in range(4):
                    b = 4 * hb + j
                    for hh in range(2):
                        vt = tile_in(pe, "slc", b, "v", hh)
                        for r in range(16):
                            at = (16 * hh + r) * P + 32 * j
                            last = to_rows(b, spt[:, at:at + 32], vt[:, r * P:r * P + P])
                        last.then_inc(S("sv_used"), 1)
                    last = to_rows(b, spn[:, 32 * j:32 * j + 32], vnew[:, 0:P], True)
                last.then_inc(S("so_rows"), 1)
                pe.wait_ge(S("so_copied"), hb + 1)
                pe.transpose(ps[:, 7, P * hb:P * hb + P], orow, ident).then_inc(S("so_done"), 1)

            def cross(l):
                for m in range(8):
                    acc_emptied(pe, ACC[f"xq{l}"] + m)

                def scores(qt):
                    n = 4 * l + qt
                    if n:
                        pe.wait_ge(S("xp_exp"), 4 * n)
                    for hd in range(4):
                        for dc in range(2):
                            c = 2 * hd + dc
                            last = mm(ps[:, 2 + hd // 2, (hd % 2) * 256:(hd % 2) * 256 + 256],
                                      big[:, c, qt * P:qt * P + P], kstore[:, c, :], dc == 0, dc == 1)
                    last.then_inc(S("xp_sc"), 1)

                def turn(qt):
                    n = 4 * l + qt
                    pe.wait_ge(S("xp_norm"), n + 1)
                    if n:
                        pe.wait_ge(S("xp_trc"), 2 * n)
                    for i in range(8):
                        last = pe.transpose(ps[:, 4 + i // 4, (i % 4) * P:(i % 4) * P + P],
                                            xpp[:, i // 2, (i % 2) * P:(i % 2) * P + P], ident)
                        if i % 4 == 3:
                            last.then_inc(S("xp_tr"), 1)

                def values(qt):
                    n = 4 * l + qt
                    pe.wait_ge(S("xp_trc"), 2 * n + 2)
                    if n:
                        pe.wait_ge(S("xo_in"), n)
                    for c in range(8):
                        for kt in range(2):
                            i = 2 * (c // 2) + kt
                            last = mm(ps[:, 6 + c // 4, (c % 4) * P:(c % 4) * P + P], vst2[:, kt, c * P:c * P + P],
                                      xpt[:, i // 4, (i % 4) * P:(i % 4) * P + P], kt == 0, kt == 1)
                    last.then_inc(S("xp_pv"), 1)

                def s_values(hb):
                    for j in range(4):
                        b = 4 * hb + j
                        mv = tile_in(pe, f"mem{l}", b, "v", 0)
                        for f in range(2):
                            for kt in range(2):
                                at = kt * P + 32 * (b // 2)
                                last = mm(ps[32 * j:32 * j + 32, 2 * hb + f, :], xst[:, at:at + 32],
                                          mv[:, kt * 1024 + 512 * f:kt * 1024 + 512 * f + 512], kt == 0, kt == 1)
                        last.then_inc(S("mv_used"), 1)

                def s_turn(hb):
                    pe.wait_ge(S("xv_copied_a"), 2 * l + hb + 1)
                    pe.wait_ge(S("xv_copied_v"), 2 * l + hb + 1)
                    for c in range(8):
                        last = pe.transpose(ps[:, 2 * hb + c // 4, (c % 4) * P:(c % 4) * P + P],
                                            xvr[:, hb, c * P:c * P + P], ident)
                    last.then_inc(S("xv_tr"), 1)

                scores(0)
                pe.wait_ge(S("xq_apart"), l + 1)
                for b in range(NB):
                    mk = tile_in(pe, f"mem{l}", b, "k", 0)
                    rows = slice(32 * (b // 2), 32 * (b // 2) + 32)
                    for c in range(8):
                        last = mm(ps[rows, 1, 0:256], xqd[:, b, c, :], mk[:, c * 256:c * 256 + 256],
                                  b % 2 == 0 and c == 0, b % 2 == 1 and c == 7)
                    last.then_inc(S("mk_used"), 1)
                scores(1)
                turn(0)
                values(0)
                pe.wait_ge(S("xs_norm"), l + 1)
                for kt in range(2):
                    last = pe.transpose(ps[:, 0, 256 + kt * P:256 + kt * P + P], xsp[:, kt * P:kt * P + P], ident)
                last.then_inc(S("xs_tr"), 1)
                scores(2)
                turn(1)
                values(1)
                pe.wait_ge(S("xs_trc"), l + 1)
                s_values(0)
                scores(3)
                turn(2)
                values(2)
                s_turn(0)
                pe.wait_ge(S("xp_exp"), 16 * (l + 1))
                s_values(1)
                turn(3)
                values(3)
                s_turn(1)
                pe.wait_ge(S("xo_in"), 4 * (l + 1))
                pe.wait_ge(S("xv_out_a"), 8 * (l + 1))
                pe.wait_ge(S("xv_out_v"), 8 * (l + 1))

            def layer_end(l):
                linear(f"w_out{l}", mix)
                stats(f"pmix{l}")
                stats(f"mem{l}")
                pe.wait_ge(S("memn_ready"), 8 * (l + 1))
                b0, g0 = WSEG[f"mk{l}"][0], ACC[f"mk{l}"]
                with pe.Fori(0, 2) as i:
                    for j in range(4):
                        acc_free(pe, g0 + j, i)
                        weights_in(pe, b0 + j, i)
                        for k in range(8):
                            last = mm(ps[:, 2 * ((g0 + j) % 4), 0:NMEM], wring[:, (b0 + j) % NSLOT, k * P:k * P + P],
                                      memn[:, k, :], k == 0, k == 7)
                        last.then_inc(ready[(g0 + j) % 4], 1)
                stats(f"xat{l}")
                b0, g0 = WSEG[f"mv{l}"][0], ACC[f"mv{l}"]
                with pe.Fori(0, 2) as i:
                    for j in range(4):
                        acc_free(pe, g0 + j, i)
                        weights_in(pe, b0 + j, i)
                        for k in range(8):
                            for kt in range(2):
                                last = mm(ps[:, 2 * ((g0 + j) % 4) + kt, 0:P], memn[:, k, kt * P:kt * P + P],
                                          wring[:, (b0 + j) % NSLOT, k * P:k * P + P], k == 0, k == 7)
                        last.then_inc(ready[(g0 + j) % 4], 1)
                pe.wait_ge(S("h_ready"), 8 * (3 * l + 2))
                linear(f"xq{l}", h)
                cross(l)
                linear(f"xo{l}", mix)
                stats(f"pxat{l}")
                stats(f"ffn_{l}")
                pe.wait_ge(S("h_ready"), 8 * (3 * l + 3))
                linear(f"ffn{l}", h)
                for m in range(2 * FC - 4, 2 * FC):
                    acc_emptied(pe, ACC[f"ffn{l}"] + m)
                b0, g0 = WSEG[f"down{l}"][0], ACC[f"down{l}"]
                with pe.Fori(0, 2) as i:
                    for j in range(4):
                        acc_free(pe, g0 + j, i)
                        for q in range(2):
                            b = b0 + 2 * j + q
                            pe.wait_ge(wfull[b % NSLOT], 32 * i + 16 * (b // NSLOT + 1))
                            for k in range(KD):
                                for a_ in range(2):
                                    last = mm(accp[(g0 + j) % 4][:, a_, :], wring[:, b % NSLOT, k * P:k * P + P],
                                              big[:, q * KD + k, a_ * H:a_ * H + H], q + k == 0, q == 1 and k == KD - 1,
                                              skip_group_check=True)
                        last.then_inc(ready[(g0 + j) % 4], 1)
                stats(f"pffn{l}")

            pe.wait_ge(S("so_out"), 8)
            layer_end(0)

            stats("mix1")
            pe.wait_ge(S("h_ready"), 8 * 4)
            linear("w_in1", h)
            for m in range(8):
                pe.wait_ge(S("xf_ready"), 2 * (m // 2) + 2)
                for k in range(2):
                    g = ACC["lru"] + 2 * m + k
                    b = WSEG["lru"][0] + m // 2
                    acc_free(pe, g)
                    weights_in(pe, b)
                    for kc in range(2):
                        t = (2 * m + k) * 2 + kc
                        for a_ in range(2):
                            last = mm(accp[g % 4][:, a_, :], wring[:, b % NSLOT, (t % 8) * P:(t % 8) * P + P],
                                      mix[:, m // 2 * 2 + kc, a_ * H:a_ * H + H], kc == 0, kc == 1, skip_group_check=True)
                    last.then_inc(ready[g % 4], 1)
            pe.wait_ge(S("lmix_ready"), 8)
            layer_end(1)


def _chunks(x):
    return np.ascontiguousarray(x.T.reshape(-1, P, x.shape[0]).transpose(1, 0, 2))


def _blocks(w, tiles):
    k, n = w.shape
    t = w.reshape(k // P, P, n // P, P).transpose(2, 0, 1, 3).reshape(-1, tiles, P, P)
    return np.ascontiguousarray(t.transpose(0, 2, 1, 3).reshape(-1, P, tiles * P))


def kernel(**inputs):
    import concourse.bacc as bacc
    from concourse.bass_utils import run_bass_kernel_spmd

    v = {k: np.asarray(t) for k, t in inputs.items()}
    arr = {}
    arr["xp"] = _chunks(v["x_prompt"][0])
    arr["xs"] = _chunks(v["x_sample"].reshape(TS, D))
    arr["mem"] = _chunks(v["mem_prompt"][0])
    past = v["state_pool"][0].transpose(2, 0, 1)
    past = np.pad(past, ((0, 0), (0, 0), (0, 4))).reshape(4, P, NB * 19)
    arr["poolold"] = np.ascontiguousarray(v["state_pool"][0, :, NT:]).reshape(P, -1)
    arr["poolpast"] = np.ascontiguousarray(past.transpose(1, 0, 2))
    for n, k in (("cmpk", "cache_cmp_k"), ("cmpv", "cache_cmp_v"), ("slck", "cache_slc_k"), ("slcv", "cache_slc_v")):
        arr[n] = np.ascontiguousarray(v[k]).reshape(-1, SUB * P)
    wk = v["cache_win_k"][0].reshape(NB, 512, P)
    wv = v["cache_win_v"][0].reshape(NB, 512, P)
    arr["winold_k"] = np.ascontiguousarray(wk[:, 4:]).reshape(P, -1)
    arr["winold_v"] = np.ascontiguousarray(wv[:, 4:]).reshape(P, -1)
    arr["wink"] = np.ascontiguousarray(wk.transpose(2, 0, 1).reshape(P, 2, 4 * 512).transpose(1, 0, 2))
    arr["winv"] = np.ascontiguousarray(
        wv.reshape(2, 4, 4, P, P).transpose(0, 3, 1, 2, 4).reshape(2, P, 4 * 512))
    arr["memk"] = np.ascontiguousarray(
        v["cache_mem_k"].reshape(2, NB, NMEM, 8, P).transpose(0, 1, 4, 3, 2).reshape(2, NB, P, 2048))
    arr["memv"] = np.ascontiguousarray(
        v["cache_mem_v"].reshape(2, NB, 2, P, D).transpose(0, 1, 3, 2, 4).reshape(2, NB, P, 2048))
    pt = v["page_table"].reshape(NB, 2, 16).astype(np.int32)
    arr["pages"] = np.ascontiguousarray(np.repeat(pt, 8, axis=2).transpose(2, 0, 1).reshape(P, 16))
    arr["const"] = CONSTANTS
    cols = [v["norm_gain"].reshape(96, P), v["mem_norm_gain"].reshape(16, P), v["pool_scale"].reshape(4, P),
            v["conv_w"].reshape(32, P), v["conv_b"].reshape(8, P), v["lru_ba"].reshape(8, P),
            v["lru_bx"].reshape(8, P), v["lru_lambda"].reshape(8, P)]
    arr["param"] = np.ascontiguousarray(np.concatenate(cols, axis=0).T)
    arr["poolw"] = np.ascontiguousarray(v["pool_w"][0].transpose(1, 0, 2))
    bd = np.zeros((P, 2, P), np.float32)
    for g in range(2):
        bd[64 * g:64 * g + 64, 0, 64 * g:64 * g + 64] = v["w_cmp_k"][0, g]
        bd[64 * g:64 * g + 64, 1, 64 * g:64 * g + 64] = v["w_cmp_v"][0, g]
    arr["wcmp"] = bd
    arr["lruh"] = np.ascontiguousarray(v["state_lru_h"][0].reshape(NB, 8, P).transpose(2, 1, 0))
    lc = np.pad(v["state_lru_conv"][0].transpose(2, 0, 1), ((0, 0), (0, 0), (0, 4)))
    arr["lruconv"] = np.ascontiguousarray(lc.reshape(8, P, NB * 7).transpose(1, 0, 2))
    wi = v["w_in_even"][0]
    q = wi[:, 512:1024].reshape(D, 2, 4, 64).transpose(0, 2, 1, 3).reshape(D, 512)
    wi = np.pad(np.concatenate([wi[:, :512], q, wi[:, 1024:]], axis=1), ((0, 0), (0, NIN * P - wi.shape[1])))
    wo = v["w_out_even"][0]
    wo = np.concatenate([wo[:512], wo[512:].reshape(2, 4, 64, D).transpose(1, 0, 2, 3).reshape(512, D)], axis=0)
    wts = {"w_in": _blocks(wi, 8), "w_out0": _blocks(wo, 8), "w_in1": _blocks(v["w_in_odd"][0], 8),
           "w_out1": _blocks(v["w_out_odd"][0], 8)}
    for l in range(2):
        for n, k in (("xq", "w_xq"), ("mk", "w_xk"), ("mv", "w_xv"), ("xo", "w_xo")):
            wts[f"{n}{l}"] = _blocks(v[k][l], 8)
        gu = np.stack([v["w_ffn_gate"][l].reshape(D, FC, P), v["w_ffn_up"][l].reshape(D, FC, P)], axis=2)
        wts[f"ffn{l}"] = _blocks(gu.reshape(D, 2 * DFF), 8)
        wts[f"down{l}"] = _blocks(v["w_ffn_down"][l], KD)
    ax = np.stack([v["lru_wa"][0], v["lru_wx"][0]], axis=0).reshape(2, 4, 2, P, 2, P)
    ax = ax.transpose(1, 4, 0, 2, 3, 5).reshape(4, 8, P, P)
    wts["lru"] = np.ascontiguousarray(ax.transpose(0, 2, 1, 3).reshape(4, P, 8 * P))
    outs = {
        "yp": [P, KC, TP], "ys": [P, KC, TS], "pool": [P, 4, 15 + TS], "poolold": [P, NB * 11 * 4], "kv": [6, P, T],
        "wink_s": [P, NB * 508], "winv_s": [P, NB * 508], "memk": [2, P, 8, NMEM], "memv": [2, P, 8, 256],
        "conv_p": [P, 8, 3], "conv_s": [P, 8, NB, 3], "lru_h": [P, 8, 9],
    }
    nc = bacc.Bacc("TRN2", target_bir_lowering=False, num_devices=1)
    feed = {f"in_{n}": t for n, t in arr.items()} | {f"w_{n}": t for n, t in wts.items()}
    a = {n: nc.dram_tensor(f"in_{n}", t.shape, mybir.dt.from_np(t.dtype), kind="ExternalInput").ap() for n, t in arr.items()}
    w = {n: nc.dram_tensor(f"w_{n}", t.shape, F32, kind="ExternalInput").ap() for n, t in wts.items()}
    o = {n: nc.dram_tensor(f"out_{n}", s, F32, kind="ExternalOutput").ap() for n, s in outs.items()}
    decoder_step(nc, a, w, o)
    r = run_bass_kernel_spmd(nc, [feed], core_ids=[0]).results[0]
    r = {n: np.asarray(r[f"out_{n}"]) for n in outs}

    def rows(t):
        return t.transpose(2, 1, 0).reshape(t.shape[2], -1)

    yp = rows(r["yp"]).reshape(1, TP, D)
    ys = rows(r["ys"]).reshape(NB, NT, D)
    pool = rows(r["pool"])
    pool_p = pool[:15].reshape(1, 1, 15, 512)
    pool_new = pool[15:].reshape(1, NB, NT, 512)
    past_rows = r["poolold"].reshape(1, NB, 11, 512)
    pool_s = np.concatenate([past_rows, pool_new], axis=2)
    kv = [rows(r["kv"][i][:, None, :]) for i in range(6)]
    kvp = [t[:TP].reshape(1, 1, TP, 2, 64) for t in kv]
    kvs = [t[TP:].reshape(NB, 1, NT, 2, 64) for t in kv]
    win = []
    for i, n in ((4, "wink_s"), (5, "winv_s")):
        win.append(kv[i][:TP].reshape(1, 1, TP, 2, 64))
        old = r[n].reshape(1, NB, 508, 2, 64)
        win.append(np.concatenate([old, kv[i][TP:].reshape(1, NB, NT, 2, 64)], axis=2))
    lh = r["lru_h"].transpose(2, 1, 0).reshape(9, D)
    conv_p = r["conv_p"].transpose(2, 1, 0).reshape(1, 1, 3, D)
    conv_s = r["conv_s"].transpose(2, 3, 1, 0).reshape(1, NB, 3, D)
    mk = r["memk"].transpose(0, 3, 2, 1).reshape(2, 1, NMEM, 4, 256)
    mv = r["memv"].reshape(2, P, 2, D).transpose(0, 2, 1, 3).reshape(2, 1, NMEM, 4, 256)
    return (yp, ys, pool_p, pool_s, kvp[0], kvs[0], kvp[1], kvs[1], kvp[2], kvs[2], kvp[3], kvs[3],
            win[0], win[1], win[2], win[3], lh[:1].reshape(1, 1, D), lh[1:].reshape(1, NB, D), conv_p, conv_s, mk, mv)
```

```python
from contextlib import ExitStack

import numpy as np

import concourse.bass as bass
from concourse import mybir

F32 = mybir.dt.float32
F32R = mybir.dt.float32r
I32 = mybir.dt.int32
U32 = mybir.dt.uint32
ALU = mybir.AluOpType
ACT = mybir.ActivationFunctionType
AXX = mybir.AxisListType.X

P = 128
D = 1024
KC = D // P
TP = 512
NB, NT = 8, 4
TS = NB * NT
T = TP + TS
H = T // 2
DFF = 2816
FC = DFF // P
KB = 8
DB = -(-FC // KB)
AFTER = 3
NMEM = 256
PAST = 4096
PAGE = 128
NPAGE = PAST // PAGE
SUB = 16
NSUB = PAST // SUB
POOLW = (2, 4, 8, 16)
EPS = 1e-6
NEG = -1e30
FORCE = 1e30
SC = 64 ** -0.5
SX = 256 ** -0.5
NIN = 15
U, Q, KCM, VCM, KSL, VSL, KWI, VWI, GT = 0, 4, 8, 9, 10, 11, 12, 13, 14
NSLOT = 4
NC = 4
EXT = 16 + TP + NB * 19
CEX = 3 + TP + NB * 7

WSEG = {}


def _segments():
    at = 0
    for name, blocks, tiles in [
        ("w_in", NIN, 8), ("w_out0", 8, 8), ("mk0", 8, 8), ("mv0", 8, 8), ("xq0", 8, 8), ("xo0", 8, 8),
        ("ffn0", 2 * FC, 8), ("down0", 8 * DB, 8),
        ("w_in1a", 8, 8), ("lru", 4, 8), ("w_in1b", 8, 8), ("w_out1", 8, 8), ("mk1", 8, 8), ("mv1", 8, 8), ("xq1", 8, 8),
        ("xo1", 8, 8), ("ffn1", 2 * FC, 8), ("down1", 8 * DB, 8),
    ]:
        WSEG[name] = (at, blocks, tiles)
        at += blocks
    return at


NBLK = _segments()

ACC = {}
NORMS = ["mix0", "mem0", "pmix0", "xat0", "pxat0", "ffn_0", "pffn0",
         "mix1", "mem1", "pmix1", "xat1", "pxat1", "ffn_1", "pffn1"]
NORM = {n: i for i, n in enumerate(NORMS)}
INNER = {"w_out0": "mem0", "xq0": "xat0", "ffn0": "ffn_0", "w_in1a": "mix1",
         "w_out1": "mem1", "xq1": "xat1", "ffn1": "ffn_1"}
FIRST = []


def _accumulators():
    n = 1
    ACC["s_mix0"] = 0
    for m in range(NIN):
        FIRST.append(("in", m))
        if m % 2 == 1:
            FIRST.append(("mean", m // 2))
        elif m >= 2:
            FIRST.append(("cmp", m // 2 - 1))
    FIRST.append(("mean", 7))
    for c in range(4):
        FIRST.append(("pool", c))
    FIRST.append(("cmp", 7))
    for i, (kind, k) in enumerate(FIRST):
        ACC[kind, k] = n + i
    n += len(FIRST)

    def place(name, k):
        nonlocal n
        ACC[name] = n
        n += k
        if name in INNER:
            ACC["s_" + INNER[name]] = ACC[name] + AFTER
            n += 1

    for l in range(2):
        if l == 1:
            for name, k in (("w_in1a", 8), ("lru", 16), ("w_in1b", 8)):
                place(name, k)
        for name, k in [(f"w_out{l}", 8), (f"s_pmix{l}", 1), (f"mk{l}", 8), (f"mv{l}", 8), (f"xq{l}", 8), (f"xo{l}", 8),
                        (f"s_pxat{l}", 1), (f"ffn{l}", 2 * FC), (f"down{l}", 8), (f"s_pffn{l}", 1)]:
            place(name, k)
    return n


NACC = _accumulators()


def acc_of(name, i):
    return ACC[name] + i + (name in INNER and i >= AFTER)


def _consumer(b):
    for name, (b0, k, _) in WSEG.items():
        if b0 <= b < b0 + k:
            i = b - b0
            if name == "w_in":
                return ACC["in", i]
            if name == "lru":
                return ACC["lru"] + 4 * i + 3
            if name.startswith("down"):
                return ACC[name] + i // DB
            return acc_of(name, i)
    raise ValueError(b)


def _part(b):
    for l in range(2):
        b0, k, _ = WSEG[f"down{l}"]
        if b0 <= b < b0 + k and (b - b0) % DB < DB - 1:
            return (DB - 1) * (8 * l + (b - b0) // DB) + (b - b0) % DB
    return None


SPLIT = [b for name, (b0, k, _) in WSEG.items() if name not in ("w_in", "lru") for b in range(b0, b0 + k)]
NSPLIT = {b: n for n, b in enumerate(SPLIT)}

TILES = [("cmp", b, kv, h) for b in range(NB) for kv in "kv" for h in range(2)]
for _hb in range(2):
    TILES += [("win", _hb, kv, 0) for kv in "kv"]
    TILES += [("slc", 4 * _hb + j, "k", h) for j in range(4) for h in range(2)]
    TILES += [("slc", 4 * _hb + j, "v", h) for j in range(4) for h in range(2)]
TILES += [("mem0", b, kv, 0) for kv in "kv" for b in range(NB)]
TILES += [("mem1", b, kv, 0) for kv in "kv" for b in range(NB)]
TILE = {t: i for i, t in enumerate(TILES)}

CONST = {}


def _constants():
    parts = []
    at = 0

    def put(name, a):
        nonlocal at
        a = np.asarray(a, np.float32).reshape(P, -1)
        CONST[name] = (at, a.shape[1])
        parts.append(a)
        at += a.shape[1]

    p = np.arange(P)
    put("ident", np.eye(P))
    put("ones", np.ones((P, P)))
    put("causal", np.where(p[None, :] > p[:, None], NEG, 0.0))
    a = np.zeros((2, P, NSUB))
    for s in range(NSUB):
        for i in (s, s - 1):
            if 0 <= i < NSUB - 1:
                a[s // P, s % P, i] = 1.0 / 32.0
    put("pair", a.transpose(1, 0, 2))
    t = (np.arange(4)[None, :] * P + p[:, None])[:, :, None]
    i = np.arange(32)[None, None, :]
    put("cmpbias", np.where((i * 16 + 31 <= t) & (i < 31), 0.0, NEG))
    put("anyblock", (p >= 31).astype(np.float32))
    j, g, c, tt = p // 32, p // 16 % 2, p // 4 % 4, p % 4
    key = np.arange(TS)
    for hb in range(2):
        own = (key[None, :] // 4 == 4 * hb + j[:, None]) & (key[None, :] % 4 <= tt[:, None])
        put(f"newbias{hb}", np.where(own, 0.0, NEG))
        put(f"rep{hb}", np.pad((key[:, None] == (16 * hb + 4 * j + tt)[None, :]).astype(np.float32), ((0, 96), (0, 0))))
    put("oldbias", np.where(np.arange(4)[None, :] <= tt[:, None], NEG, 0.0))
    put("headmask", np.repeat(np.arange(8)[None, :] == (4 * g + c)[:, None], 3, axis=1))
    same = (j[:, None] == j[None, :]) & (g[:, None] == g[None, :]) & (tt[:, None] == tt[None, :])
    put("heads", same)
    fix = np.ones((4, 16))
    for k, w in enumerate(POOLW):
        fix[k, :w] = w / np.minimum(np.arange(w) + 1.0, w)
    put("poolfix", np.broadcast_to(fix.reshape(1, -1), (P, 64)))
    put("subrow", (p % 8))
    return np.concatenate(parts, axis=1)


CONSTANTS = _constants()

PARAM = {"gain": 0, "memgain": 96, "poolscale": 112, "convw": 116, "convb": 148, "ba": 156, "bx": 164, "lam": 172}
NPARAM = 180


def decoder_step(nc, a, w, o):
    with ExitStack() as ctx:
        def sb(name, shape, dt=F32):
            return ctx.enter_context(nc.sbuf_tensor(name, shape, dt))

        def sb_both(name, shape):
            at = -(-nc.sbuf_base // 32) * 32
            t = sb(name, shape)
            r = nc.alloc_sbuf_tensor_at(name + "_r", shape, F32R, offset=at)
            assert nc.sbuf_base == at + 4 * int(np.prod(shape[1:]))
            return t, r

        sems = {}

        def S(name):
            if name not in sems:
                sems[name] = ctx.enter_context(nc.semaphore(name))
            return sems[name]

        x = sb("x", [P, KC, T])
        work, work_r = sb_both("work", [P, 2 * KC, T])
        h = work[:, 0:KC, :]
        y = work[:, KC:2 * KC, :]
        mc, mc_r = sb_both("mc", [P, KC * T + NC * 2048])
        mix = mc[:, 0:KC * T].rearrange("p (c t) -> p c t", c=KC)
        big, big_r = sb_both("big", [P, FC, T])
        wring, wring_r = sb_both("wring", [P, NSLOT, KB * P])
        whi = sb("whi", [P, 2, KB * P], F32R)
        cring = mc[:, KC * T:KC * T + NC * 2048].rearrange("p (s n) -> p s n", s=NC)
        kstore = sb("kstore", [P, 8, 256])
        vstore = sb("vstore", [P, 8, 256])
        cst = sb("cst", [P, CONSTANTS.shape[1]])
        par = sb("par", [P, NPARAM])
        sq = sb("sq", [P, 2, T])
        ssum = sb("ssum", [P, T])
        rms = sb("rms", [P, T])
        rinv = sb("rinv", [P, T])
        idx = sb("idx", [P, 16], I32)
        small = sb("small", [P, 640])
        epsc = sb("epsc", [P, 1])
        spb = sb("spb", [P, 64])
        lh0 = sb("lh0", [P, 8, 8])
        lh = sb("lh", [P, 8, 9])
        ps = ctx.enter_context(nc.psum_tensor("ps", [P, 8, 512], F32))

        def C(name):
            at, n = CONST[name]
            return cst[:, at:at + n]

        def G(name, k):
            return par[:, PARAM[name] + k:PARAM[name] + k + 1]

        def halves(ap):
            return ap.rearrange("p (a n) -> p a n", a=2)

        swork = work[:, :, :].rearrange("p c t -> p (c t)")
        ybase = KC * T
        ext = swork[:, ybase:ybase + 4 * EXT].rearrange("p (g n) -> p g n", g=4)
        poolw_sb = swork[:, ybase + 4 * EXT:ybase + 4 * EXT + 512].rearrange("p (g n) -> p g n", g=4)
        wcmp_sb = swork[:, ybase + 4 * EXT + 512:ybase + 4 * EXT + 768].rearrange("p (g n) -> p g n", g=2)
        bufs = [mix[:, 0:2, :].rearrange("p c t -> p (c t)")[:, 0:EXT],
                mix[:, 2:4, :].rearrange("p c t -> p (c t)")[:, 0:EXT]]
        flat = big[:, 15:22, :].rearrange("p c t -> p (c t)")
        ktb = flat[:, 0:1024].rearrange("p (b n) -> p b n", b=2)
        meant = flat[:, 1024:1536].rearrange("p (k n) -> p k n", k=2)
        vcp4 = flat[:, 1024:1536].rearrange("p (q n) -> p q n", q=4)
        subs = flat[:, 1536:2560].rearrange("p (b n) -> p b n", b=8)
        mv4 = flat[:, 1536:2048].rearrange("p (q n) -> p q n", q=4)
        vnew = flat[:, 2048:2304]
        grw = flat[:, 2304:2328]
        pcs = flat[:, 2352:2448].rearrange("p (k n) -> p k n", k=3)
        s32 = flat[:, 2448:2512].rearrange("p (k n) -> p k n", k=2)
        vnat = flat[:, 2560:3584].rearrange("p (v k n) -> p v k n", v=2, k=4)
        pp = swork[:, 0:2048].rearrange("p (u r n) -> p u r n", u=2, r=2)
        ppt = swork[:, 2048:4096].rearrange("p (u r n) -> p u r n", u=2, r=2)
        pcm = swork[:, 4096:5120]
        pct = swork[:, 5120:6144].rearrange("p (k n) -> p k n", k=2)
        sslc = swork[:, 0:PAST + TS]
        spt = swork[:, ybase:ybase + PAST]
        uflat = big[:, 0:4, :].rearrange("p c t -> p (c t)")
        pce = uflat[:, 0:264]
        swin = uflat[:, 264:808]
        pwt = uflat[:, 808:1320]
        pst2 = uflat[:, 1320:1576]
        orow = pst2[:, 0:P]
        pwn = uflat[:, 1576:1704]
        spn = uflat[:, 1704:1832]
        maskb = uflat[:, 1832:1904]
        sel = uflat[:, 1904:1976]
        m8 = uflat[:, 1976:1984]
        qbd = small[:, 0:256]
        kcp = small[:, 256:288]
        gpr = small[:, 288:384].rearrange("p (q n) -> p q n", q=4)
        gtok = small[:, 384:408]
        mp = small[:, 408:440]
        grow = small[:, 440:446].rearrange("p (k n) -> p k n", k=2)
        sst = small[:, 448:472].rearrange("p (k n) -> p k n", k=6)
        pst = small[:, 472:488].rearrange("p (u r n) -> p u r n", u=2, r=2)
        xsm = small[:, 488:492]
        xpm = small[:, 492:508]
        tmp8 = small[:, 512:576].rearrange("p (c b) -> p c b", c=8)
        flatx = big[:, 8:22, :].rearrange("p c t -> p (c t)")
        xpp = flatx[:, 0:1024].rearrange("p (h n) -> p h n", h=4)
        xpt = flatx[:, 1024:2048].rearrange("p (k n) -> p k n", k=2)
        xst = flatx[:, 2048:2304]
        xsp = flatx[:, 2304:2560]
        xqd = flatx[:, 2560:4608].rearrange("p (b c n) -> p b c n", b=NB, c=8)
        xvr = flatx[:, 2560:4608].rearrange("p (b n) -> p b n", b=2)
        memn = flatx[:, 5568:7616].rearrange("p (c n) -> p c n", c=8)
        vst2 = vstore[:, :, :].rearrange("p b n -> p (b n)").rearrange("p (k n) -> p k n", k=2)
        cext = big[:, 13:22, :].rearrange("p c t -> p (c t)")[:, 0:8 * CEX].rearrange("p (c n) -> p c n", c=8)
        flatx_r = big_r[:, 8:22, :].rearrange("p c t -> p (c t)")
        memhi = flatx_r[:, 0:2048].rearrange("p (c n) -> p c n", c=8)
        memlo = flatx_r[:, 5568:7616].rearrange("p (c n) -> p c n", c=8)
        hidhi = mc_r[:, 0:FC * T].rearrange("p (c t) -> p c t", c=FC)
        hr, yr = work_r[:, 0:KC, :], work_r[:, KC:2 * KC, :]
        mixr = mc_r[:, 0:KC * T].rearrange("p (c t) -> p c t", c=KC)
        yb = mc[:, KC * T:2 * KC * T].rearrange("p (c t) -> p c t", c=KC)
        cv = [mc[:, 2 * KC * T + q * CEX:2 * KC * T + (q + 1) * CEX] for q in range(2)]
        uprow = kstore[:, :, :].rearrange("p b n -> p (b n)")[:, 0:2 * T].rearrange("p (b t) -> p b t", b=2)
        lsp = spb[:, 0:8]
        lsn = spb[:, 8:16]
        ident = C("ident")

        accp = [ps[:, 2 * q:2 * q + 2, 0:H] for q in range(4)]
        ready = [S(f"acc_ready{q}") for q in range(4)]
        drained = [S(f"acc_drained{q}") for q in range(4)]
        wfull = [S(f"weights_full{s}") for s in range(NSLOT)]
        cfull = [S(f"cache_full{s}") for s in range(NC)]

        def acc_free(e, g, i=0):
            if g >= 4:
                e.wait_ge(drained[g % 4], i + g // 4)

        def acc_done(e, g, i=0):
            e.wait_ge(ready[g % 4], i + (g // 4 + 1))

        def acc_emptied(e, g, i=0):
            e.wait_ge(drained[g % 4], i + (g // 4 + 1))

        def weights_in(e, b, i=0):
            e.wait_ge(wfull[b % NSLOT], 16 * i + 16 * (b // NSLOT + 1))

        def block_used(e, b, i=0):
            part = _part(b)
            if part is None:
                acc_done(e, _consumer(b), i)
            else:
                e.wait_ge(S("part_used"), part + 1)

        def F(ap):
            return ap.bitcast(F32)

        def block_at(b, tiles):
            return (wring[:, b % NSLOT, 0:tiles * P], wring_r[:, b % NSLOT, 0:tiles * P],
                    whi[:, NSPLIT[b] % 2, 0:tiles * P])

        def tiles_of(b):
            for l in range(2):
                b0, k, _ = WSEG[f"down{l}"]
                if b0 <= b < b0 + k and (b - b0) % DB == DB - 1:
                    return FC - KB * (DB - 1)
            return KB

        def tile_in(e, *t):
            n = TILE[t]
            e.wait_ge(cfull[n % NC], 16 * (n // NC + 1))
            return cring[:, n % NC, :]

        def s_places(hb, hd, q):
            src = ps[:, 2 * hb + hd // 2, (hd % 2) * 256:(hd % 2) * 256 + 256].rearrange("p (d j r) -> p d j r", d=2, j=2)
            dst = mix[:, 2 * hd:2 * hd + 2, TP + 16 * hb:TP + 16 * hb + 16].rearrange("p d (j r) -> p d j r", j=2)
            return dst[:, :, :, 4 * q:4 * q + 4], src[:, :, :, 48 * q + 4 * hd:48 * q + 4 * hd + 4]

        def sample(ap):
            return ap.rearrange("p (b t) -> p b t", b=NB)

        block = ctx.enter_context(nc.Block())

        @block.sync
        def _(sp):
            sp.dma_start(x[:, :, TP:T], a["xs"]).then_inc(S("xs_loaded"), 16)
            for c in range(4):
                sp.dma_start(x[:, 2 * c:2 * c + 2, 0:TP], a["xp"][:, 2 * c:2 * c + 2, :]).then_inc(S(f"x_loaded{c}"), 16)
            sp.dma_start(par[:, :], a["param"]).then_inc(S("const_loaded"), 16)
            sp.dma_start(cst[:, :], a["const"]).then_inc(S("const_loaded"), 16)
            sp.dma_start(poolw_sb, a["poolw"]).then_inc(S("small_loaded"), 16)
            sp.dma_start(wcmp_sb, a["wcmp"]).then_inc(S("small_loaded"), 16)
            sp.dma_start(lh0[:, :, :], a["lruh"]).then_inc(S("h0_loaded"), 16)

            def load(name):
                b0, k, tiles = WSEG[name]
                dst = [wring[:, s, :] for s in range(NSLOT)]
                looped = k == 2 * FC
                for i in range(8 if looped else k):
                    b = b0 + i
                    if b >= NSLOT:
                        block_used(sp, b - NSLOT)
                    n = tiles_of(b) * P
                    sp.dma_start(dst[b % NSLOT][:, 0:n], w[name][i][:, 0:n]).then_inc(wfull[b % NSLOT], 16)
                    if i == 3 and name.startswith("w_out"):
                        if name == "w_out0":
                            sp.wait_ge(S("so_done"), 2)
                        else:
                            sp.wait_ge(S("lmix_ready"), 8)
                        sp.dma_start(memn, a["mem"]).then_inc(S("mem_loaded"), 16)
                    if i == 3 and name == "w_in1a":
                        acc_done(sp, ACC["down0"] + 7)
                        sp.wait_ge(S("conv_zero"), 1)
                        sp.dma_start(cext[:, :, 3 + TP:CEX], a["lruconv"]).then_inc(S("conv_past"), 16)
                if looped:
                    with sp.Fori(0, k // 4 - 2) as i:
                        for j in range(4):
                            acc_done(sp, _consumer(b0 + 4 + j), i)
                            s = (b0 + j) % NSLOT
                            sp.dma_start(dst[s], w[name][4 * i + (8 + j)]).then_inc(wfull[s], 16)

            for name in WSEG:
                load(name)
            for name, n in (("out_pool", 1), ("out_kv", 6), ("win_copied", 3), ("out_mem", 4), ("out_conv", 9),
                            ("out_y", 2), ("out_lru", 1)):
                sp.wait_ge(S(name), 16 * n)

        @block.gpsimd
        def _(pool):
            pool.dma_start(idx[:, :], a["pages"]).then_inc(S("pages_loaded"), 16)
            pool.memset(epsc[:, :], EPS).then_inc(S("eps_set"), 1)
            pool.memset(ext, 0.0).then_inc(S("ext_zero"), 1)
            pool.memset(qbd, 0.0).then_inc(S("qbd_zero"), 1)
            pool.wait_ge(S("ext_zero"), 1)
            pool.dma_start(ext[:, :, 16 + TP:EXT], a["poolpast"]).then_inc(S("pool_past"), 16)
            pool.dma_start(o["wink_s"], a["winold_k"]).then_inc(S("win_copied"), 16)
            pool.dma_start(o["winv_s"], a["winold_v"]).then_inc(S("win_copied"), 16)
            pool.dma_start(o["poolold"], a["poolold"]).then_inc(S("win_copied"), 16)

            def tile_used(n):
                kind, b, kv, hh = TILES[n]
                if kind == "cmp":
                    pool.wait_ge(S("sub_ready"), n + 1)
                elif kind == "win":
                    pool.wait_ge(S("sw_sc" if kv == "k" else "sw_pv"), b + 1)
                elif kind == "slc" and kv == "k":
                    pool.wait_ge(S("kt_tr"), 4 * (2 * b + hh + 1))
                elif kind == "slc":
                    pool.wait_ge(S("sv_used"), 2 * b + hh + 1)
                else:
                    pool.wait_ge(S("mk_used" if kv == "k" else "mv_used"), 8 * int(kind[3]) + b + 1)

            def tile(n):
                kind, b, kv, hh = TILES[n]
                s = n % NC
                if n >= NC:
                    tile_used(n - NC)
                dst = cring[:, s, :]
                if kind == "cmp" or kind == "slc":
                    pool.indirect_dma_start(dst, None, a[kind + kv], bass.IndirectOffsetOnAxis(
                        ap=idx[:, 2 * b + hh:2 * b + hh + 1].bitcast(U32), axis=0)).then_inc(cfull[s], 16)
                elif kind == "win":
                    pool.dma_start(dst, a["win" + kv][b]).then_inc(cfull[s], 16)
                else:
                    pool.dma_start(dst, a["mem" + kv][int(kind[3]), b]).then_inc(cfull[s], 16)

            def add(r):
                for c in range(8):
                    pool.wait_ge(S("y_scaled"), 8 * r + c + 1)
                    pool.tensor_tensor(x[:, c, :], x[:, c, :], y[:, c, :], ALU.add).then_inc(S("x_ready"), 1)

            def sums(name):
                n = NORM[name]
                wd = NMEM if name.startswith("mem") else T
                for c in range(1, 7):
                    pool.wait_ge(S("sq_ready"), 8 * n + c + 1)
                    if c == 1 and n:
                        pool.wait_ge(S("rms_ready"), n)
                    if c > 1:
                        pool.wait_ge(S("sq_summed"), 6 * n + c - 1)
                    pool.tensor_tensor(ssum[:, 0:wd], sq[:, 0, 0:wd] if c == 1 else ssum[:, 0:wd], sq[:, c % 2, 0:wd],
                                       ALU.add).then_inc(S("sq_summed"), 1)

            pool.wait_ge(S("idx_ready"), 1)
            for n in range(NC):
                tile(n)
            sums("mix0")
            k = 0
            at = NC
            for g in range(4):
                pool.wait_ge(S("ext_ready"), g + 1)
                if g:
                    pool.wait_ge(S("pool_d"), g)
                src, lo = ext[:, g, :], 0
                for lev in range(g + 1):
                    dst = bufs[lev % 2]
                    sh = 1 << lev
                    if lev:
                        pool.wait_ge(S("win_step"), k)
                    lo += sh
                    pool.tensor_tensor(dst[:, lo:EXT], src[:, lo:EXT], src[:, lo - sh:EXT - sh],
                                       ALU.add).then_inc(S("win_step"), 1)
                    k += 1
                    src = dst
                pool.wait_ge(S("win_step"), k)
                pool.tensor_tensor(src[:, 16:32], src[:, 16:32], C("poolfix")[:, 16 * g:16 * g + 16],
                                   ALU.mult).then_inc(S("win_step"), 1)
                k += 1
                for _ in range(6):
                    tile(at)
                    at += 1
            for n in range(at, TILE["mem0", 0, "k", 0]):
                tile(n)
            for l in range(2):
                if l:
                    sums("mix1")
                    for m in range(8):
                        acc_emptied(pool, ACC["lru"] + 2 * m + 1)
                        pool.tensor_tensor(big[:, 8 + m, :], big[:, 8 + m, :], mix[:, m, :], ALU.mult).then_inc(S("gated"), 1)
                    pool.wait_ge(S("lmix_ready"), 8)
                n0 = TILE[f"mem{l}", 0, "k", 0]
                for n in range(n0, n0 + NC):
                    tile(n)
                sums(f"mem{l}")
                sums(f"pmix{l}")
                add(3 * l)
                acc_done(pool, acc_of(f"w_out{l}", 7))
                if l == 0:
                    pool.wait_ge(S("out_kv"), 16 * 6)
                pool.memset(xqd, 0.0).then_inc(S("xq_zero"), 1)
                sums(f"xat{l}")
                for n in range(n0 + NC, n0 + 16):
                    tile(n)
                sums(f"pxat{l}")
                add(3 * l + 1)
                sums(f"ffn_{l}")
                sums(f"pffn{l}")
                add(3 * l + 2)

        @block.scalar
        def _(act):
            act.wait_ge(S("const_loaded"), 32)
            act.wait_ge(S("eps_set"), 1)
            act.wait_ge(S("sp_abs"), 1)
            act.activation(spb[:, 16:24], spb[:, 24:32], ACT.Exp, scale=-1.0).then_inc(S("sp_exp"), 1)

            def square(name, c, src):
                n = NORM[name]
                wd = NMEM if name.startswith("mem") else T
                if c >= 2:
                    act.wait_ge(S("sq_summed"), 6 * n + max(c - 2, 1))
                elif c == 0 and n:
                    act.wait_ge(S("sq_summed"), 6 * n)
                dst = sq[:, c % 2, 0:wd]
                if len(src.shape) == 3:
                    dst = halves(dst)
                act.activation(dst, src, ACT.Square).then_inc(S("sq_ready"), 1)

            def root(name):
                g = ACC["s_" + name]
                acc_done(act, g)
                if NORM[name]:
                    act.wait_ge(S("rinv_ready"), NORM[name])
                if name.startswith("mem"):
                    src, dst = ps[:, 2 * (g % 4), 0:NMEM], rms[:, 0:NMEM]
                else:
                    src, dst = accp[g % 4], halves(rms[:, :])
                act.activation(dst, src, ACT.Sqrt, bias=epsc[:, 0:1], scale=1.0 / D).then_inc(S("rms_ready"), 1)
                act.wait_ge(S("rms_ready"), NORM[name] + 1)
                act.sem_inc(drained[g % 4], 1)

            def w_hi(b, i=0):
                weights_in(act, b, i)
                n = NSPLIT[b]
                if n >= 2:
                    block_used(act, SPLIT[n - 2], i)
                src, _, dst = block_at(b, tiles_of(b))
                act.activation(dst, src, ACT.Copy).then_inc(S("w_hi"), 1)

            def w_next(name, m, i=0):
                b = WSEG[name][0] + m + 2
                w_hi(b, i)

            def ahead(name):
                r = ["xat0", "ffn_0", "mix1", "xat1", "ffn_1"].index(name)
                for c in range(8):
                    act.wait_ge(S("x_ready"), 8 * r + c + 1)
                    act.activation(hr[:, c, :], x[:, c, :], ACT.Copy, scale=G("gain", 16 * (r + 1) + c)).then_inc(S("xg_ready"), 1)

            def mix_hi(sem=None):
                for c in range(8):
                    if sem:
                        act.wait_ge(S(sem), c + 1)
                    act.activation(hr[:, c, :], mix[:, c, :], ACT.Copy).then_inc(S("mix_hi"), 1)

            def evict_y(name, norm, gain):
                down = name.startswith("down")
                for m in range(8):
                    g = acc_of(name, m)
                    for q in range(DB if down else 1):
                        b = WSEG[name][0] + (DB * m + q if down else m) + 2
                        if b < NBLK and not (name in INNER and m in (1, 2)):
                            w_hi(b)
                    acc_done(act, g)
                    act.activation(halves(y[:, m, :]), accp[g % 4], ACT.Copy, scale=G("gain", 8 * gain + m)).then_inc(S("y_ready"), 1)
                    square(norm, m, accp[g % 4])
                    act.wait_ge(S("sq_ready"), 8 * NORM[norm] + m + 1)
                    act.sem_inc(drained[g % 4], 1)
                    if m == 0 and name in INNER:
                        w_next(name, 1)
                        w_next(name, 2)
                        root(INNER[name])
                    if m == 2 and name in INNER:
                        l = int(name[-1])
                        act.wait_ge(S("memn_ready"), 8 * (l + 1))
                        if l == 0:
                            act.wait_ge(S("out_kv"), 16 * 6)
                        act.activation(memhi, memn, ACT.Copy).then_inc(S("mem_hi"), 1)
                root(norm)

            def evict(g, out, src):
                acc_done(act, g)
                act.activation(out, src, ACT.Copy).then_inc(drained[g % 4], 1)

            act.wait_ge(S("xs_loaded"), 16)
            for c in range(8):
                act.wait_ge(S(f"x_loaded{c // 2}"), 16)
                square("mix0", c, x[:, c, :])
            root("mix0")
            for kind, k in FIRST:
                g = ACC[kind, k]
                pa, pb = 2 * (g % 4), 2 * (g % 4) + 1
                if kind == "in":
                    evict(g, halves(big[:, k, :]), accp[g % 4])
                    if k == 3:
                        for q in range(4):
                            acc_emptied(act, ACC["in", q])
                        act.dma_start(o["pool"], big[:, U:U + 4, TP - 15:T]).then_inc(S("out_pool"), 16)
                    if KCM <= k <= VWI:
                        acc_emptied(act, g)
                        act.dma_start(o["kv"][k - KCM], big[:, k, :]).then_inc(S("out_kv"), 16)
                elif kind == "mean":
                    evict(g, meant, ps[:, pa:pa + 2, 0:NSUB])
                elif kind == "cmp":
                    acc_done(act, g)
                    act.activation(kstore[:, k, :], ps[:, pa, 0:NSUB], ACT.Copy)
                    act.activation(vstore[:, k, :], ps[:, pb, 0:NSUB], ACT.Copy).then_inc(drained[g % 4], 1)
                else:
                    acc_done(act, g)
                    if k == 0:
                        act.wait_ge(S("pool_d"), 4)
                    act.activation(halves(mix[:, k, :]), accp[g % 4], ACT.Copy,
                                   scale=G("poolscale", k)).then_inc(drained[g % 4], 1)

            act.wait_ge(S("zeroed"), 1)
            act.wait_ge(S("prep_small"), 1)
            act.activation(kcp, ps[:, 0, 0:32], ACT.Copy).then_inc(S("prep_ready"), 1)
            act.wait_ge(S("prep_small"), 2)
            act.activation(vcp4, ps[:, 5, :].rearrange("p (q n) -> p q n", q=4), ACT.Copy).then_inc(S("prep_ready"), 1)
            for v in range(2):
                act.wait_ge(S("prep_v"), v + 1)
                act.activation(vnat[:, v, :, :].rearrange("p k n -> p (k n)"), ps[:, 1 + v, :],
                               ACT.Copy).then_inc(S("prep_ready"), 1)
            act.wait_ge(S("prep_new"), 1)
            act.activation(vnew[0:TS, :], ps[0:TS, 3, 0:256], ACT.Copy).then_inc(S("prep_ready"), 1)
            act.activation(gtok[0:TS, :], ps[0:TS, 3, 256:280], ACT.Sigmoid).then_inc(S("gates_ready"), 1)
            act.activation(gpr, ps[:, 4, :].rearrange("p (k n) -> p k n", k=4)[:, :, 0:24],
                           ACT.Sigmoid).then_inc(S("gates_ready"), 1)
            act.wait_ge(S("pc_sub"), 1)
            act.activation(pcm, pcm, ACT.Exp, scale=SC).then_inc(S("pc_exp"), 1)
            for k in range(2):
                act.wait_ge(S("pc_tr"), k + 1)
                act.activation(pct[:, k, :], ps[:, k, :], ACT.Copy).then_inc(S("pc_trc"), 1)

            def p_exp(u):
                n = (u % 4 + 1) * P
                for br in range(2):
                    act.wait_ge(S("pa_max"), 2 * u + br + 1)
                    if u >= 2:
                        act.wait_ge(S("pa_tr"), 2 * (u - 2) + br + 1)
                    act.activation(pp[:, u % 2, br, 0:n], ps[:, 2 * (u % 2) + br, 0:n], ACT.Exp,
                                   bias=pst[:, u % 2, br, 1:2], scale=SC,
                                   accum_out=pst[:, u % 2, br, 2:3]).then_inc(S("pa_exp"), 1)

            def p_evac(u):
                n = (u % 4 + 1) * P
                for br in range(2):
                    act.wait_ge(S("pa_tr"), 2 * u + br + 1)
                    if u >= 2:
                        act.wait_ge(S("pa_pv"), u - 1)
                    act.activation(ppt[:, u % 2, br, 0:n], ps[:, 4 + br, 0:n], ACT.Copy).then_inc(S("pa_trc"), 1)

            def p_out(c):
                act.wait_ge(S("pa_pv"), 8 * c + 8)
                act.activation(mix[:, 4 + c, 0:TP], ps[:, 6 + c % 2, :], ACT.Copy).then_inc(S("pa_out"), 1)

            for u in range(34):
                if 1 <= u <= 32:
                    p_evac(u - 1)
                if u < 32:
                    p_exp(u)
                if u >= 2 and (u - 2) % 8 == 7:
                    p_out((u - 2) // 8)

            def soft(sbuf, k):
                act.wait_ge(S("sm_max"), k + 1)
                act.activation(sbuf, sbuf, ACT.Exp, bias=sst[:, k, 1:2], scale=SC,
                               accum_out=sst[:, k, 2:3]).then_inc(S("sm_exp"), 1)

            for hb in range(2):
                soft(pce[:, 1:256], 3 * hb)
                act.wait_ge(S("sc_tr"), hb + 1)
                act.activation(pst2, ps[:, 6, 0:256], ACT.Copy).then_inc(S("sc_trc"), 1)
                act.wait_ge(S("sw_sc"), hb + 1)
                act.activation(swin[:, 0:512], ps[:, 2, :], ACT.Copy).then_inc(S("sw_cp"), 1)
                soft(swin, 3 * hb + 1)
                act.wait_ge(S("sw_tr"), hb + 1)
                act.activation(pwt, ps[:, 0, :], ACT.Copy).then_inc(S("sw_trc"), 1)
                act.activation(pwn[0:TS, :], ps[0:TS, 1, 0:P], ACT.Copy).then_inc(S("sw_trc"), 1)
                for k in range(32):
                    n = 32 * hb + k
                    act.wait_ge(S("kt_tr"), n + 1)
                    if n >= 2:
                        act.wait_ge(S("kt_sc"), n - 1)
                    act.activation(ktb[:, n % 2, :], ps[:, n % 2, :], ACT.Copy).then_inc(S("kt_trc"), 1)
                soft(sslc, 3 * hb + 2)
                for k in range(8):
                    act.wait_ge(S("sp_tr"), 8 * hb + k + 1)
                    act.activation(spt[:, k * 512:(k + 1) * 512], ps[:, k % 2, :], ACT.Copy).then_inc(S("sp_trc"), 1)
                act.wait_ge(S("spn_tr"), hb + 1)
                act.activation(spn[0:TS, :], ps[0:TS, 5, 0:P], ACT.Copy).then_inc(S("spn_trc"), 1)
                act.wait_ge(S("so_rows"), hb + 1)
                act.activation(orow, ps[:, 7, 256 + P * hb:384 + P * hb], ACT.Copy).then_inc(S("so_copied"), 1)
            for m in range(2):
                w_hi(WSEG["w_out0"][0] + m)
            act.wait_ge(S("so_done"), 2)
            for g in range(2):
                rows = slice(64 * g, 64 * g + 64)
                for c in range(4):
                    act.activation(
                        sample(mix[rows, 4 + c, TP:T]),
                        ps[rows, 7, 0:256].rearrange("p (b g c t) -> p b g c t", g=2, c=4, t=4)[:, :, g, c, :],
                        ACT.Copy).then_inc(S("so_out"), 1)
            act.wait_ge(S("so_out"), 8)
            mix_hi()

            def cross(l):

                def x_exp(qt):
                    n = 4 * l + qt
                    act.wait_ge(S("xp_max"), n + 1)
                    if n:
                        act.wait_ge(S("xp_tr"), 2 * n)
                    for hd in range(4):
                        act.activation(xpp[:, hd, :], ps[:, 2 + hd // 2, (hd % 2) * 256:(hd % 2) * 256 + 256],
                                       ACT.Exp, bias=xpm[:, 4 + hd:5 + hd], scale=SX,
                                       accum_out=xpm[:, 8 + hd:9 + hd]).then_inc(S("xp_exp"), 1)

                def x_evac(qt):
                    n = 4 * l + qt
                    if n:
                        act.wait_ge(S("xp_pv"), n)
                    for k in range(2):
                        act.wait_ge(S("xp_tr"), 2 * n + k + 1)
                        act.activation(xpt[:, k, :], ps[:, 4 + k, :], ACT.Copy).then_inc(S("xp_trc"), 1)

                def x_out(qt):
                    act.wait_ge(S("xp_pv"), 4 * l + qt + 1)
                    act.activation(mix[:, :, qt * P:qt * P + P],
                                   ps[:, 6:8, :].rearrange("p a (c t) -> p (a c) t", c=4), ACT.Copy).then_inc(S("xo_in"), 1)

                def s_copy(hb):
                    act.wait_ge(S("mv_used"), 8 * l + 4 * (hb + 1))
                    act.activation(xvr[:, hb, 0:512], ps[:, 2 * hb, :], ACT.Copy).then_inc(S("xv_copied_a"), 1)

                def s_out(hb):
                    act.wait_ge(S("xv_tr"), 2 * l + hb + 1)
                    for hd in (0, 1):
                        for q in range(2):
                            dst, src = s_places(hb, hd, q)
                            act.activation(dst, src, ACT.Copy).then_inc(S("xv_out_a"), 1)

                x_exp(0)
                act.wait_ge(S("xs_max"), l + 1)
                act.activation(xsp, ps[:, 1, 0:256], ACT.Exp, bias=xsm[:, 1:2], scale=SX,
                               accum_out=xsm[:, 2:3]).then_inc(S("xs_exp"), 1)
                x_evac(0)
                x_exp(1)
                x_out(0)
                act.wait_ge(S("xs_tr"), l + 1)
                act.activation(xst, ps[:, 0, 256:512], ACT.Copy).then_inc(S("xs_trc"), 1)
                x_evac(1)
                x_exp(2)
                x_out(1)
                s_copy(0)
                x_evac(2)
                x_exp(3)
                x_out(2)
                s_out(0)
                s_copy(1)
                x_evac(3)
                x_out(3)
                s_out(1)

            def layer_end(l):
                if l:
                    mix_hi("lmix_ready")
                act.wait_ge(S("mem_loaded"), 16 * (l + 1))
                for c in range(8):
                    square(f"mem{l}", c, memn[:, c, :])
                evict_y(f"w_out{l}", f"pmix{l}", 6 * l + 1)
                if l:
                    act.wait_ge(S("out_mem"), 32)
                ahead(f"xat{l}")
                for m in range(8):
                    w_next(f"mk{l}", m)
                    g = ACC[f"mk{l}"] + m
                    evict(g, kstore[:, m, :], ps[:, 2 * (g % 4), 0:NMEM])
                for m in range(4, 8):
                    acc_emptied(act, ACC[f"mk{l}"] + m)
                act.dma_start(o["memk"][l], kstore[:, :, :]).then_inc(S("out_mem"), 16)
                for m in range(8):
                    w_next(f"mv{l}", m)
                    g = ACC[f"mv{l}"] + m
                    evict(g, vst2[:, :, m * P:m * P + P], ps[:, 2 * (g % 4):2 * (g % 4) + 2, 0:P])
                    square(f"xat{l}", m, x[:, m, :])
                for m in range(4, 8):
                    acc_emptied(act, ACC[f"mv{l}"] + m)
                act.dma_start(o["memv"][l], vstore[:, :, :]).then_inc(S("out_mem"), 16)
                for m in range(AFTER):
                    w_next(f"xq{l}", m)
                root(f"xat{l}")
                for m in range(AFTER, 8):
                    w_next(f"xq{l}", m)
                cross(l)
                act.wait_ge(S("xv_out_a"), 8 * (l + 1))
                act.wait_ge(S("xv_out_v"), 8 * (l + 1))
                mix_hi()
                evict_y(f"xo{l}", f"pxat{l}", 6 * l + 3)
                ahead(f"ffn_{l}")
                name = f"ffn{l}"
                for m in range(8):
                    square(f"ffn_{l}", m, x[:, m, :])
                    if m == 5:
                        w_next(name, 0)

                def hid_parts(gs, m, hid, hh, k, i=0):
                    for j in range(2):
                        if m + 2 * j >= AFTER:
                            w_next(name, m + 2 * j, i)
                        acc_emptied(act, gs[2 * j], i)
                        act.activation(hid[j], hid[j], ACT.Silu).then_inc(S("silu_ready"), 1)
                        if m + 2 * j + 1 >= AFTER:
                            w_next(name, m + 2 * j + 1, i)
                        act.wait_ge(S("hidden"), 2 * i + (k + j + 1))
                        act.activation(hh[j], hid[j], ACT.Copy).then_inc(S("hid_hi"), 1)

                for m in range(1, AFTER):
                    w_next(name, m)
                root(f"ffn_{l}")
                hid_parts([acc_of(name, j) for j in range(4)], 0, [big[:, j, :] for j in range(2)],
                          [hidhi[:, j, :] for j in range(2)], FC * l)
                with act.Fori(0, FC // 2 - 1) as i:
                    hid_parts([acc_of(name, 4 + j) for j in range(4)], 4, [big[:, 2 * i + (2 + j), :] for j in range(2)],
                              [hidhi[:, 2 * i + (2 + j), :] for j in range(2)], FC * l + 2, i)
                evict_y(f"down{l}", f"pffn{l}", 6 * l + 5)

            layer_end(0)

            ahead("mix1")
            for m in range(8):
                square("mix1", m, x[:, m, :])
                if m == 5:
                    w_next("w_in1a", 0)
            for m in range(1, AFTER):
                w_next("w_in1a", m)
            root("mix1")
            for m in range(AFTER, 6):
                w_next("w_in1a", m)
            for m in range(4, 8):
                acc_emptied(act, acc_of("w_in1a", m))
            act.dma_start(o["conv_p"], cext[:, :, TP:TP + 3]).then_inc(S("out_conv"), 16)
            for c in range(8):
                act.dma_start(o["conv_s"][:, c, :, :], sample(cext[:, c, 3 + TP:CEX])[:, :, 4:7]).then_inc(S("out_conv"), 16)
            for m in range(8):
                for k in range(2):
                    g = ACC["lru"] + 2 * m + k
                    acc_done(act, g)
                    if m == 5 and k == 1:
                        act.wait_ge(S("out_conv"), 16 * 9)
                        act.wait_ge(S("xf_ready"), 8)
                    act.activation(halves(big[:, 8 * k + m, :]), accp[g % 4], ACT.Sigmoid,
                                   bias=G("ba" if k == 0 else "bx", m)).then_inc(drained[g % 4], 1)
                if m == 4 or m == 6:
                    w_hi(WSEG["w_in1b"][0] + m // 2 - 2)
            act.wait_ge(S("sp_ready"), 1)
            for m in range(12, 16):
                acc_emptied(act, ACC["lru"] + m)
            for half in range(2):
                for m in range(4 * half, 4 * half + 4):
                    if half:
                        act.wait_ge(S("gated_scaled"), m - 3)
                    act.activation(big[:, 16 + m % 4, :], big[:, m, :], ACT.Tanh, scale=lsp[:, m:m + 1]).then_inc(S("th_ready"), 1)
                    act.wait_ge(S("th_ready"), m + 1)
                    act.activation(big[:, m, :], big[:, m, :], ACT.Exp, scale=lsn[:, m:m + 1]).then_inc(S("a_ready"), 1)
                    act.wait_ge(S("a_ready"), m + 1)
                    act.wait_ge(S("gated"), m + 1)
                    act.activation(mix[:, m, :], big[:, m, :], ACT.Square).then_inc(S("a2_ready"), 1)
                w_next("w_in1b", 2 * half)
                for m in range(4 * half, 4 * half + 4):
                    act.wait_ge(S("m2_ready"), m + 1)
                    act.activation(big[:, 16 + m % 4, :], big[:, 16 + m % 4, :], ACT.Sqrt).then_inc(S("mult_ready"), 1)
                w_next("w_in1b", 2 * half + 1)
            for m in range(8):
                if m >= 4:
                    w_next("w_in1b", m)
                acc_emptied(act, ACC["w_in1b"] + m)
                act.activation(yb[:, m, :], yb[:, m, :], ACT.Gelu_apprx_tanh).then_inc(S("gelu_ready"), 1)
            act.wait_ge(S("lru_done"), 2)
            act.dma_start(o["lru_h"], lh[:, :, :]).then_inc(S("out_lru"), 16)
            layer_end(1)
            act.wait_ge(S("x_ready"), 48)
            act.dma_start(o["yp"], x[:, :, 0:TP]).then_inc(S("out_y"), 16)
            act.dma_start(o["ys"], x[:, :, TP:T]).then_inc(S("out_y"), 16)

        @block.vector
        def _(dve):
            steps = [0]

            def link(ins):
                steps[0] += 1
                ins.then_inc(S("dve_step"), 1)
                dve.wait_ge(S("dve_step"), steps[0])

            dve.wait_ge(S("const_loaded"), 32)
            dve.wait_ge(S("pages_loaded"), 16)
            dve.tensor_scalar(idx[:, :], idx[:, :], 8.0, C("subrow"), ALU.mult, ALU.add).then_inc(S("idx_ready"), 1)
            lam = par[:, PARAM["lam"]:PARAM["lam"] + 8]
            link(dve.tensor_scalar(spb[:, 32:40], lam, -1.0, None, ALU.mult))
            dve.tensor_tensor(spb[:, 24:32], lam, spb[:, 32:40], ALU.max).then_inc(S("sp_abs"), 1)
            dve.wait_ge(S("sp_exp"), 1)
            e, z, s1, s2, acc = spb[:, 16:24], spb[:, 32:40], spb[:, 40:48], spb[:, 48:56], spb[:, 56:64]
            link(dve.tensor_scalar(s1, e, 2.0, None, ALU.add))
            link(dve.reciprocal(s1, s1))
            link(dve.tensor_tensor(s1, s1, e, ALU.mult))
            link(dve.tensor_tensor(s2, s1, s1, ALU.mult))
            link(dve.tensor_scalar(acc, s2, 1.0 / 17, None, ALU.mult))
            for k in (15, 13, 11, 9, 7, 5, 3):
                link(dve.scalar_tensor_tensor(out=acc, in0=acc, scalar=1.0 / k, in1=s2, op0=ALU.add, op1=ALU.mult))
            link(dve.scalar_tensor_tensor(out=acc, in0=acc, scalar=1.0, in1=s1, op0=ALU.add, op1=ALU.mult))
            link(dve.tensor_scalar(z, z, 0.0, None, ALU.max))
            link(dve.scalar_tensor_tensor(out=acc, in0=acc, scalar=2.0, in1=z, op0=ALU.mult, op1=ALU.add))
            dve.tensor_scalar(lsp, acc, 8.0, None, ALU.mult)
            dve.tensor_scalar(lsn, acc, -8.0, None, ALU.mult).then_inc(S("sp_ready"), 1)

            def inverse(name):
                wd = NMEM if name.startswith("mem") else T
                dve.wait_ge(S("rms_ready"), NORM[name] + 1)
                dve.reciprocal(rinv[:, 0:wd], rms[:, 0:wd]).then_inc(S("rinv_ready"), 1)
                dve.wait_ge(S("rinv_ready"), NORM[name] + 1)

            def norm_apply(name, gain):
                inverse(name)
                for c in range(8):
                    dve.scalar_tensor_tensor(out=h[:, c, :], in0=x[:, c, :], scalar=G("gain", 8 * gain + c),
                                             in1=rinv[:, :], op0=ALU.mult, op1=ALU.mult).then_inc(S("h_ready"), 1)

            def residual(name, r):
                inverse(name)
                dve.wait_ge(S("y_ready"), 8 * (r + 1))
                for c in range(10):
                    if c < 8:
                        dve.tensor_tensor(y[:, c, :], y[:, c, :], rinv[:, :], ALU.mult).then_inc(S("y_scaled"), 1)
                    if c >= 2 and r < 5:
                        x_lo(r, c - 2)

            def w_lo(b, i=0):
                dve.wait_ge(S("w_hi"), 4 * i + (NSPLIT[b] + 1))
                src, lo, hi = block_at(b, tiles_of(b))
                dve.tensor_tensor(lo, src, F(hi), ALU.subtract).then_inc(S("w_lo"), 1)

            def w_next(name, m, i=0):
                w_lo(WSEG[name][0] + m + 2, i)

            def x_lo(r, c):
                dve.wait_ge(S("xg_ready"), 8 * r + c + 1)
                dve.scalar_tensor_tensor(out=yr[:, c, :], in0=x[:, c, :], scalar=G("gain", 16 * (r + 1) + c), in1=F(hr[:, c, :]),
                                         op0=ALU.mult, op1=ALU.subtract).then_inc(S("x_lo"), 1)

            def mix_lo(r):
                for c in range(8):
                    dve.wait_ge(S("mix_hi"), 8 * r + c + 1)
                    dve.tensor_tensor(mixr[:, c, :], mix[:, c, :], F(hr[:, c, :]), ALU.subtract).then_inc(S("mix_lo"), 1)

            norm_apply("mix0", 0)
            dve.wait_ge(S("ext_zero"), 1)
            dve.wait_ge(S("pool_past"), 16)
            wsteps = 0
            for b in range(NB):
                for kv in range(2):
                    for hh in range(2):
                        n = 4 * b + 2 * kv + hh
                        src = tile_in(dve, "cmp", b, "kv"[kv], hh)
                        if b >= 2:
                            acc_done(dve, ACC["mean", b - 2])
                        dve.tensor_reduce(subs[:, n % 8, :], src.rearrange("p (r c) -> p c r", r=SUB), AXX,
                                          ALU.add).then_inc(S("sub_ready"), 1)
                if b < 4:
                    acc_emptied(dve, ACC["in", b])
                    dve.tensor_copy(ext[:, b, 16:16 + TP], big[:, b, 0:TP])
                    dve.tensor_copy(sample(ext[:, b, 16 + TP:EXT])[:, :, 15:19],
                                    sample(big[:, b, TP:T])).then_inc(S("ext_ready"), 1)
                if 1 <= b <= 4:
                    g = b - 1
                    wsteps += g + 2
                    dve.wait_ge(S("win_step"), wsteps)
                    dve.scalar_tensor_tensor(out=mix[:, 4 + g, 0:TP], in0=bufs[g % 2][:, 16:16 + TP],
                                             scalar=1.0 / POOLW[g], in1=big[:, g, 0:TP], op0=ALU.mult, op1=ALU.subtract)
                    dve.scalar_tensor_tensor(out=sample(mix[:, 4 + g, TP:T]),
                                             in0=sample(bufs[g % 2][:, 16 + TP:EXT])[:, :, 15:19],
                                             scalar=1.0 / POOLW[g], in1=sample(big[:, g, TP:T]),
                                             op0=ALU.mult, op1=ALU.subtract).then_inc(S("pool_d"), 1)

            for k in (VCM, VWI, GT):
                acc_emptied(dve, ACC["in", k])
            for g in range(2):
                rows = slice(64 * g, 64 * g + 64)
                if not g:
                    dve.wait_ge(S("qbd_zero"), 1)
                for c in range(4):
                    last = dve.tensor_copy(qbd[rows, :].rearrange("p (b g c t) -> p b g c t", g=2, c=4, t=4)[:, :, g, c, :],
                                           sample(big[rows, Q + c, TP:T]))
            last.then_inc(S("qbd_ready"), 1)
            acc_done(dve, ACC["cmp", 7])
            dve.memset(mv4, 0.0)
            dve.memset(vnew, 0.0)
            dve.memset(mp, 0.0)
            for k in range(2):
                last = dve.tensor_reduce(s32[:, k, :], big[:, KCM + k, 0:TP].rearrange("p (s r) -> p s r", r=SUB),
                                         AXX, ALU.add)
            link(last)
            link(dve.tensor_tensor(mp[:, 0:31], s32[:, 0, 0:31], s32[:, 0, 1:32], ALU.add))
            dve.tensor_scalar(mp[:, 0:31], mp[:, 0:31], 1.0 / 32, None, ALU.mult)
            link(dve.tensor_tensor(s32[:, 1, 0:31], s32[:, 1, 0:31], s32[:, 1, 1:32], ALU.add))
            for q in range(4):
                last = dve.tensor_scalar(mv4[:, q, 32 * q:32 * q + 31], s32[:, 1, 0:31], 1.0 / 32, None, ALU.mult)
            last.then_inc(S("means_ready"), 1)
            dve.wait_ge(S("out_pool"), 16)
            dve.memset(pwn, 0.0)
            dve.memset(spn, 0.0)
            dve.memset(pce, 0.0).then_inc(S("zeroed"), 1)
            for hb in range(2):
                dve.wait_ge(S("grow_mm"), 1)
                link(dve.tensor_tensor(grw, ps[:, 0, 64 + 32 * hb:88 + 32 * hb], C("headmask"), ALU.mult))
                link(dve.tensor_reduce(grow[:, hb, :], grw.rearrange("p (h r) -> p r h", r=3), AXX, ALU.add))
            dve.wait_ge(S("pc_sc"), 1)
            for k in range(2):
                last = dve.tensor_tensor(pcm[:, 512 * k:512 * k + 512].rearrange("p (h n) -> p h n", h=4),
                                         ps[:, 6 + k, :].rearrange("p (h n) -> p h n", h=4),
                                         C("cmpbias").unsqueeze(1).to_broadcast([P, 4, P]), ALU.add)
            link(last)
            pc3 = pcm.rearrange("p (u n) -> p u n", n=32)

            def over(col):
                return col.unsqueeze(2).to_broadcast([P, 32, 32])

            link(dve.tensor_reduce(pcs[:, 0, :], pc3, AXX, ALU.max))
            dve.tensor_tensor(pc3, pc3, over(pcs[:, 0, :]), ALU.subtract).then_inc(S("pc_sub"), 1)
            dve.wait_ge(S("pc_exp"), 1)
            link(dve.tensor_reduce(pcs[:, 1, :], pc3, AXX, ALU.add))
            link(dve.reciprocal(pcs[:, 2, :], pcs[:, 1, :]))
            dve.wait_ge(S("gates_ready"), 2)
            r4 = pcs[:, 2, :].rearrange("p (h q) -> p h q", q=4)
            gv = gpr.rearrange("p q (g c r) -> p g c r q", g=2, c=4)
            for c in range(4):
                for g in range(2):
                    last = dve.tensor_tensor(r4[:, 4 * g + c, :], r4[:, 4 * g + c, :], gv[:, g, c, 0, :], ALU.mult)
            link(last)
            link(dve.tensor_scalar(r4[:, :, 0], r4[:, :, 0], C("anyblock"), None, ALU.mult))
            dve.tensor_tensor(pc3, pc3, over(pcs[:, 2, :]), ALU.mult).then_inc(S("pc_norm"), 1)

            def p_max(u):
                qt = u % 4
                n = (qt + 1) * P
                for br in range(2):
                    dve.wait_ge(S("pa_sc"), 2 * u + br + 1)
                    bank = 2 * (u % 2) + br
                    diag = ps[:, bank, qt * P:n]
                    link(dve.tensor_tensor(diag, diag, C("causal"), ALU.add))
                    link(dve.tensor_reduce(pst[:, u % 2, br, 0:1], ps[:, bank, 0:n], AXX, ALU.max))
                    dve.tensor_scalar(pst[:, u % 2, br, 1:2], pst[:, u % 2, br, 0:1], -SC, None,
                                      ALU.mult).then_inc(S("pa_max"), 1)

            def p_norm(u):
                c, g, qt = u // 8, u // 4 % 2, u % 4
                n = (qt + 1) * P
                for br in range(2):
                    dve.wait_ge(S("pa_exp"), 2 * u + br + 1)
                    link(dve.reciprocal(pst[:, u % 2, br, 3:4], pst[:, u % 2, br, 2:3]))
                    gate = gpr[:, qt, 3 * (4 * g + c) + 1 + br:3 * (4 * g + c) + 2 + br]
                    dve.tensor_scalar(pp[:, u % 2, br, 0:n], pp[:, u % 2, br, 0:n], pst[:, u % 2, br, 3:4], gate,
                                      ALU.mult, ALU.mult).then_inc(S("pa_norm"), 1)

            for u in range(33):
                if u:
                    p_norm(u - 1)
                if u < 32:
                    p_max(u)

            def s_max(sbuf, k):
                link(dve.tensor_reduce(sst[:, k, 0:1], sbuf, AXX, ALU.max))
                dve.tensor_scalar(sst[:, k, 1:2], sst[:, k, 0:1], -SC, None, ALU.mult).then_inc(S("sm_max"), 1)
                dve.wait_ge(S("sm_exp"), k + 1)
                link(dve.reciprocal(sst[:, k, 3:4], sst[:, k, 2:3]))

            dve.wait_ge(S("pa_pv"), 32)
            for hb in range(2):
                dve.wait_ge(S("sc_sc"), hb + 1)
                if hb:
                    dve.wait_ge(S("sc_tr"), 1)
                link(dve.tensor_copy(pce[:, 1:256], ps[:, 4, 0:255]))
                s_max(pce[:, 1:256], 3 * hb)
                dve.tensor_scalar(pce[:, 1:256], pce[:, 1:256], sst[:, 3 * hb, 3:4], None,
                                  ALU.mult).then_inc(S("sc_norm"), 1)
                dve.wait_ge(S("sc_imp"), hb + 1)
                imp = sel[:, 0:65]
                link(dve.tensor_copy(imp, ps[:, 5, 0:257:4]))
                for k in range(1, 5):
                    link(dve.tensor_tensor(imp, imp, ps[:, 5, k:k + 257:4], ALU.add))
                dve.memset(sel[:, 0:1], FORCE)
                link(dve.memset(sel[:, 63:65], FORCE))
                for _ in range(2):
                    link(dve.max(m8, imp))
                    link(dve.match_replace(imp, m8, imp, -2.0))
                dve.tensor_scalar(maskb[:, 0:65], imp, -1.0, NEG, ALU.is_gt, ALU.mult)
                dve.tensor_scalar(pce[:, 1:256], pce[:, 1:256], grow[:, hb, 0:1], None,
                                  ALU.mult).then_inc(S("sc_gate"), 1)
                dve.wait_ge(S("sw_cp"), hb + 1)
                dve.tensor_tensor(swin[:, 0:4], swin[:, 0:4], C("oldbias"), ALU.add)
                if hb:
                    dve.wait_ge(S("sw_tr"), 1)
                link(dve.tensor_tensor(swin[:, 512:544], ps[:, 3, 0:TS], C(f"newbias{hb}"), ALU.add))
                s_max(swin, 3 * hb + 1)
                dve.tensor_scalar(swin, swin, sst[:, 3 * hb + 1, 3:4], grow[:, hb, 2:3], ALU.mult,
                                  ALU.mult).then_inc(S("sw_norm"), 1)
                if hb:
                    dve.wait_ge(S("sp_tr"), 8)
                    dve.wait_ge(S("spn_tr"), 1)
                for k in range(32):
                    n = 32 * hb + k
                    j, hh, q = k // 8, k // 4 % 2, k % 4
                    rows = slice(32 * j, 32 * j + 32)
                    at = (16 * hh + 4 * q) * P
                    dve.wait_ge(S("kt_sc"), n + 1)
                    dve.tensor_tensor(
                        sslc[rows, at:at + 512].rearrange("p (r b s) -> p r b s", r=4, s=4),
                        ps[rows, 2 + n % 2, :].rearrange("p (r b s) -> p r b s", r=4, s=4),
                        maskb[rows, 32 * hh:32 * hh + 32].unsqueeze(1).unsqueeze(3).to_broadcast([32, 4, 32, 4]),
                        ALU.add).then_inc(S("sl_ev"), 1)
                dve.wait_ge(S("sl_new"), hb + 1)
                dve.wait_ge(S("sl_ev"), 32 * (hb + 1))
                link(dve.tensor_tensor(sslc[:, PAST:PAST + TS], ps[:, 4, 0:TS], C(f"newbias{hb}"), ALU.add))
                s_max(sslc, 3 * hb + 2)
                dve.tensor_scalar(sslc, sslc, sst[:, 3 * hb + 2, 3:4], grow[:, hb, 1:2], ALU.mult,
                                  ALU.mult).then_inc(S("sl_norm"), 1)

            def layer_end(l):
                name = f"w_out{l}"
                if l == 0:
                    w_lo(WSEG[name][0])
                    w_lo(WSEG[name][0] + 1)
                    mix_lo(0)
                for m in range(AFTER):
                    w_next(name, m)
                inverse(f"mem{l}")
                for c in range(8):
                    dve.scalar_tensor_tensor(out=memn[:, c, :], in0=memn[:, c, :], scalar=G("memgain", 8 * l + c),
                                             in1=rinv[:, 0:NMEM], op0=ALU.mult, op1=ALU.mult).then_inc(S("memn_ready"), 1)
                dve.wait_ge(S("mem_hi"), l + 1)
                dve.tensor_tensor(memlo, memn, F(memhi), ALU.subtract).then_inc(S("mem_lo"), 1)
                for m in range(3, 8):
                    w_next(name, m)
                dve.wait_ge(S("memn_ready"), 8 * (l + 1))
                residual(f"pmix{l}", 3 * l)
                for m in range(8):
                    w_next(f"mk{l}", m)
                for m in range(8):
                    w_next(f"mv{l}", m)
                if l == 0:
                    dve.wait_ge(S("out_kv"), 16 * 6)
                for m in range(AFTER):
                    w_next(f"xq{l}", m)
                inverse(f"xat{l}")
                for m in range(8):
                    g = acc_of(f"xq{l}", m)
                    acc_done(dve, g)
                    dve.tensor_tensor(halves(big[:, m, :]), accp[g % 4], halves(rinv[:, :]), ALU.mult).then_inc(drained[g % 4], 1)
                    if m >= AFTER:
                        w_next(f"xq{l}", m)
                dve.wait_ge(S("xq_zero"), l + 1)
                for c in range(8):
                    acc_emptied(dve, acc_of(f"xq{l}", c))
                    for q in range(2):
                        last = dve.tensor_copy(xqd[:, q::2, c, 16 * q + 4 * (c // 2):16 * q + 4 * (c // 2) + 4],
                                               sample(big[:, c, TP:T])[:, q::2, :])
                last.then_inc(S("xq_apart"), 1)

                def x_soft(qt):
                    n = 4 * l + qt
                    dve.wait_ge(S("xp_sc"), n + 1)
                    link(dve.tensor_reduce(xpm[:, 0:4], ps[:, 2:4, :].rearrange("p a (h n) -> p (a h) n", h=2), AXX, ALU.max))
                    dve.tensor_scalar(xpm[:, 4:8], xpm[:, 0:4], -SX, None, ALU.mult).then_inc(S("xp_max"), 1)
                    dve.wait_ge(S("xp_exp"), 4 * (n + 1))
                    link(dve.reciprocal(xpm[:, 12:16], xpm[:, 8:12]))
                    dve.tensor_tensor(xpp, xpp, xpm[:, 12:16].unsqueeze(2).to_broadcast([P, 4, 256]),
                                      ALU.mult).then_inc(S("xp_norm"), 1)

                def s_copy(hb):
                    dve.wait_ge(S("mv_used"), 8 * l + 4 * (hb + 1))
                    dve.tensor_copy(xvr[:, hb, 512:1024], ps[:, 2 * hb + 1, :]).then_inc(S("xv_copied_v"), 1)

                def s_out(hb):
                    dve.wait_ge(S("xv_tr"), 2 * l + hb + 1)
                    for hd in (2, 3):
                        for q in range(2):
                            dst, src = s_places(hb, hd, q)
                            dve.tensor_copy(dst, src).then_inc(S("xv_out_v"), 1)

                x_soft(0)
                dve.wait_ge(S("mk_used"), 8 * (l + 1))
                link(dve.tensor_reduce(xsm[:, 0:1], ps[:, 1, 0:256], AXX, ALU.max))
                dve.tensor_scalar(xsm[:, 1:2], xsm[:, 0:1], -SX, None, ALU.mult).then_inc(S("xs_max"), 1)
                dve.wait_ge(S("xs_exp"), l + 1)
                link(dve.reciprocal(xsm[:, 3:4], xsm[:, 2:3]))
                dve.tensor_scalar(xsp, xsp, xsm[:, 3:4], None, ALU.mult).then_inc(S("xs_norm"), 1)
                x_soft(1)
                x_soft(2)
                s_copy(0)
                x_soft(3)
                s_out(0)
                s_copy(1)
                s_out(1)
                mix_lo(2 * l + 1)
                for m in range(8):
                    w_next(f"xo{l}", m)
                residual(f"pxat{l}", 3 * l + 1)
                dve.wait_ge(S("out_mem"), 32 * (l + 1))
                name = f"ffn{l}"
                for m in range(AFTER):
                    w_next(name, m)
                inverse(f"ffn_{l}")

                def hidden(gs, m, hid, lo, hh, n0, i=0):
                    for j in range(2):
                        g = gs[2 * j]
                        acc_done(dve, g, i)
                        dve.tensor_tensor(halves(hid[j]), accp[g % 4], halves(rinv[:, :]), ALU.mult).then_inc(drained[g % 4], 1)
                        if m + 2 * j >= AFTER:
                            w_next(name, m + 2 * j, i)
                        g = gs[2 * j + 1]
                        acc_done(dve, g, i)
                        dve.tensor_tensor(halves(uprow[:, j, :]), accp[g % 4], halves(rinv[:, :]), ALU.mult).then_inc(drained[g % 4], 1)
                        acc_emptied(dve, g, i)
                        dve.wait_ge(S("silu_ready"), 2 * i + (n0 + j + 1))
                        dve.tensor_tensor(hid[j], hid[j], uprow[:, j, :], ALU.mult).then_inc(S("hidden"), 1)
                        if m + 2 * j + 1 >= AFTER:
                            w_next(name, m + 2 * j + 1, i)
                        dve.wait_ge(S("hid_hi"), 2 * i + (n0 + j + 1))
                        dve.tensor_tensor(lo[j], hid[j], F(hh[j]), ALU.subtract).then_inc(S("hid_lo"), 1)

                hidden([acc_of(name, j) for j in range(4)], 0, [big[:, j, :] for j in range(2)], [big_r[:, j, :] for j in range(2)],
                       [hidhi[:, j, :] for j in range(2)], FC * l)
                with dve.Fori(0, FC // 2 - 1) as i:
                    hidden([acc_of(name, 4 + j) for j in range(4)], 4, [big[:, 2 * i + (2 + j), :] for j in range(2)],
                           [big_r[:, 2 * i + (2 + j), :] for j in range(2)],
                           [hidhi[:, 2 * i + (2 + j), :] for j in range(2)], FC * l + 2, i)
                for m in range(8 * DB):
                    b = WSEG[f"down{l}"][0] + m + 2
                    if b < NBLK:
                        w_lo(b)
                residual(f"pffn{l}", 3 * l + 2)

            layer_end(0)

            acc_done(dve, ACC["down0"] + 7)
            dve.memset(cext[:, :, 0:3], 0.0).then_inc(S("conv_zero"), 1)
            for m in range(AFTER):
                w_next("w_in1a", m)
            inverse("mix1")
            dve.wait_ge(S("conv_past"), 16)
            n = CEX - 3
            for m in range(8):
                g = acc_of("w_in1a", m)
                pa = 2 * (g % 4)
                acc_done(dve, g)
                dve.tensor_tensor(cext[:, m, 3:3 + H], ps[:, pa, 0:H], rinv[:, 0:H], ALU.mult)
                dve.tensor_tensor(cext[:, m, 3 + H:3 + TP], ps[:, pa + 1, 0:TP - H], rinv[:, H:TP], ALU.mult)
                dve.tensor_tensor(sample(cext[:, m, 3 + TP:CEX])[:, :, 3:7], sample(ps[:, pa + 1, TP - H:H]),
                                  sample(rinv[:, TP:T]), ALU.mult).then_inc(drained[g % 4], 1)
                acc_emptied(dve, g)
                if AFTER <= m < 6:
                    w_next("w_in1a", m)
                link(dve.tensor_scalar(cv[m % 2][:, 0:n], cext[:, m, 0:n], G("convw", m), G("convb", m), ALU.mult, ALU.add))
                for k in (1, 2):
                    link(dve.scalar_tensor_tensor(out=cv[m % 2][:, 0:n], in0=cext[:, m, k:k + n], scalar=G("convw", 8 * k + m),
                                                  in1=cv[m % 2][:, 0:n], op0=ALU.mult, op1=ALU.add))
                dve.scalar_tensor_tensor(out=mix[:, m, 0:TP], in0=cext[:, m, 3:3 + TP], scalar=G("convw", 24 + m),
                                         in1=cv[m % 2][:, 0:TP], op0=ALU.mult, op1=ALU.add)
                dve.scalar_tensor_tensor(out=sample(mix[:, m, TP:T]), in0=sample(cext[:, m, 3 + TP:CEX])[:, :, 3:7],
                                         scalar=G("convw", 24 + m), in1=sample(cv[m % 2][:, 3 + TP:CEX])[:, :, 0:4],
                                         op0=ALU.mult, op1=ALU.add).then_inc(S("xf_ready"), 1)

            def branch(m):
                g = ACC["w_in1b"] + m
                acc_done(dve, g)
                dve.tensor_tensor(halves(yb[:, m, :]), accp[g % 4], halves(rinv[:, :]), ALU.mult).then_inc(drained[g % 4], 1)

            def col(ap, m0, t):
                return ap[:, m0:m0 + 4, TP:T].rearrange("p c (b t) -> p c b t", t=NT)[:, :, :, t]

            dve.wait_ge(S("xf_ready"), 8)
            for m in range(2):
                w_lo(WSEG["w_in1b"][0] + m)
            for half in range(2):
                m0 = 4 * half
                for m in range(m0, m0 + 4):
                    dve.wait_ge(S("a2_ready"), m + 1)
                    dve.scalar_tensor_tensor(out=big[:, 16 + m % 4, :], in0=mix[:, m, :], scalar=1.0, in1=big[:, 16 + m % 4, :],
                                             op0=ALU.add, op1=ALU.mult).then_inc(S("m2_ready"), 1)
                w_next("w_in1b", 2 * half)
                branch(2 * half)
                for m in range(m0, m0 + 4):
                    dve.wait_ge(S("mult_ready"), m + 1)
                    link(dve.memset(big[:, 16 + m % 4, 0:1], 1.0))
                    dve.tensor_tensor(big[:, 8 + m, :], big[:, 8 + m, :], big[:, 16 + m % 4, :],
                                      ALU.mult).then_inc(S("gated_scaled"), 1)
                    dve.wait_ge(S("gated_scaled"), m + 1)
                    link(dve.tensor_tensor_scan(mix[:, m, 0:TP], big[:, m, 0:TP], big[:, 8 + m, 0:TP], 0.0, ALU.mult, ALU.add))
                w_next("w_in1b", 2 * half + 1)
                branch(2 * half + 1)
                if not half:
                    dve.wait_ge(S("h0_loaded"), 16)
                for t in range(NT):
                    prev = lh0[:, m0:m0 + 4, :] if t == 0 else col(mix, m0, t - 1)
                    link(dve.tensor_tensor(tmp8[:, 0:4, :], col(big, m0, t), prev, ALU.mult))
                    link(dve.tensor_tensor(col(mix, m0, t), tmp8[:, 0:4, :], col(big, 8 + m0, t), ALU.add))
                dve.tensor_copy(lh[:, m0:m0 + 4, 0:1], mix[:, m0:m0 + 4, TP - 1:TP])
                dve.tensor_copy(lh[:, m0:m0 + 4, 1:9], col(mix, m0, NT - 1)).then_inc(S("lru_done"), 1)
            for m in range(4, 8):
                w_next("w_in1b", m)
                branch(m)
            for m in range(8):
                dve.wait_ge(S("gelu_ready"), m + 1)
                dve.tensor_tensor(mix[:, m, :], mix[:, m, :], yb[:, m, :], ALU.mult).then_inc(S("lmix_ready"), 1)
            mix_lo(2)
            layer_end(1)

        @block.tensor
        def _(pe):
            pe.wait_ge(S("const_loaded"), 32)

            def mm(out, lhsT, rhs, start, stop, **kw):
                return pe.matmul(out, lhsT, rhs, start=start, stop=stop, **kw)

            def stats(name):
                g = ACC["s_" + name]
                acc_free(pe, g)
                wd = NMEM if name.startswith("mem") else H
                pe.wait_ge(S("sq_summed"), 6 * (NORM[name] + 1))
                banks = range(1 if name.startswith("mem") else 2)
                for a_ in banks:
                    mm(ps[:, 2 * (g % 4) + a_, 0:wd], C("ones"), ssum[:, a_ * wd:a_ * wd + wd], True, False)
                pe.wait_ge(S("sq_ready"), 8 * (NORM[name] + 1))
                for a_ in banks:
                    last = mm(ps[:, 2 * (g % 4) + a_, 0:wd], C("ones"), sq[:, 1, a_ * wd:a_ * wd + wd], False, True)
                last.then_inc(ready[g % 4], 1)

            def plain(g, b, src, tiles, wt, kn, arrives=None):
                weights_in(pe, b)
                for k in range(kn):
                    if arrives:
                        pe.wait_ge(S(arrives), k + 1)
                    for a_ in range(2):
                        last = mm(accp[g % 4][:, a_, :], wring[:, b % NSLOT, (wt + k) * P:(wt + k) * P + P],
                                  src[:, k, a_ * H:a_ * H + H], k == 0, k == kn - 1, skip_group_check=True)
                return last

            def chunk(g, b, hi, lo, n_i=0, tiles=KB, k0=0, kn=KB, arrives=None):
                pe.wait_ge(S("w_lo"), n_i + (NSPLIT[b] + 1))
                _, wl, wh = block_at(b, tiles)
                last = None
                for k in range(tiles):
                    if arrives:
                        pe.wait_ge(S(arrives[0]), arrives[1] + k0 + k + 1)
                    at = slice(k * P, k * P + P)
                    first, end = k0 + k == 0, k0 + k == kn - 1
                    for wt, src, p_ in ((wh, hi, 0), (wh, lo, 1), (wl, hi, 2)):
                        for a_ in range(2):
                            last = mm(accp[g % 4][:, a_, :], wt[:, at], src[:, k0 + k, a_ * H:a_ * H + H],
                                      first and p_ == 0, end and p_ == 2, skip_group_check=True)
                return last

            def linear(name, hi, lo, arrives=None):
                b0, k, _ = WSEG[name]
                for m in range(4 if k > 8 else 8):
                    g = acc_of(name, m)
                    acc_free(pe, g)
                    chunk(g, b0 + m, hi, lo, arrives=None if m else arrives).then_inc(ready[g % 4], 1)
                    if m == AFTER - 1 and name in INNER:
                        stats(INNER[name])
                if k > 8:
                    with pe.Fori(0, k // 4 - 1) as i:
                        for j in range(4):
                            g = acc_of(name, 4 + j)
                            acc_free(pe, g, i)
                            chunk(g, b0 + 4 + j, hi, lo, 4 * i).then_inc(ready[g % 4], 1)

            stats("mix0")
            for kind, k in FIRST:
                g = ACC[kind, k]
                pa, pb = 2 * (g % 4), 2 * (g % 4) + 1
                acc_free(pe, g)
                if kind == "in":
                    last = plain(g, WSEG["w_in"][0] + k, h, 8, 0, KC, None if k else "h_ready")
                elif kind == "mean":
                    for kv in range(2):
                        for hh in range(2):
                            n = 4 * k + 2 * kv + hh
                            pe.wait_ge(S("sub_ready"), n + 1)
                            last = mm(ps[:, pa + kv, 0:NSUB], subs[:, n % 8, :], C("pair")[:, hh * NSUB:hh * NSUB + NSUB],
                                      hh == 0, hh == 1)
                elif kind == "cmp":
                    if k == 0:
                        pe.wait_ge(S("small_loaded"), 32)
                    acc_emptied(pe, ACC["mean", k])
                    mm(ps[:, pa, 0:NSUB], wcmp_sb[:, 0, :], meant[:, 0, :], True, True)
                    for kt in range(2):
                        last = mm(ps[:, pb, kt * P:kt * P + P], meant[:, 1, kt * P:kt * P + P], wcmp_sb[:, 1, :], True, True)
                else:
                    pe.wait_ge(S("pool_d"), k + 1)
                    for a_ in range(2):
                        last = mm(accp[g % 4][:, a_, :], poolw_sb[:, k, :], mix[:, 4 + k, a_ * H:a_ * H + H], True, True)
                last.then_inc(ready[g % 4], 1)

            for kind, k in FIRST[-4:]:
                acc_emptied(pe, ACC[kind, k])
            pe.wait_ge(S("means_ready"), 1)
            mm(ps[:, 0, 0:32], wcmp_sb[:, 0, :], mp, True, True).then_inc(S("prep_small"), 1)
            for q in range(4):
                last = mm(ps[:, 5, q * P:q * P + P], mv4[:, q, :], wcmp_sb[:, 1, :], True, True)
            last.then_inc(S("prep_small"), 1)
            for v, chunk_ in enumerate((VSL, VWI)):
                for k in range(4):
                    last = pe.transpose(ps[:, 1 + v, k * P:k * P + P], big[:, chunk_, k * P:k * P + P], ident)
                last.then_inc(S("prep_v"), 1)
            for k in range(4):
                pe.transpose(ps[:, 4, k * P:k * P + P], big[:, GT, k * P:k * P + P], ident)
            for v, chunk_ in enumerate((VSL, VWI, GT)):
                last = pe.transpose(ps[0:TS, 3, v * P:v * P + P], big[:, chunk_, TP:T], ident)
            last.then_inc(S("prep_new"), 1)
            pe.wait_ge(S("prep_ready"), 1)
            for u in range(32):
                c, g, qt = u // 8, u // 4 % 2, u % 4
                rows = slice(64 * g, 64 * g + 64)
                at = (4 * c + qt) * 32
                last = mm(ps[:, 6 + g, at:at + 32], big[rows, Q + c, qt * P:qt * P + P],
                          kcp[rows, :], True, True)
            last.then_inc(S("pc_sc"), 1)
            pe.wait_ge(S("gates_ready"), 1)
            for hb in range(2):
                last = mm(ps[:, 0, 64 + 32 * hb:88 + 32 * hb], C(f"rep{hb}")[0:TS, :], gtok[0:TS, :], True, True)
            last.then_inc(S("grow_mm"), 1)
            pe.wait_ge(S("prep_ready"), 5)
            pe.wait_ge(S("pc_norm"), 1)
            for hd in range(8):
                last = pe.transpose(ps[:, hd // 4, (hd % 4) * P:(hd % 4) * P + P], pcm[:, hd * P:hd * P + P], ident)
                if hd % 4 == 3:
                    last.then_inc(S("pc_tr"), 1)

            pe.wait_ge(S("pc_trc"), 2)
            pe.wait_ge(S("gates_ready"), 2)

            def p_scores(u):
                c, g, qt = u // 8, u // 4 % 2, u % 4
                n = (qt + 1) * P
                rows = slice(64 * g, 64 * g + 64)
                if u >= 2:
                    pe.wait_ge(S("pa_exp"), 2 * (u - 1))
                for br, kc in enumerate((KSL, KWI)):
                    mm(ps[:, 2 * (u % 2) + br, 0:n], big[rows, Q + c, qt * P:qt * P + P], big[rows, kc, 0:n],
                       True, True).then_inc(S("pa_sc"), 1)

            def p_turn(u):
                for br in range(2):
                    pe.wait_ge(S("pa_norm"), 2 * u + br + 1)
                    if u:
                        pe.wait_ge(S("pa_trc"), 2 * (u - 1) + br + 1)
                    for k in range(u % 4 + 1):
                        last = pe.transpose(ps[:, 4 + br, k * P:k * P + P], pp[:, u % 2, br, k * P:k * P + P], ident)
                    last.then_inc(S("pa_tr"), 1)

            def p_values(u):
                c, g, qt = u // 8, u // 4 % 2, u % 4
                hd = 4 * g + c
                if u % 8 == 0 and c >= 2:
                    pe.wait_ge(S("pa_out"), c - 1)
                pe.wait_ge(S("pa_trc"), 2 * u + 2)
                out = ps[64 * g:64 * g + 64, 6 + c % 2, qt * P:qt * P + P]
                cols = slice(64 * g, 64 * g + 64)
                mm(out, vcp4[:, qt, cols], pct[:, hd // 4, (hd % 4) * P:(hd % 4) * P + P], True, False)
                for br in range(2):
                    for k in range(qt + 1):
                        last = mm(out, vnat[:, br, k, cols], ppt[:, u % 2, br, k * P:k * P + P], False,
                                  br == 1 and k == qt)
                last.then_inc(S("pa_pv"), 1)

            for u in range(34):
                if u < 32:
                    p_scores(u)
                if 1 <= u <= 32:
                    p_turn(u - 1)
                if u >= 2:
                    p_values(u - 2)

            pe.wait_ge(S("pa_out"), 4)
            pe.wait_ge(S("qbd_ready"), 1)
            opened = [False] * NB

            def to_rows(b, probs, values, stop=False):
                at = 256 + P * (b // 4)
                ins = mm(ps[32 * (b % 4):32 * (b % 4) + 32, 7, at:at + P], probs, values, not opened[b], stop,
                         skip_group_check=True)
                opened[b] = True
                return ins

            for hb in range(2):
                if hb:
                    pe.wait_ge(S("sw_cp"), 1)
                for j in range(4):
                    b = 4 * hb + j
                    last = mm(ps[32 * j:32 * j + 32, 4, 0:NSUB], qbd[:, 32 * b:32 * b + 32], kstore[:, b, :], True, True)
                last.then_inc(S("sc_sc"), 1)
                pe.wait_ge(S("sc_norm"), hb + 1)
                if hb:
                    pe.wait_ge(S("spn_trc"), 1)
                mm(ps[:, 5, 0:264], C("heads"), pce, True, True).then_inc(S("sc_imp"), 1)
                wk = tile_in(pe, "win", hb, "k", 0)
                for j in range(4):
                    b = 4 * hb + j
                    mm(ps[32 * j:32 * j + 32, 2, :], qbd[:, 32 * b:32 * b + 32], wk[:, j * 512:j * 512 + 512], True, True)
                rows4 = qbd[:, 128 * hb:128 * hb + 128]
                mm(ps[:, 3, 0:TS], rows4, big[:, KWI, TP:T], True, True).then_inc(S("sw_sc"), 1)
                pe.wait_ge(S("sc_gate"), hb + 1)
                if hb:
                    pe.wait_ge(S("sw_trc"), 2)
                for kt in range(2):
                    last = pe.transpose(ps[:, 6, kt * P:kt * P + P], pce[:, 1 + kt * P:1 + kt * P + P], ident)
                last.then_inc(S("sc_tr"), 1)
                pe.wait_ge(S("sc_trc"), hb + 1)
                if hb:
                    pe.wait_ge(S("so_copied"), 1)
                for j in range(4):
                    b = 4 * hb + j
                    for kt in range(2):
                        to_rows(b, pst2[:, kt * P + 32 * j:kt * P + 32 * j + 32], vstore[:, b, kt * P:kt * P + P])
                pe.wait_ge(S("sw_norm"), hb + 1)
                for kt in range(4):
                    pe.transpose(ps[:, 0, kt * P:kt * P + P], swin[:, kt * P:kt * P + P], ident)
                pe.transpose(ps[0:TS, 1, 0:P], swin[:, 512:544], ident).then_inc(S("sw_tr"), 1)
                wv = tile_in(pe, "win", hb, "v", 0)
                pe.wait_ge(S("sw_trc"), 2 * (hb + 1))
                for j in range(4):
                    b = 4 * hb + j
                    to_rows(b, pwn[:, 32 * j:32 * j + 32], vnew[:, P:2 * P])
                    for kt in range(4):
                        last = to_rows(b, pwt[:, kt * P + 32 * j:kt * P + 32 * j + 32],
                                       wv[:, j * 512 + kt * P:j * 512 + kt * P + P])
                last.then_inc(S("sw_pv"), 1)
                if hb:
                    pe.wait_ge(S("sp_trc"), 8)
                for k in range(33):
                    n = 32 * hb + k
                    if k < 32:
                        if k % 4 == 0:
                            kt_ = tile_in(pe, "slc", 4 * hb + k // 8, "k", k // 4 % 2)
                        if n >= 2:
                            pe.wait_ge(S("kt_trc"), n - 1)
                        for r in range(4):
                            at = (4 * (k % 4) + r) * P
                            last = pe.transpose(ps[:, n % 2, r * P:r * P + P], kt_[:, at:at + P], ident)
                        last.then_inc(S("kt_tr"), 1)
                    if k:
                        n -= 1
                        j = (k - 1) // 8
                        pe.wait_ge(S("kt_trc"), n + 1)
                        if n >= 2:
                            pe.wait_ge(S("sl_ev"), n - 1)
                        b = 4 * hb + j
                        mm(ps[32 * j:32 * j + 32, 2 + n % 2, :], qbd[:, 32 * b:32 * b + 32], ktb[:, n % 2, :],
                           True, True).then_inc(S("kt_sc"), 1)
                mm(ps[:, 4, 0:TS], rows4, big[:, KSL, TP:T], True, True).then_inc(S("sl_new"), 1)
                pe.wait_ge(S("sl_norm"), hb + 1)
                for k in range(8):
                    if k >= 2:
                        pe.wait_ge(S("sp_trc"), 8 * hb + k - 1)
                    for r in range(4):
                        at = (4 * k + r) * P
                        last = pe.transpose(ps[:, k % 2, r * P:r * P + P], sslc[:, at:at + P], ident)
                    last.then_inc(S("sp_tr"), 1)
                pe.transpose(ps[0:TS, 5, 0:P], sslc[:, PAST:PAST + TS], ident).then_inc(S("spn_tr"), 1)
                pe.wait_ge(S("sp_trc"), 8 * (hb + 1))
                pe.wait_ge(S("spn_trc"), hb + 1)
                for j in range(4):
                    b = 4 * hb + j
                    for hh in range(2):
                        vt = tile_in(pe, "slc", b, "v", hh)
                        for r in range(16):
                            at = (16 * hh + r) * P + 32 * j
                            last = to_rows(b, spt[:, at:at + 32], vt[:, r * P:r * P + P])
                        last.then_inc(S("sv_used"), 1)
                    last = to_rows(b, spn[:, 32 * j:32 * j + 32], vnew[:, 0:P], True)
                last.then_inc(S("so_rows"), 1)
                pe.wait_ge(S("so_copied"), hb + 1)
                pe.transpose(ps[:, 7, P * hb:P * hb + P], orow, ident).then_inc(S("so_done"), 1)

            def cross(l):
                for m in range(8):
                    acc_emptied(pe, acc_of(f"xq{l}", m))

                def scores(qt):
                    n = 4 * l + qt
                    if n:
                        pe.wait_ge(S("xp_exp"), 4 * n)
                    for hd in range(4):
                        for dc in range(2):
                            c = 2 * hd + dc
                            last = mm(ps[:, 2 + hd // 2, (hd % 2) * 256:(hd % 2) * 256 + 256],
                                      big[:, c, qt * P:qt * P + P], kstore[:, c, :], dc == 0, dc == 1)
                    last.then_inc(S("xp_sc"), 1)

                def turn(qt):
                    n = 4 * l + qt
                    pe.wait_ge(S("xp_norm"), n + 1)
                    if n:
                        pe.wait_ge(S("xp_trc"), 2 * n)
                    for i in range(8):
                        last = pe.transpose(ps[:, 4 + i // 4, (i % 4) * P:(i % 4) * P + P],
                                            xpp[:, i // 2, (i % 2) * P:(i % 2) * P + P], ident)
                        if i % 4 == 3:
                            last.then_inc(S("xp_tr"), 1)

                def values(qt):
                    n = 4 * l + qt
                    pe.wait_ge(S("xp_trc"), 2 * n + 2)
                    if n:
                        pe.wait_ge(S("xo_in"), n)
                    for c in range(8):
                        for kt in range(2):
                            i = 2 * (c // 2) + kt
                            last = mm(ps[:, 6 + c // 4, (c % 4) * P:(c % 4) * P + P], vst2[:, kt, c * P:c * P + P],
                                      xpt[:, i // 4, (i % 4) * P:(i % 4) * P + P], kt == 0, kt == 1)
                    last.then_inc(S("xp_pv"), 1)

                def s_values(hb):
                    for j in range(4):
                        b = 4 * hb + j
                        mv = tile_in(pe, f"mem{l}", b, "v", 0)
                        for f in range(2):
                            for kt in range(2):
                                at = kt * P + 32 * (b // 2)
                                last = mm(ps[32 * j:32 * j + 32, 2 * hb + f, :], xst[:, at:at + 32],
                                          mv[:, kt * 1024 + 512 * f:kt * 1024 + 512 * f + 512], kt == 0, kt == 1)
                        last.then_inc(S("mv_used"), 1)

                def s_turn(hb):
                    pe.wait_ge(S("xv_copied_a"), 2 * l + hb + 1)
                    pe.wait_ge(S("xv_copied_v"), 2 * l + hb + 1)
                    for c in range(8):
                        last = pe.transpose(ps[:, 2 * hb + c // 4, (c % 4) * P:(c % 4) * P + P],
                                            xvr[:, hb, c * P:c * P + P], ident)
                    last.then_inc(S("xv_tr"), 1)

                scores(0)
                pe.wait_ge(S("xq_apart"), l + 1)
                for b in range(NB):
                    mk = tile_in(pe, f"mem{l}", b, "k", 0)
                    rows = slice(32 * (b // 2), 32 * (b // 2) + 32)
                    for c in range(8):
                        last = mm(ps[rows, 1, 0:256], xqd[:, b, c, :], mk[:, c * 256:c * 256 + 256],
                                  b % 2 == 0 and c == 0, b % 2 == 1 and c == 7)
                    last.then_inc(S("mk_used"), 1)
                scores(1)
                turn(0)
                values(0)
                pe.wait_ge(S("xs_norm"), l + 1)
                for kt in range(2):
                    last = pe.transpose(ps[:, 0, 256 + kt * P:256 + kt * P + P], xsp[:, kt * P:kt * P + P], ident)
                last.then_inc(S("xs_tr"), 1)
                scores(2)
                turn(1)
                values(1)
                pe.wait_ge(S("xs_trc"), l + 1)
                s_values(0)
                scores(3)
                turn(2)
                values(2)
                s_turn(0)
                pe.wait_ge(S("xp_exp"), 16 * (l + 1))
                s_values(1)
                turn(3)
                values(3)
                s_turn(1)
                pe.wait_ge(S("xo_in"), 4 * (l + 1))
                pe.wait_ge(S("xv_out_a"), 8 * (l + 1))
                pe.wait_ge(S("xv_out_v"), 8 * (l + 1))

            def layer_end(l):
                linear(f"w_out{l}", hr, mixr, ("mix_lo", 16 * l))
                stats(f"pmix{l}")
                pe.wait_ge(S("mem_lo"), l + 1)
                b0, g0 = WSEG[f"mk{l}"][0], ACC[f"mk{l}"]
                with pe.Fori(0, 2) as i:
                    for j in range(4):
                        acc_free(pe, g0 + j, i)
                        pe.wait_ge(S("w_lo"), 4 * i + (NSPLIT[b0 + j] + 1))
                        _, wl, wh = block_at(b0 + j, KB)
                        for k in range(8):
                            for wt, src, p_ in ((wh, memhi, 0), (wh, memlo, 1), (wl, memhi, 2)):
                                last = mm(ps[:, 2 * ((g0 + j) % 4), 0:NMEM], wt[:, k * P:k * P + P], src[:, k, :],
                                          k == 0 and p_ == 0, k == 7 and p_ == 2)
                        last.then_inc(ready[(g0 + j) % 4], 1)
                b0, g0 = WSEG[f"mv{l}"][0], ACC[f"mv{l}"]
                with pe.Fori(0, 2) as i:
                    for j in range(4):
                        acc_free(pe, g0 + j, i)
                        pe.wait_ge(S("w_lo"), 4 * i + (NSPLIT[b0 + j] + 1))
                        _, wl, wh = block_at(b0 + j, KB)
                        for k in range(8):
                            for kt in range(2):
                                for wt, src, p_ in ((wh, memhi, 0), (wl, memhi, 1), (wh, memlo, 2)):
                                    last = mm(ps[:, 2 * ((g0 + j) % 4) + kt, 0:P], src[:, k, kt * P:kt * P + P],
                                              wt[:, k * P:k * P + P], k == 0 and p_ == 0, k == 7 and p_ == 2,
                                              skip_group_check=True)
                        last.then_inc(ready[(g0 + j) % 4], 1)
                linear(f"xq{l}", hr, yr, ("x_lo", 8 * 3 * l))
                cross(l)
                linear(f"xo{l}", hr, mixr, ("mix_lo", 16 * l + 8))
                stats(f"pxat{l}")
                linear(f"ffn{l}", hr, yr, ("x_lo", 8 * (3 * l + 1)))
                b0, g0 = WSEG[f"down{l}"][0], ACC[f"down{l}"]
                for m in range(8):
                    acc_free(pe, g0 + m)
                    for q in range(DB):
                        b = b0 + DB * m + q
                        last = chunk(g0 + m, b, hidhi, big_r, 0, tiles_of(b), KB * q, FC, None if m else ("hid_lo", FC * l))
                        last.then_inc(*((ready[(g0 + m) % 4], 1) if q == DB - 1 else (S("part_used"), 1)))
                stats(f"pffn{l}")

            pe.wait_ge(S("so_out"), 8)
            layer_end(0)

            linear("w_in1a", hr, yr, ("x_lo", 16))
            for m in range(8):
                pe.wait_ge(S("xf_ready"), 2 * (m // 2) + 2)
                for k in range(2):
                    g = ACC["lru"] + 2 * m + k
                    b = WSEG["lru"][0] + m // 2
                    acc_free(pe, g)
                    plain(g, b, mix[:, m // 2 * 2:m // 2 * 2 + 2, :], 2, (2 * m + k) * 2 % 8, 2).then_inc(ready[g % 4], 1)
            linear("w_in1b", hr, yr)
            layer_end(1)


def _chunks(x):
    return np.ascontiguousarray(x.T.reshape(-1, P, x.shape[0]).transpose(1, 0, 2))


def _blocks(w, tiles):
    k, n = w.shape
    t = w.reshape(k // P, P, n // P, P).transpose(2, 0, 1, 3).reshape(-1, tiles, P, P)
    return np.ascontiguousarray(t.transpose(0, 2, 1, 3).reshape(-1, P, tiles * P))


def kernel(**inputs):
    import concourse.bacc as bacc
    from concourse.bass_utils import run_bass_kernel_spmd

    v = {k: np.asarray(t) for k, t in inputs.items()}
    arr = {}
    arr["xp"] = _chunks(v["x_prompt"][0])
    arr["xs"] = _chunks(v["x_sample"].reshape(TS, D))
    arr["mem"] = _chunks(v["mem_prompt"][0])
    past = v["state_pool"][0].transpose(2, 0, 1)
    past = np.pad(past, ((0, 0), (0, 0), (0, 4))).reshape(4, P, NB * 19)
    arr["poolold"] = np.ascontiguousarray(v["state_pool"][0, :, NT:]).reshape(P, -1)
    arr["poolpast"] = np.ascontiguousarray(past.transpose(1, 0, 2))
    for n, k in (("cmpk", "cache_cmp_k"), ("cmpv", "cache_cmp_v"), ("slck", "cache_slc_k"), ("slcv", "cache_slc_v")):
        arr[n] = np.ascontiguousarray(v[k]).reshape(-1, SUB * P)
    wk = v["cache_win_k"][0].reshape(NB, 512, P)
    wv = v["cache_win_v"][0].reshape(NB, 512, P)
    arr["winold_k"] = np.ascontiguousarray(wk[:, 4:]).reshape(P, -1)
    arr["winold_v"] = np.ascontiguousarray(wv[:, 4:]).reshape(P, -1)
    arr["wink"] = np.ascontiguousarray(wk.transpose(2, 0, 1).reshape(P, 2, 4 * 512).transpose(1, 0, 2))
    arr["winv"] = np.ascontiguousarray(
        wv.reshape(2, 4, 4, P, P).transpose(0, 3, 1, 2, 4).reshape(2, P, 4 * 512))
    arr["memk"] = np.ascontiguousarray(
        v["cache_mem_k"].reshape(2, NB, NMEM, 8, P).transpose(0, 1, 4, 3, 2).reshape(2, NB, P, 2048))
    arr["memv"] = np.ascontiguousarray(
        v["cache_mem_v"].reshape(2, NB, 2, P, D).transpose(0, 1, 3, 2, 4).reshape(2, NB, P, 2048))
    pt = v["page_table"].reshape(NB, 2, 16).astype(np.int32)
    arr["pages"] = np.ascontiguousarray(np.repeat(pt, 8, axis=2).transpose(2, 0, 1).reshape(P, 16))
    arr["const"] = CONSTANTS
    cols = [v["norm_gain"].reshape(96, P), v["mem_norm_gain"].reshape(16, P), v["pool_scale"].reshape(4, P),
            v["conv_w"].reshape(32, P), v["conv_b"].reshape(8, P), v["lru_ba"].reshape(8, P),
            v["lru_bx"].reshape(8, P), v["lru_lambda"].reshape(8, P)]
    arr["param"] = np.ascontiguousarray(np.concatenate(cols, axis=0).T)
    arr["poolw"] = np.ascontiguousarray(v["pool_w"][0].transpose(1, 0, 2))
    bd = np.zeros((P, 2, P), np.float32)
    for g in range(2):
        bd[64 * g:64 * g + 64, 0, 64 * g:64 * g + 64] = v["w_cmp_k"][0, g]
        bd[64 * g:64 * g + 64, 1, 64 * g:64 * g + 64] = v["w_cmp_v"][0, g]
    arr["wcmp"] = bd
    arr["lruh"] = np.ascontiguousarray(v["state_lru_h"][0].reshape(NB, 8, P).transpose(2, 1, 0))
    lc = np.pad(v["state_lru_conv"][0].transpose(2, 0, 1), ((0, 0), (0, 0), (0, 4)))
    arr["lruconv"] = np.ascontiguousarray(lc.reshape(8, P, NB * 7).transpose(1, 0, 2))
    wi = v["w_in_even"][0]
    q = wi[:, 512:1024].reshape(D, 2, 4, 64).transpose(0, 2, 1, 3).reshape(D, 512)
    wi = np.pad(np.concatenate([wi[:, :512], q, wi[:, 1024:]], axis=1), ((0, 0), (0, NIN * P - wi.shape[1])))
    wo = v["w_out_even"][0]
    wo = np.concatenate([wo[:512], wo[512:].reshape(2, 4, 64, D).transpose(1, 0, 2, 3).reshape(512, D)], axis=0)
    wts = {"w_in": _blocks(wi, 8), "w_out0": _blocks(wo, 8), "w_in1a": _blocks(v["w_in_odd"][0][:, :D], 8),
           "w_in1b": _blocks(v["w_in_odd"][0][:, D:], 8), "w_out1": _blocks(v["w_out_odd"][0], 8)}
    for l in range(2):
        for n, k in (("xq", "w_xq"), ("mk", "w_xk"), ("mv", "w_xv"), ("xo", "w_xo")):
            wts[f"{n}{l}"] = _blocks(v[k][l], 8)
        gu = np.stack([v["w_ffn_gate"][l].reshape(D, FC, P), v["w_ffn_up"][l].reshape(D, FC, P)], axis=2)
        wts[f"ffn{l}"] = _blocks(gu.reshape(D, 2 * DFF), 8)
        dn = np.pad(v["w_ffn_down"][l], ((0, DB * KB * P - DFF), (0, 0)))
        wts[f"down{l}"] = _blocks(dn, KB)
    ax = np.stack([v["lru_wa"][0], v["lru_wx"][0]], axis=0).reshape(2, 4, 2, P, 2, P)
    ax = ax.transpose(1, 4, 0, 2, 3, 5).reshape(4, 8, P, P)
    wts["lru"] = np.ascontiguousarray(ax.transpose(0, 2, 1, 3).reshape(4, P, 8 * P))
    outs = {
        "yp": [P, KC, TP], "ys": [P, KC, TS], "pool": [P, 4, 15 + TS], "poolold": [P, NB * 11 * 4], "kv": [6, P, T],
        "wink_s": [P, NB * 508], "winv_s": [P, NB * 508], "memk": [2, P, 8, NMEM], "memv": [2, P, 8, 256],
        "conv_p": [P, 8, 3], "conv_s": [P, 8, NB, 3], "lru_h": [P, 8, 9],
    }
    nc = bacc.Bacc("TRN2", target_bir_lowering=False, num_devices=1)
    feed = {f"in_{n}": t for n, t in arr.items()} | {f"w_{n}": t for n, t in wts.items()}
    a = {n: nc.dram_tensor(f"in_{n}", t.shape, mybir.dt.from_np(t.dtype), kind="ExternalInput").ap() for n, t in arr.items()}
    w = {n: nc.dram_tensor(f"w_{n}", t.shape, F32, kind="ExternalInput").ap() for n, t in wts.items()}
    o = {n: nc.dram_tensor(f"out_{n}", s, F32, kind="ExternalOutput").ap() for n, s in outs.items()}
    decoder_step(nc, a, w, o)
    r = run_bass_kernel_spmd(nc, [feed], core_ids=[0]).results[0]
    r = {n: np.asarray(r[f"out_{n}"]) for n in outs}

    def rows(t):
        return t.transpose(2, 1, 0).reshape(t.shape[2], -1)

    yp = rows(r["yp"]).reshape(1, TP, D)
    ys = rows(r["ys"]).reshape(NB, NT, D)
    pool = rows(r["pool"])
    pool_p = pool[:15].reshape(1, 1, 15, 512)
    pool_new = pool[15:].reshape(1, NB, NT, 512)
    past_rows = r["poolold"].reshape(1, NB, 11, 512)
    pool_s = np.concatenate([past_rows, pool_new], axis=2)
    kv = [rows(r["kv"][i][:, None, :]) for i in range(6)]
    kvp = [t[:TP].reshape(1, 1, TP, 2, 64) for t in kv]
    kvs = [t[TP:].reshape(NB, 1, NT, 2, 64) for t in kv]
    win = []
    for i, n in ((4, "wink_s"), (5, "winv_s")):
        win.append(kv[i][:TP].reshape(1, 1, TP, 2, 64))
        old = r[n].reshape(1, NB, 508, 2, 64)
        win.append(np.concatenate([old, kv[i][TP:].reshape(1, NB, NT, 2, 64)], axis=2))
    lh = r["lru_h"].transpose(2, 1, 0).reshape(9, D)
    conv_p = r["conv_p"].transpose(2, 1, 0).reshape(1, 1, 3, D)
    conv_s = r["conv_s"].transpose(2, 3, 1, 0).reshape(1, NB, 3, D)
    mk = r["memk"].transpose(0, 3, 2, 1).reshape(2, 1, NMEM, 4, 256)
    mv = r["memv"].reshape(2, P, 2, D).transpose(0, 2, 1, 3).reshape(2, 1, NMEM, 4, 256)
    return (yp, ys, pool_p, pool_s, kvp[0], kvs[0], kvp[1], kvs[1], kvp[2], kvs[2], kvp[3], kvs[3],
            win[0], win[1], win[2], win[3], lh[:1].reshape(1, 1, D), lh[1:].reshape(1, NB, D), conv_p, conv_s, mk, mv)
```

```python
from contextlib import ExitStack

import numpy as np

import concourse.bass as bass
from concourse import mybir

F32 = mybir.dt.float32
F32R = mybir.dt.float32r
I32 = mybir.dt.int32
U32 = mybir.dt.uint32
ALU = mybir.AluOpType
ACT = mybir.ActivationFunctionType
AXX = mybir.AxisListType.X

P = 128
D = 1024
KC = D // P
TP = 512
NB, NT = 8, 4
TS = NB * NT
T = TP + TS
H = T // 2
DFF = 2816
FC = DFF // P
KB = 8
DB = -(-FC // KB)
AFTER = 2
NMEM = 256
PAST = 4096
SUB = 16
NSUB = PAST // SUB
POOLW = (2, 4, 8, 16)
EPS = 1e-6
NEG = -1e30
FORCE = 1e30
SC = 64 ** -0.5
SX = 256 ** -0.5
NIN = 15
U, Q, KCM, VCM, KSL, VSL, KWI, VWI, GT = 0, 4, 8, 9, 10, 11, 12, 13, 14
NSLOT = 4
NC = 4
EXT = 16 + TP + NB * 19
CEX = 3 + TP + NB * 7

WSEG = {}


def _segments():
    at = 0
    for name, blocks, tiles in [
        ("w_in", NIN, 8), ("w_out0", 8, 8), ("mk0", 8, 8), ("mv0", 8, 8), ("xq0", 8, 8), ("xo0", 8, 8),
        ("ffn0", 2 * FC, 8), ("down0", 8 * DB, 8),
        ("w_in1a", 8, 8), ("lru", 4, 8), ("w_in1b", 8, 8), ("w_out1", 8, 8), ("mk1", 8, 8), ("mv1", 8, 8), ("xq1", 8, 8),
        ("xo1", 8, 8), ("ffn1", 2 * FC, 8), ("down1", 8 * DB, 8),
    ]:
        WSEG[name] = (at, blocks, tiles)
        at += blocks
    return at


NBLK = _segments()

ACC = {}
NORMS = ["mix0", "mem0", "pmix0", "xat0", "pxat0", "ffn_0", "pffn0",
         "mix1", "mem1", "pmix1", "xat1", "pxat1", "ffn_1", "pffn1"]
NORM = {n: i for i, n in enumerate(NORMS)}
INNER = {"w_out0": "mem0", "xq0": "xat0", "ffn0": "ffn_0", "w_in1a": "mix1",
         "w_out1": "mem1", "xq1": "xat1", "ffn1": "ffn_1"}
FIRST = []


def _accumulators():
    n = 1
    ACC["s_mix0"] = 0
    for m in range(NIN):
        FIRST.append(("in", m))
        if m % 2 == 1:
            FIRST.append(("mean", m // 2))
        elif m >= 2:
            FIRST.append(("cmp", m // 2 - 1))
    FIRST.append(("mean", 7))
    for c in range(4):
        FIRST.append(("pool", c))
    FIRST.append(("cmp", 7))
    for i, (kind, k) in enumerate(FIRST):
        ACC[kind, k] = n + i
    n += len(FIRST)

    def place(name, k):
        nonlocal n
        ACC[name] = n
        n += k
        if name in INNER:
            ACC["s_" + INNER[name]] = ACC[name] + AFTER
            n += 1

    for l in range(2):
        if l == 1:
            for name, k in (("w_in1a", 8), ("lru", 16), ("w_in1b", 8)):
                place(name, k)
        for name, k in [(f"w_out{l}", 8), (f"s_pmix{l}", 1), (f"mk{l}", 8), (f"mv{l}", 2), (f"xq{l}", 8), (f"xo{l}", 8),
                        (f"s_pxat{l}", 1), (f"ffn{l}", 2 * FC), (f"down{l}", 8), (f"s_pffn{l}", 1)]:
            place(name, k)
    return n


NACC = _accumulators()


def acc_of(name, i):
    return ACC[name] + i + (name in INNER and i >= AFTER)


PER = {"mv": 4, "down": DB}


def _consumer(b):
    for name, (b0, k, _) in WSEG.items():
        if b0 <= b < b0 + k:
            i = b - b0
            if name == "w_in":
                return ACC["in", i]
            if name == "lru":
                return ACC["lru"] + 4 * i + 3
            if name[:-1] in PER:
                return ACC[name] + i // PER[name[:-1]]
            return acc_of(name, i)
    raise ValueError(b)


PARTS = {b: n for n, b in enumerate(
    b for name, (b0, k, _) in WSEG.items() if name[:-1] in PER
    for b in range(b0, b0 + k) if (b - b0) % PER[name[:-1]] < PER[name[:-1]] - 1)}
SPLIT = [b for name, (b0, k, _) in WSEG.items() if name not in ("w_in", "lru") for b in range(b0, b0 + k)]
NSPLIT = {b: n for n, b in enumerate(SPLIT)}

TILES = [("cmp", b, kv, h) for b in range(NB) for kv in "kv" for h in range(2)]
for _hb in range(2):
    TILES += [("win", _hb, "k", 0)]
    TILES += [("slc", 4 * _hb + j, "k", h) for j in range(2) for h in range(2)]
    TILES += [("win", _hb, "v", 0)]
    TILES += [("slc", 4 * _hb + j, "k", h) for j in range(2, 4) for h in range(2)]
    TILES += [("slc", 4 * _hb + j, "v", h) for j in range(4) for h in range(2)]
TILES += [("mem0", b, kv, 0) for kv in "kv" for b in range(NB)]
TILES += [("mem1", b, kv, 0) for kv in "kv" for b in range(NB)]
TILE = {t: i for i, t in enumerate(TILES)}
XC = 2
PLACE = []
TURN = []
BEFORE = []


def _places():
    last = {}
    turns = {}
    n0 = TILE["win", 0, "k", 0]
    for n, (kind, *_) in enumerate(TILES):
        if kind == "cmp":
            s = n % NC
        else:
            s = (n - (TILE[kind, 0, "k", 0] if kind.startswith("mem") else n0)) % (NC + XC)
        PLACE.append(s)
        turns[s] = turns.get(s, 0) + 1
        TURN.append(turns[s])
        BEFORE.append(last.get(s))
        last[s] = n


_places()

CONST = {}


def _constants():
    parts = []
    at = 0

    def put(name, a):
        nonlocal at
        a = np.asarray(a, np.float32).reshape(P, -1)
        CONST[name] = (at, a.shape[1])
        parts.append(a)
        at += a.shape[1]

    p = np.arange(P)
    put("ident", np.eye(P))
    put("ones", np.ones((P, P)))
    put("causal", np.where(p[None, :] > p[:, None], NEG, 0.0))
    a = np.zeros((2, P, NSUB))
    for s in range(NSUB):
        for i in (s, s - 1):
            if 0 <= i < NSUB - 1:
                a[s // P, s % P, i] = 1.0 / 32.0
    put("pair", a.transpose(1, 0, 2))
    t = (np.arange(4)[None, :] * P + p[:, None])[:, :, None]
    i = np.arange(32)[None, None, :]
    put("cmpbias", np.where((i * 16 + 31 <= t) & (i < 31), 0.0, NEG))
    put("anyblock", (p >= 31).astype(np.float32))
    j, g, c, tt = p // 32, p // 16 % 2, p // 4 % 4, p % 4
    key = np.arange(TS)
    for hb in range(2):
        own = (key[None, :] // 4 == 4 * hb + j[:, None]) & (key[None, :] % 4 <= tt[:, None])
        put(f"newbias{hb}", np.where(own, 0.0, NEG))
        put(f"rep{hb}", np.pad((key[:, None] == (16 * hb + 4 * j + tt)[None, :]).astype(np.float32), ((0, 96), (0, 0))))
    put("oldbias", np.where(np.arange(4)[None, :] <= tt[:, None], NEG, 0.0))
    put("headmask", np.repeat(np.arange(8)[None, :] == (4 * g + c)[:, None], 3, axis=1))
    same = (j[:, None] == j[None, :]) & (g[:, None] == g[None, :]) & (tt[:, None] == tt[None, :])
    put("heads", same)
    fix = np.ones((4, 16))
    for k, w in enumerate(POOLW):
        fix[k, :w] = w / np.minimum(np.arange(w) + 1.0, w)
    put("poolfix", np.broadcast_to(fix.reshape(1, -1), (P, 64)))
    put("subrow", (p % 8))
    return np.concatenate(parts, axis=1)


CONSTANTS = _constants()

PARAM = {"gain": 0, "memgain": 96, "poolscale": 112, "convw": 116, "convb": 148, "ba": 156, "bx": 164, "lam": 172}
NPARAM = 180


def decoder_step(nc, a, w, o):
    with ExitStack() as ctx:
        def sb(name, shape, dt=F32):
            return ctx.enter_context(nc.sbuf_tensor(name, shape, dt))

        def sb_both(name, shape):
            at = -(-nc.sbuf_base // 32) * 32
            t = sb(name, shape)
            r = nc.alloc_sbuf_tensor_at(name + "_r", shape, F32R, offset=at)
            assert nc.sbuf_base == at + 4 * int(np.prod(shape[1:]))
            return t, r

        sems = {}

        def S(name):
            if name not in sems:
                sems[name] = ctx.enter_context(nc.semaphore(name))
            return sems[name]

        x = sb("x", [P, KC, T])
        work, work_r = sb_both("work", [P, 2 * KC, T])
        h = work[:, 0:KC, :]
        y = work[:, KC:2 * KC, :]
        mc, mc_r = sb_both("mc", [P, KC * T + NC * 2048])
        mix = mc[:, 0:KC * T].rearrange("p (c t) -> p c t", c=KC)
        big, big_r = sb_both("big", [P, FC, T])
        wring, wring_r = sb_both("wring", [P, NSLOT, KB * P])
        whi = sb("whi", [P, 2, KB * P], F32R)
        cring = mc[:, KC * T:KC * T + NC * 2048].rearrange("p (s n) -> p s n", s=NC)
        kstore = sb("kstore", [P, 8, 256])
        vstore = sb("vstore", [P, 8, 256])
        cst = sb("cst", [P, CONSTANTS.shape[1]])
        par = sb("par", [P, NPARAM])
        sq = sb("sq", [P, 2, T])
        ssum = sb("ssum", [P, T])
        rms = sb("rms", [P, T])
        rinv = sb("rinv", [P, T])
        idx = sb("idx", [P, 16], I32)
        small = sb("small", [P, 640])
        epsc = sb("epsc", [P, 1])
        spb = sb("spb", [P, 64])
        lh0 = sb("lh0", [P, 8, 8])
        lh = sb("lh", [P, 8, 9])
        ps = ctx.enter_context(nc.psum_tensor("ps", [P, 8, 512], F32))

        def C(name):
            at, n = CONST[name]
            return cst[:, at:at + n]

        def G(name, k):
            return par[:, PARAM[name] + k:PARAM[name] + k + 1]

        def halves(ap):
            return ap.rearrange("p (a n) -> p a n", a=2)

        swork = work[:, :, :].rearrange("p c t -> p (c t)")
        ybase = KC * T
        ext = swork[:, ybase:ybase + 4 * EXT].rearrange("p (g n) -> p g n", g=4)
        poolw_sb = swork[:, ybase + 4 * EXT:ybase + 4 * EXT + 512].rearrange("p (g n) -> p g n", g=4)
        wcmp_sb = swork[:, ybase + 4 * EXT + 512:ybase + 4 * EXT + 768].rearrange("p (g n) -> p g n", g=2)
        bufs = [mix[:, 0:2, :].rearrange("p c t -> p (c t)")[:, 0:EXT],
                mix[:, 2:4, :].rearrange("p c t -> p (c t)")[:, 0:EXT]]
        flat = big[:, 15:22, :].rearrange("p c t -> p (c t)")
        ktb = flat[:, 0:1024].rearrange("p (b n) -> p b n", b=2)
        meant = flat[:, 1024:1536].rearrange("p (k n) -> p k n", k=2)
        vcp4 = flat[:, 0:512].rearrange("p (q n) -> p q n", q=4)
        subs = flat[:, 1536:2560].rearrange("p (b n) -> p b n", b=8)
        mv4 = flat[:, 512:1024].rearrange("p (q n) -> p q n", q=4)
        vnew = flat[:, 1024:1280]
        grw = flat[:, 2304:2328]
        pcs = flat[:, 2352:2448].rearrange("p (k n) -> p k n", k=3)
        s32 = flat[:, 2448:2512].rearrange("p (k n) -> p k n", k=2)
        vnat = flat[:, 2560:3584].rearrange("p (v k n) -> p v k n", v=2, k=4)
        pp = swork[:, 0:2048].rearrange("p (u r n) -> p u r n", u=2, r=2)
        ppt = swork[:, 2048:4096].rearrange("p (u r n) -> p u r n", u=2, r=2)
        pcm = swork[:, 4096:5120]
        pct = swork[:, 5120:6144].rearrange("p (k n) -> p k n", k=2)
        sslc = swork[:, 0:PAST + TS]
        spt = swork[:, ybase:ybase + PAST]
        uflat = big[:, 0:4, :].rearrange("p c t -> p (c t)")
        pce = uflat[:, 0:264]
        swin = uflat[:, 264:808]
        pwt = uflat[:, 808:1320]
        pst2 = uflat[:, 1320:1576]
        orow = pst2[:, 0:P]
        pwn = uflat[:, 1576:1704]
        spn = uflat[:, 1704:1832]
        maskb = uflat[:, 1832:1904]
        sel = uflat[:, 1904:1976]
        m8 = uflat[:, 1976:1984]
        qbd = small[:, 0:256]
        convs = small[:, 0:192].rearrange("p (c b t) -> p c b t", c=8, b=NB)
        convp = small[:, 192:216].rearrange("p (c t) -> p c t", c=8)
        kcp = small[:, 256:288]
        gpr = small[:, 288:384].rearrange("p (q n) -> p q n", q=4)
        gtok = small[:, 384:408]
        mp = small[:, 408:440]
        grow = small[:, 440:446].rearrange("p (k n) -> p k n", k=2)
        sst = small[:, 448:472].rearrange("p (k n) -> p k n", k=6)
        pst = small[:, 472:488].rearrange("p (u r n) -> p u r n", u=2, r=2)
        xsm = small[:, 488:492]
        xpm = small[:, 492:508]
        smx = small[:, 576:585]
        sxs = small[:, 586:595]
        sfac = small[:, 596:597]
        tmp8 = small[:, 512:576].rearrange("p (c b) -> p c b", c=8)
        flatx = big[:, 8:22, :].rearrange("p c t -> p (c t)")
        xpp = flatx[:, 0:1024].rearrange("p (h n) -> p h n", h=4)
        xst = flatx[:, 1024:1280]
        xqd = flatx[:, 1280:3328].rearrange("p (b c n) -> p b c n", b=NB, c=8)
        xvr = flatx[:, 1280:3328].rearrange("p (b n) -> p b n", b=2)
        xpt = flatx[:, 3520:7616].rearrange("p (k n) -> p k n", k=8)
        xsp = rms[:, 0:256]
        memn = flatx[:, 5568:7616].rearrange("p (c n) -> p c n", c=8)
        vst2 = vstore[:, :, :].rearrange("p b n -> p (b n)").rearrange("p (k n) -> p k n", k=2)
        cext = big[:, 13:22, :].rearrange("p c t -> p (c t)")[:, 0:8 * CEX].rearrange("p (c n) -> p c n", c=8)
        flatx_r = big_r[:, 8:22, :].rearrange("p c t -> p (c t)")
        memhi = flatx_r[:, 0:2048].rearrange("p (c n) -> p c n", c=8)
        memlo = flatx_r[:, 5568:7616].rearrange("p (c n) -> p c n", c=8)
        hidhi = mc_r[:, 0:FC * T].rearrange("p (c t) -> p c t", c=FC)
        hr, yr = work_r[:, 0:KC, :], work_r[:, KC:2 * KC, :]
        mixr = mc_r[:, 0:KC * T].rearrange("p (c t) -> p c t", c=KC)
        yb = mc[:, KC * T:2 * KC * T].rearrange("p (c t) -> p c t", c=KC)
        cv = [mc[:, 2 * KC * T + q * CEX:2 * KC * T + (q + 1) * CEX] for q in range(2)]
        uprow = kstore[:, :, :].rearrange("p b n -> p (b n)")[:, 0:2 * T].rearrange("p (b t) -> p b t", b=2)
        th = [big[:, 16, :], big[:, 17, :], mc[:, 2 * KC * T:2 * KC * T + T], mc[:, 2 * KC * T + T:2 * KC * T + 2 * T]]
        lsp = spb[:, 0:8]
        lsn = spb[:, 8:16]
        ident = C("ident")

        accp = [ps[:, 2 * q:2 * q + 2, 0:H] for q in range(4)]
        ready = [S(f"acc_ready{q}") for q in range(4)]
        drained = [S(f"acc_drained{q}") for q in range(4)]
        wfull = [S(f"weights_full{s}") for s in range(NSLOT)]
        cfull = [S(f"cache_full{s}") for s in range(NC + XC)]
        cplace = [cring[:, s, :] for s in range(NC)] + [
            big[:, Q:Q + 4, :].rearrange("p c t -> p (c t)")[:, 0:2048], flat[:, 1280:3328]]

        def acc_free(e, g, i=0):
            if g >= 4:
                e.wait_ge(drained[g % 4], i + g // 4)

        def acc_done(e, g, i=0):
            e.wait_ge(ready[g % 4], i + (g // 4 + 1))

        def acc_emptied(e, g, i=0):
            e.wait_ge(drained[g % 4], i + (g // 4 + 1))

        def weights_in(e, b, i=0):
            e.wait_ge(wfull[b % NSLOT], 16 * i + 16 * (b // NSLOT + 1))

        def block_used(e, b, i=0):
            if b in PARTS:
                e.wait_ge(S("part_used"), PARTS[b] + 1)
            else:
                acc_done(e, _consumer(b), i)

        def F(ap):
            return ap.bitcast(F32)

        def block_at(b, tiles):
            return (wring[:, b % NSLOT, 0:tiles * P], wring_r[:, b % NSLOT, 0:tiles * P],
                    whi[:, NSPLIT[b] % 2, 0:tiles * P])

        def tiles_of(b):
            for l in range(2):
                b0, k, _ = WSEG[f"down{l}"]
                if b0 <= b < b0 + k and (b - b0) % DB == DB - 1:
                    return FC - KB * (DB - 1)
            return KB

        def tile_in(e, *t):
            n = TILE[t]
            e.wait_ge(cfull[PLACE[n]], 16 * TURN[n])
            return place_of(n)

        def s_places(hb, hd, q):
            src = ps[:, 6 * hb + hd // 2, (hd % 2) * 256:(hd % 2) * 256 + 256].rearrange("p (d j r) -> p d j r", d=2, j=2)
            dst = mix[:, 2 * hd:2 * hd + 2, TP + 16 * hb:TP + 16 * hb + 16].rearrange("p d (j r) -> p d j r", j=2)
            return dst[:, :, :, 4 * q:4 * q + 4], src[:, :, :, 48 * q + 4 * hd:48 * q + 4 * hd + 4]

        def place_of(n):
            s = PLACE[n]
            if s >= NC and TILES[n][0].startswith("mem"):
                return mc[:, (s - NC) * 2048:(s - NC) * 2048 + 2048]
            return cplace[s]

        def sample(ap):
            return ap.rearrange("p (b t) -> p b t", b=NB)

        block = ctx.enter_context(nc.Block())

        @block.sync
        def _(sp):
            for c in range(4):
                if c == 1:
                    sp.dma_start(x[:, :, TP:T], a["xs"]).then_inc(S("xs_loaded"), 16)
                sp.dma_start(x[:, 2 * c:2 * c + 2, 0:TP], a["xp"][:, 2 * c:2 * c + 2, :]).then_inc(S(f"x_loaded{c}"), 16)
            sp.dma_start(par[:, :], a["param"]).then_inc(S("const_loaded"), 16)
            sp.dma_start(cst[:, :], a["const"]).then_inc(S("const_loaded"), 16)
            sp.dma_start(poolw_sb, a["poolw"]).then_inc(S("small_loaded"), 16)
            sp.dma_start(wcmp_sb, a["wcmp"]).then_inc(S("small_loaded"), 16)
            sp.dma_start(lh0[:, :, :], a["lruh"]).then_inc(S("h0_loaded"), 16)

            def load(name):
                b0, k, tiles = WSEG[name]
                dst = [wring[:, s, :] for s in range(NSLOT)]
                looped = k == 2 * FC
                for i in range(8 if looped else k):
                    b = b0 + i
                    if b >= NSLOT:
                        block_used(sp, b - NSLOT)
                    n = tiles_of(b) * P
                    sp.dma_start(dst[b % NSLOT][:, 0:n], w[name][i][:, 0:n]).then_inc(wfull[b % NSLOT], 16)
                    if (name, i) in (("w_out0", 3), ("w_out1", 0)):
                        if name == "w_out0":
                            sp.wait_ge(S("so_done"), 2)
                        else:
                            sp.wait_ge(S("xf_ready"), 8)
                            sp.wait_ge(S("pool_set"), 5)
                        sp.dma_start(memn, a["mem"]).then_inc(S("mem_loaded"), 16)
                    if i == 3 and name == "w_in1a":
                        acc_done(sp, ACC["down0"] + 7)
                        sp.wait_ge(S("conv_zero"), 1)
                        sp.dma_start(cext[:, :, 3 + TP:CEX], a["lruconv"]).then_inc(S("conv_past"), 16)
                if looped:
                    with sp.Fori(0, k // 4 - 2) as i:
                        for j in range(4):
                            acc_done(sp, _consumer(b0 + 4 + j), i)
                            s = (b0 + j) % NSLOT
                            sp.dma_start(dst[s], w[name][4 * i + (8 + j)]).then_inc(wfull[s], 16)

            for name in WSEG:
                load(name)
            for name, n in (("out_pool", 1), ("out_kv", 6), ("win_copied", 3), ("out_mem", 4), ("out_conv", 2),
                            ("out_y", 8), ("out_lru", 1)):
                sp.wait_ge(S(name), 16 * n)

        @block.gpsimd
        def _(pool):
            pool.dma_start(idx[:, :], a["pages"]).then_inc(S("pages_loaded"), 16)
            pool.memset(epsc[:, :], EPS).then_inc(S("pool_set"), 1)
            pool.memset(ext, 0.0).then_inc(S("pool_set"), 1)
            pool.memset(qbd, 0.0).then_inc(S("pool_set"), 1)
            pool.wait_ge(S("pool_set"), 2)
            pool.dma_start(ext[:, :, 16 + TP:EXT], a["poolpast"]).then_inc(S("pool_past"), 16)
            def tile_used(n):
                kind, b, kv, hh = TILES[n]
                if kind == "cmp":
                    pool.wait_ge(S("sub_ready"), n + 1)
                elif kind == "win":
                    pool.wait_ge(S("sw_sc" if kv == "k" else "sw_pv"), b + 1)
                elif kind == "slc" and kv == "k":
                    pool.wait_ge(S("kt_tr"), 4 * (2 * b + hh + 1))
                elif kind == "slc":
                    pool.wait_ge(S("sv_used"), 2 * b + hh + 1)
                else:
                    pool.wait_ge(S("mk_used" if kv == "k" else "mv_used"), 8 * int(kind[3]) + b + 1)

            def tile(n):
                kind, b, kv, hh = TILES[n]
                s = PLACE[n]
                if BEFORE[n] is not None:
                    tile_used(BEFORE[n])
                elif s >= NC:
                    pool.wait_ge(S("pa_pv"), 32)
                dst = place_of(n)
                if kind == "cmp" or kind == "slc":
                    pool.indirect_dma_start(dst, None, a[kind + kv], bass.IndirectOffsetOnAxis(
                        ap=idx[:, 2 * b + hh:2 * b + hh + 1].bitcast(U32), axis=0)).then_inc(cfull[s], 16)
                elif kind == "win":
                    pool.dma_start(dst, a["win" + kv][b]).then_inc(cfull[s], 16)
                else:
                    pool.dma_start(dst, a["mem" + kv][int(kind[3]), b]).then_inc(cfull[s], 16)

            def add(r):
                for c in range(0, 8, 2):
                    pool.wait_ge(S("y_scaled"), 8 * r + c + 1)
                    pool.tensor_tensor(x[:, c, :], x[:, c, :], y[:, c, :], ALU.add).then_inc(S("x_ready0"), 1)

            def sums(name, upto=7):
                n = NORM[name]
                wd = NMEM if name.startswith("mem") else T
                for c in range(1, upto):
                    pool.wait_ge(S("sq_ready"), 8 * n + c + 1)
                    if c == 1 and n:
                        pool.wait_ge(S("rms_ready"), n)
                    if c > 1:
                        pool.wait_ge(S("sq_summed"), 6 * n + c - 1)
                    pool.tensor_tensor(ssum[:, 0:wd], sq[:, 0, 0:wd] if c == 1 else ssum[:, 0:wd], sq[:, c % 2, 0:wd],
                                       ALU.add).then_inc(S("sq_summed"), 1)

            pool.wait_ge(S("idx_ready"), 1)
            for n in range(NC):
                tile(n)
            k = 0
            at = NC
            for g in range(4):
                pool.wait_ge(S("ext_ready"), g + 1)
                if g:
                    pool.wait_ge(S("pool_d"), g)
                src, lo = ext[:, g, :], 0
                for lev in range(g + 1):
                    dst = bufs[lev % 2]
                    sh = 1 << lev
                    if lev:
                        pool.wait_ge(S("win_step"), k)
                    lo += sh
                    pool.tensor_tensor(dst[:, lo:EXT], src[:, lo:EXT], src[:, lo - sh:EXT - sh],
                                       ALU.add).then_inc(S("win_step"), 1)
                    k += 1
                    src = dst
                pool.wait_ge(S("win_step"), k)
                pool.tensor_tensor(src[:, 16:32], src[:, 16:32], C("poolfix")[:, 16 * g:16 * g + 16],
                                   ALU.mult).then_inc(S("win_step"), 1)
                k += 1
                for _ in range(6):
                    tile(at)
                    at += 1
            for n in range(at, TILE["win", 0, "k", 0]):
                tile(n)
            pool.dma_start(o["wink_s"], a["winold_k"]).then_inc(S("win_copied"), 16)
            pool.dma_start(o["winv_s"], a["winold_v"]).then_inc(S("win_copied"), 16)
            pool.dma_start(o["poolold"], a["poolold"]).then_inc(S("win_copied"), 16)
            for n in range(TILE["win", 0, "k", 0], TILE["mem0", 0, "k", 0]):
                tile(n)
            for l in range(2):
                if l:
                    sums("mix1", 4)
                    for m in range(4, 8):
                        acc_emptied(pool, acc_of("w_in1a", m))
                    pool.tensor_copy(convp, cext[:, :, TP:TP + 3]).then_inc(S("pool_set"), 1)
                    pool.tensor_copy(convs, cext[:, :, 3 + TP:CEX].rearrange("p c (b t) -> p c b t", b=NB)[:, :, :, 4:7]
                                     ).then_inc(S("pool_set"), 1)
                    for m in range(8):
                        acc_emptied(pool, ACC["lru"] + 2 * m + 1)
                        pool.tensor_tensor(big[:, 8 + m, :], big[:, 8 + m, :], mix[:, m, :], ALU.mult).then_inc(S("gated"), 1)
                    pool.wait_ge(S("lmix_ready"), 8)
                n0 = TILE[f"mem{l}", 0, "k", 0]
                for n in range(n0, n0 + NC):
                    tile(n)
                sums(f"mem{l}")
                sums(f"pmix{l}")
                add(3 * l)
                sums(f"xat{l}")
                acc_done(pool, ACC[f"mv{l}"] + 1)
                pool.memset(xqd, 0.0).then_inc(S("xq_zero"), 1)
                for n in range(n0 + NC, n0 + 16):
                    tile(n)
                sums(f"pxat{l}")
                add(3 * l + 1)
                sums(f"ffn_{l}", 4)
                sums(f"pffn{l}")
                add(3 * l + 2)

        @block.scalar
        def _(act):
            def square(name, c, src):
                n = NORM[name]
                wd = NMEM if name.startswith("mem") else T
                if c >= 2:
                    act.wait_ge(S("sq_summed"), 6 * n + max(c - 2, 1))
                elif c == 0 and n:
                    act.wait_ge(S("sq_summed"), 6 * n)
                dst = sq[:, c % 2, 0:wd]
                if len(src.shape) == 3:
                    dst = halves(dst)
                act.activation(dst, src, ACT.Square).then_inc(S("sq_ready"), 1)

            def root(name):
                g = ACC["s_" + name]
                acc_done(act, g)
                if NORM[name]:
                    act.wait_ge(S("rinv_ready"), NORM[name])
                if name.startswith("mem"):
                    src, dst = ps[:, 2 * (g % 4), 0:NMEM], rms[:, 0:NMEM]
                else:
                    src, dst = accp[g % 4], halves(rms[:, :])
                act.activation(dst, src, ACT.Sqrt, bias=epsc[:, 0:1], scale=1.0 / D).then_inc(S("rms_ready"), 1)
                act.wait_ge(S("rms_ready"), NORM[name] + 1)
                act.sem_inc(drained[g % 4], 1)

            def w_hi(b, i=0):
                weights_in(act, b, i)
                n = NSPLIT[b]
                if n >= 2:
                    block_used(act, SPLIT[n - 2], i)
                src, _, dst = block_at(b, tiles_of(b))
                act.activation(dst, src, ACT.Copy).then_inc(S("w_hi"), 1)

            def w_next(name, m, i=0):
                b = WSEG[name][0] + m + 2
                w_hi(b, i)

            def ahead(name, chunks=range(8)):
                r = ["xat0", "ffn_0", "mix1", "xat1", "ffn_1"].index(name)
                for c in chunks:
                    act.wait_ge(S(f"x_ready{c % 2}"), 4 * r + c // 2 + 1)
                    act.activation(hr[:, c, :], x[:, c, :], ACT.Copy, scale=G("gain", 16 * (r + 1) + c)).then_inc(S("xg_ready"), 1)

            def mix_hi(chunks=range(8), sem=None):
                for c in chunks:
                    if sem:
                        act.wait_ge(S(sem), c + 1)
                    act.activation(hr[:, c, :], mix[:, c, :], ACT.Copy).then_inc(S("mix_hi"), 1)

            def evict_y(name, norm, gain):
                down = name.startswith("down")
                for m in range(8):
                    g = acc_of(name, m)
                    for q in range(DB if down else 1):
                        b = WSEG[name][0] + (DB * m + q if down else m) + 2
                        if b < NBLK and not (name in INNER and 0 < m < AFTER):
                            w_hi(b)
                    acc_done(act, g)
                    act.activation(halves(y[:, m, :]), accp[g % 4], ACT.Copy, scale=G("gain", 8 * gain + m)).then_inc(S("y_ready"), 1)
                    square(norm, m, accp[g % 4])
                    act.wait_ge(S("sq_ready"), 8 * NORM[norm] + m + 1)
                    act.sem_inc(drained[g % 4], 1)
                    if m == 0 and name in INNER:
                        for q in range(1, AFTER):
                            w_next(name, q)
                        root(INNER[name])
                    if m == 2 and name in INNER:
                        l = int(name[-1])
                        act.wait_ge(S("memn_ready"), 8 * (l + 1))
                        if l == 0:
                            act.wait_ge(S("out_kv"), 16 * 6)
                        act.activation(memhi, memn, ACT.Copy).then_inc(S("mem_hi"), 1)
                root(norm)

            def evict(g, out, src):
                acc_done(act, g)
                act.activation(out, src, ACT.Copy).then_inc(drained[g % 4], 1)

            act.wait_ge(S("xs_loaded"), 16)
            for c in range(8):
                act.wait_ge(S(f"x_loaded{c // 2}"), 16)
                square("mix0", c, x[:, c, :])
            act.wait_ge(S("const_loaded"), 32)
            act.wait_ge(S("pool_set"), 1)
            root("mix0")
            act.wait_ge(S("sp_abs"), 1)
            act.activation(spb[:, 16:24], spb[:, 24:32], ACT.Exp, scale=-1.0).then_inc(S("sp_exp"), 1)
            for kind, k in FIRST:
                g = ACC[kind, k]
                pa, pb = 2 * (g % 4), 2 * (g % 4) + 1
                if kind == "in":
                    evict(g, halves(big[:, k, :]), accp[g % 4])
                    if k == 3:
                        for q in range(4):
                            acc_emptied(act, ACC["in", q])
                        act.dma_start(o["pool"], big[:, U:U + 4, TP - 15:T]).then_inc(S("out_pool"), 16)
                    if KCM <= k <= VWI:
                        acc_emptied(act, g)
                        act.dma_start(o["kv"][k - KCM], big[:, k, :]).then_inc(S("out_kv"), 16)
                elif kind == "mean":
                    evict(g, meant, ps[:, pa:pa + 2, 0:NSUB])
                elif kind == "cmp":
                    acc_done(act, g)
                    act.activation(kstore[:, k, :], ps[:, pa, 0:NSUB], ACT.Copy)
                    act.activation(vstore[:, k, :], ps[:, pb, 0:NSUB], ACT.Copy).then_inc(drained[g % 4], 1)
                else:
                    acc_done(act, g)
                    if k == 0:
                        act.wait_ge(S("pool_d"), 4)
                    act.activation(halves(mix[:, k, :]), accp[g % 4], ACT.Copy,
                                   scale=G("poolscale", k)).then_inc(drained[g % 4], 1)

            act.wait_ge(S("zeroed"), 1)
            act.wait_ge(S("prep_small"), 1)
            act.activation(kcp, ps[:, 0, 0:32], ACT.Copy).then_inc(S("prep_ready"), 1)
            act.wait_ge(S("prep_small"), 2)
            act.activation(vcp4, ps[:, 5, :].rearrange("p (q n) -> p q n", q=4), ACT.Copy).then_inc(S("prep_ready"), 1)
            for v in range(2):
                act.wait_ge(S("prep_v"), v + 1)
                act.activation(vnat[:, v, :, :].rearrange("p k n -> p (k n)"), ps[:, 1 + v, :],
                               ACT.Copy).then_inc(S("prep_ready"), 1)
            act.wait_ge(S("prep_new"), 1)
            act.activation(vnew[0:TS, :], ps[0:TS, 3, 0:256], ACT.Copy).then_inc(S("prep_ready"), 1)
            act.activation(gtok[0:TS, :], ps[0:TS, 3, 256:280], ACT.Sigmoid).then_inc(S("gates_ready"), 1)
            act.activation(gpr, ps[:, 4, :].rearrange("p (k n) -> p k n", k=4)[:, :, 0:24],
                           ACT.Sigmoid).then_inc(S("gates_ready"), 1)
            act.wait_ge(S("pc_sub"), 1)
            act.activation(pcm, pcm, ACT.Exp, scale=SC).then_inc(S("pc_exp"), 1)
            for k in range(2):
                act.wait_ge(S("pc_tr"), k + 1)
                act.activation(pct[:, k, :], ps[:, k, :], ACT.Copy).then_inc(S("pc_trc"), 1)

            def p_exp(u):
                n = (u % 4 + 1) * P
                for br in range(2):
                    act.wait_ge(S("pa_max"), 2 * u + br + 1)
                    if u >= 2:
                        act.wait_ge(S("pa_tr"), 2 * (u - 2) + br + 1)
                    act.activation(pp[:, u % 2, br, 0:n], ps[:, 2 * (u % 2) + br, 0:n], ACT.Exp,
                                   bias=pst[:, u % 2, br, 1:2], scale=SC,
                                   accum_out=pst[:, u % 2, br, 2:3]).then_inc(S("pa_exp"), 1)

            def p_evac(u):
                n = (u % 4 + 1) * P
                for br in range(2):
                    act.wait_ge(S("pa_tr"), 2 * u + br + 1)
                    if u >= 2:
                        act.wait_ge(S("pa_pv"), u - 1)
                    act.activation(ppt[:, u % 2, br, 0:n], ps[:, 4 + br, 0:n], ACT.Copy).then_inc(S("pa_trc"), 1)

            def p_out(c):
                act.wait_ge(S("pa_pv"), 8 * c + 8)
                act.activation(mix[:, 4 + c, 0:TP], ps[:, 6 + c % 2, :], ACT.Copy).then_inc(S("pa_out"), 1)

            for u in range(34):
                if 1 <= u <= 32:
                    p_evac(u - 1)
                if u < 32:
                    p_exp(u)
                if u >= 2 and (u - 2) % 8 == 7:
                    p_out((u - 2) // 8)

            def soft(sbuf, k):
                act.wait_ge(S("sm_max"), k + 1)
                act.activation(sbuf, sbuf, ACT.Exp, bias=sst[:, k, 1:2], scale=SC,
                               accum_out=sst[:, k, 2:3]).then_inc(S("sm_exp"), 1)

            for hb in range(2):
                soft(pce[:, 1:256], 3 * hb)
                act.wait_ge(S("sw_sc"), hb + 1)
                act.activation(swin[:, 0:512], ps[:, 2, :], ACT.Copy).then_inc(S("sw_cp"), 1)
                for k in range(32):
                    n = 32 * hb + k
                    act.wait_ge(S("kt_tr"), n + 1)
                    if n >= 2:
                        act.wait_ge(S("kt_sc"), n - 1)
                    act.activation(ktb[:, n % 2, :], ps[:, n % 2, :], ACT.Copy).then_inc(S("kt_trc"), 1)
                    if k == 3:
                        soft(swin, 3 * hb + 1)
                    if k == 11:
                        act.wait_ge(S("sc_tr"), hb + 1)
                        act.activation(pst2, ps[:, 6, 0:256], ACT.Copy).then_inc(S("sc_trc"), 1)
                        act.wait_ge(S("sw_tr"), hb + 1)
                        act.activation(pwt, ps[:, 4, :], ACT.Copy).then_inc(S("sw_trc"), 1)
                        act.activation(pwn[0:TS, :], ps[0:TS, 5, 384:512], ACT.Copy).then_inc(S("sw_trc"), 1)

                def s_exp(k):
                    piece = sslc[:, 512 * k:min(512 * k + 512, PAST + TS)]
                    act.activation(piece, piece, ACT.Exp, bias=sst[:, 3 * hb + 2, 1:2], scale=SC,
                                   accum_out=sxs[:, k:k + 1]).then_inc(S("sx_exp"), 1)

                act.wait_ge(S("sm_max"), 3 * hb + 3)
                for k in range(11):
                    if k < 9:
                        s_exp(k)
                    if 2 <= k < 10:
                        act.wait_ge(S("sp_tr"), 8 * hb + k - 1)
                        act.activation(spt[:, (k - 2) * 512:(k - 1) * 512], ps[:, k % 2, :], ACT.Copy).then_inc(S("sp_trc"), 1)
                act.wait_ge(S("spn_tr"), hb + 1)
                act.activation(spn[0:TS, :], ps[0:TS, 5, 0:P], ACT.Copy).then_inc(S("spn_trc"), 1)
            for m in range(2):
                w_hi(WSEG["w_out0"][0] + m)
            act.wait_ge(S("so_done"), 2)
            for g in range(2):
                rows = slice(64 * g, 64 * g + 64)
                for c in range(4):
                    act.activation(
                        sample(mix[rows, 4 + c, TP:T]),
                        ps[rows, 7, 0:256].rearrange("p (b g c t) -> p b g c t", g=2, c=4, t=4)[:, :, g, c, :],
                        ACT.Copy).then_inc(S("so_out"), 1)
            act.wait_ge(S("so_out"), 8)
            mix_hi()

            def cross(l):

                def x_exp(qt):
                    n = 4 * l + qt
                    act.wait_ge(S("xp_max"), n + 1)
                    if n:
                        act.wait_ge(S("xp_tr"), 2 * n)
                    for hd in range(4):
                        act.activation(xpp[:, hd, :], ps[:, 2 + hd // 2, (hd % 2) * 256:(hd % 2) * 256 + 256],
                                       ACT.Exp, bias=xpm[:, 4 + hd:5 + hd], scale=SX,
                                       accum_out=xpm[:, 8 + hd:9 + hd]).then_inc(S("xp_exp"), 1)

                def x_evac(qt):
                    n = 4 * l + qt
                    for k in range(2):
                        act.wait_ge(S("xp_tr"), 2 * n + k + 1)
                        act.activation(xpt[:, 4 * k:4 * k + 4, qt * P:qt * P + P],
                                       ps[:, 4 + k, :].rearrange("p (i t) -> p i t", i=4), ACT.Copy).then_inc(S("xp_trc"), 1)

                def s_copy(hb):
                    act.wait_ge(S("mv_used"), 8 * l + 4 * (hb + 1))
                    act.activation(xvr[:, hb, 0:512], ps[:, 6 * hb, :], ACT.Copy).then_inc(S("xv_copied_a"), 1)

                def s_out(hb):
                    act.wait_ge(S("xv_tr"), 2 * l + hb + 1)
                    for hd in (0, 1):
                        for q in range(2):
                            dst, src = s_places(hb, hd, q)
                            act.activation(dst, src, ACT.Copy).then_inc(S("xv_out_a"), 1)

                x_exp(0)
                act.wait_ge(S("xs_max"), l + 1)
                act.activation(xsp, ps[:, 1, 0:256], ACT.Exp, bias=xsm[:, 1:2], scale=SX,
                               accum_out=xsm[:, 2:3]).then_inc(S("xs_exp"), 1)
                x_evac(0)
                x_exp(1)
                act.wait_ge(S("xs_tr"), l + 1)
                act.activation(xst, ps[:, 0, 256:512], ACT.Copy).then_inc(S("xs_trc"), 1)
                s_copy(0)
                x_evac(1)
                x_exp(2)
                s_out(0)
                x_evac(2)
                x_exp(3)
                s_copy(1)
                x_evac(3)
                s_out(1)
                act.wait_ge(S("xv_out_a"), 8 * (l + 1))
                act.wait_ge(S("xv_out_v"), 8 * (l + 1))
                for c in range(8):
                    act.wait_ge(S("xp_pv"), 8 * l + c + 1)
                    act.activation(mix[:, c, 0:TP], ps[:, 2 + c % 2, :], ACT.Copy).then_inc(S("xo_in"), 1)
                    act.wait_ge(S("xo_in"), 8 * l + c + 1)
                    mix_hi([c])

            def layer_end(l):
                act.wait_ge(S("mem_loaded"), 16 * (l + 1))
                for c in range(8):
                    square(f"mem{l}", c, memn[:, c, :])
                evict_y(f"w_out{l}", f"pmix{l}", 6 * l + 1)
                if l:
                    act.wait_ge(S("out_mem"), 32)
                for m in range(8):
                    w_next(f"mk{l}", m)
                    g = ACC[f"mk{l}"] + m
                    evict(g, kstore[:, m, :], ps[:, 2 * (g % 4), 0:NMEM])
                    if m >= 4:
                        ahead(f"xat{l}", [m - 4])
                for m in range(4, 8):
                    acc_emptied(act, ACC[f"mk{l}"] + m)
                act.dma_start(o["memk"][l], kstore[:, :, :]).then_inc(S("out_mem"), 16)
                for m in range(8):
                    w_next(f"mv{l}", m)
                    if m % 4 == 3:
                        f, g = m // 4, ACC[f"mv{l}"] + m // 4
                        evict(g, vst2[:, :, f * 512:f * 512 + 512], ps[:, 2 * (g % 4):2 * (g % 4) + 2, :])
                    if m < 4:
                        ahead(f"xat{l}", [4 + m])
                    square(f"xat{l}", m, x[:, m, :])
                for f in range(2):
                    acc_emptied(act, ACC[f"mv{l}"] + f)
                act.dma_start(o["memv"][l], vstore[:, :, :]).then_inc(S("out_mem"), 16)
                for m in range(AFTER):
                    w_next(f"xq{l}", m)
                root(f"xat{l}")
                for m in range(AFTER, 8):
                    w_next(f"xq{l}", m)
                cross(l)
                evict_y(f"xo{l}", f"pxat{l}", 6 * l + 3)
                ahead(f"ffn_{l}")
                name = f"ffn{l}"
                for m in range(8):
                    square(f"ffn_{l}", m, x[:, m, :])
                    if m == 5:
                        w_next(name, 0)

                def hid_parts(gs, m, hid, hh, k, i=0):
                    for j in range(2):
                        if m + 2 * j >= AFTER:
                            w_next(name, m + 2 * j, i)
                        acc_emptied(act, gs[2 * j], i)
                        act.activation(hid[j], hid[j], ACT.Silu).then_inc(S("silu_ready"), 1)
                        if m + 2 * j + 1 >= AFTER:
                            w_next(name, m + 2 * j + 1, i)
                        act.wait_ge(S("hidden"), 2 * i + (k + j + 1))
                        act.activation(hh[j], hid[j], ACT.Copy).then_inc(S("hid_hi"), 1)

                for m in range(1, AFTER):
                    w_next(name, m)
                root(f"ffn_{l}")
                hid_parts([acc_of(name, j) for j in range(4)], 0, [big[:, j, :] for j in range(2)],
                          [hidhi[:, j, :] for j in range(2)], FC * l)
                with act.Fori(0, FC // 2 - 1) as i:
                    hid_parts([acc_of(name, 4 + j) for j in range(4)], 4, [big[:, 2 * i + (2 + j), :] for j in range(2)],
                              [hidhi[:, 2 * i + (2 + j), :] for j in range(2)], FC * l + 2, i)
                evict_y(f"down{l}", f"pffn{l}", 6 * l + 5)

            layer_end(0)

            ahead("mix1")
            for m in range(8):
                square("mix1", m, x[:, m, :])
                if m == 5:
                    w_next("w_in1a", 0)
            for m in range(1, AFTER):
                w_next("w_in1a", m)
            root("mix1")
            for m in range(AFTER, 6):
                w_next("w_in1a", m)
            act.wait_ge(S("pool_set"), 5)
            act.dma_start(o["conv_p"], convp).then_inc(S("out_conv"), 16)
            act.dma_start(o["conv_s"], convs).then_inc(S("out_conv"), 16)
            for m in range(8):
                for k in range(2):
                    g = ACC["lru"] + 2 * m + k
                    acc_done(act, g)
                    if m == 5 and k == 1:
                        act.wait_ge(S("xf_ready"), 8)
                    act.activation(halves(big[:, 8 * k + m, :]), accp[g % 4], ACT.Sigmoid,
                                   bias=G("ba" if k == 0 else "bx", m)).then_inc(drained[g % 4], 1)
                if m == 4 or m == 6:
                    w_hi(WSEG["w_in1b"][0] + m // 2 - 2)
            act.wait_ge(S("sp_ready"), 1)
            for m in range(12, 16):
                acc_emptied(act, ACC["lru"] + m)
            for half in range(2):
                for m in range(4 * half, 4 * half + 4):
                    if half:
                        act.wait_ge(S("gated_scaled"), m - 3)
                    act.activation(th[m % 4], big[:, m, :], ACT.Tanh, scale=lsp[:, m:m + 1]).then_inc(S("th_ready"), 1)
                    act.wait_ge(S("th_ready"), m + 1)
                    act.activation(big[:, m, :], big[:, m, :], ACT.Exp, scale=lsn[:, m:m + 1]).then_inc(S("a_ready"), 1)
                    act.wait_ge(S("a_ready"), m + 1)
                    act.wait_ge(S("gated"), m + 1)
                    act.activation(mix[:, m, :], big[:, m, :], ACT.Square).then_inc(S("a2_ready"), 1)
                    if m % 2:
                        w_next("w_in1b", m // 2)
                for m in range(4 * half, 4 * half + 4):
                    act.wait_ge(S("m2_ready"), m + 1)
                    act.activation(th[m % 4], th[m % 4], ACT.Sqrt).then_inc(S("mult_ready"), 1)
            for m in range(8):
                if m >= 4:
                    w_next("w_in1b", m)
                if m == 7:
                    acc_done(act, ACC["w_in1b"] + 7)
                    mix_hi(range(4), "lmix_ready")
                acc_emptied(act, ACC["w_in1b"] + m)
                act.activation(yb[:, m, :], yb[:, m, :], ACT.Gelu_apprx_tanh).then_inc(S("gelu_ready"), 1)
            mix_hi(range(4, 8), "lmix_ready")
            act.wait_ge(S("lru_done"), 2)
            act.dma_start(o["lru_h"], lh[:, :, :]).then_inc(S("out_lru"), 16)
            layer_end(1)
            for c in range(0, 8, 2):
                for q in range(2):
                    act.wait_ge(S(f"x_ready{q}"), 20 + c // 2 + 1)
                act.dma_start(o["yp"][:, c:c + 2, :], x[:, c:c + 2, 0:TP]).then_inc(S("out_y"), 16)
                act.dma_start(o["ys"][:, c:c + 2, :], x[:, c:c + 2, TP:T]).then_inc(S("out_y"), 16)

        @block.vector
        def _(dve):
            steps = [0]

            def link(ins):
                steps[0] += 1
                ins.then_inc(S("dve_step"), 1)
                dve.wait_ge(S("dve_step"), steps[0])

            def sums(name, first=4):
                for c in range(first, 7):
                    dve.wait_ge(S("sq_ready"), 8 * NORM[name] + c + 1)
                    if c > 1:
                        dve.wait_ge(S("sq_summed"), 6 * NORM[name] + c - 1)
                    dve.tensor_tensor(ssum[:, :], sq[:, 0, :] if c == 1 else ssum[:, :], sq[:, c % 2, :],
                                      ALU.add).then_inc(S("sq_summed"), 1)

            sums("mix0", 1)
            dve.wait_ge(S("const_loaded"), 32)
            dve.wait_ge(S("pages_loaded"), 16)
            dve.tensor_scalar(idx[:, :], idx[:, :], 8.0, C("subrow"), ALU.mult, ALU.add).then_inc(S("idx_ready"), 1)
            def inverse(name):
                wd = NMEM if name.startswith("mem") else T
                dve.wait_ge(S("rms_ready"), NORM[name] + 1)
                dve.reciprocal(rinv[:, 0:wd], rms[:, 0:wd]).then_inc(S("rinv_ready"), 1)
                dve.wait_ge(S("rinv_ready"), NORM[name] + 1)

            def norm_apply(name, gain):
                inverse(name)
                for c in range(8):
                    dve.scalar_tensor_tensor(out=h[:, c, :], in0=x[:, c, :], scalar=G("gain", 8 * gain + c),
                                             in1=rinv[:, :], op0=ALU.mult, op1=ALU.mult).then_inc(S("h_ready"), 1)

            def residual(name, r, between=None):
                inverse(name)
                dve.wait_ge(S("y_ready"), 8 * (r + 1))
                for c in range(9):
                    if c < 8:
                        dve.tensor_tensor(y[:, c, :], y[:, c, :], rinv[:, :], ALU.mult).then_inc(S("y_scaled"), 1)
                    if c and c % 2 == 0:
                        dve.wait_ge(S("y_scaled"), 8 * r + c)
                        dve.tensor_tensor(x[:, c - 1, :], x[:, c - 1, :], y[:, c - 1, :], ALU.add).then_inc(S("x_ready1"), 1)
                    if between and c in (0, 3, 6, 8):
                        w_next(between, 3 + (0, 3, 6, 8).index(c))
                if r < 5 and not between:
                    for c in range(8):
                        x_lo(r, c)

            def w_lo(b, i=0):
                dve.wait_ge(S("w_hi"), 4 * i + (NSPLIT[b] + 1))
                src, lo, hi = block_at(b, tiles_of(b))
                dve.tensor_tensor(lo, src, F(hi), ALU.subtract).then_inc(S("w_lo"), 1)

            def w_next(name, m, i=0):
                w_lo(WSEG[name][0] + m + 2, i)

            def x_lo(r, c):
                dve.wait_ge(S("xg_ready"), 8 * r + c + 1)
                dve.scalar_tensor_tensor(out=yr[:, c, :], in0=x[:, c, :], scalar=G("gain", 16 * (r + 1) + c), in1=F(hr[:, c, :]),
                                         op0=ALU.mult, op1=ALU.subtract).then_inc(S("x_lo"), 1)

            def mix_lo(r, chunks=range(8)):
                for c in chunks:
                    dve.wait_ge(S("mix_hi"), 8 * r + c + 1)
                    dve.tensor_tensor(mixr[:, c, :], mix[:, c, :], F(hr[:, c, :]), ALU.subtract).then_inc(S("mix_lo"), 1)

            norm_apply("mix0", 0)
            lam = par[:, PARAM["lam"]:PARAM["lam"] + 8]
            link(dve.tensor_scalar(spb[:, 32:40], lam, -1.0, None, ALU.mult))
            dve.tensor_tensor(spb[:, 24:32], lam, spb[:, 32:40], ALU.max).then_inc(S("sp_abs"), 1)
            dve.wait_ge(S("sp_exp"), 1)
            e, z, s1, s2, acc = spb[:, 16:24], spb[:, 32:40], spb[:, 40:48], spb[:, 48:56], spb[:, 56:64]
            link(dve.tensor_scalar(s1, e, 2.0, None, ALU.add))
            link(dve.reciprocal(s1, s1))
            link(dve.tensor_tensor(s1, s1, e, ALU.mult))
            link(dve.tensor_tensor(s2, s1, s1, ALU.mult))
            link(dve.tensor_scalar(acc, s2, 1.0 / 17, None, ALU.mult))
            for k in (15, 13, 11, 9, 7, 5, 3):
                link(dve.scalar_tensor_tensor(out=acc, in0=acc, scalar=1.0 / k, in1=s2, op0=ALU.add, op1=ALU.mult))
            link(dve.scalar_tensor_tensor(out=acc, in0=acc, scalar=1.0, in1=s1, op0=ALU.add, op1=ALU.mult))
            link(dve.tensor_scalar(z, z, 0.0, None, ALU.max))
            link(dve.scalar_tensor_tensor(out=acc, in0=acc, scalar=2.0, in1=z, op0=ALU.mult, op1=ALU.add))
            dve.tensor_scalar(lsp, acc, 8.0, None, ALU.mult)
            dve.tensor_scalar(lsn, acc, -8.0, None, ALU.mult).then_inc(S("sp_ready"), 1)
            dve.wait_ge(S("pool_set"), 2)
            dve.wait_ge(S("pool_past"), 16)
            wsteps = 0
            for b in range(NB):
                for kv in range(2):
                    for hh in range(2):
                        n = 4 * b + 2 * kv + hh
                        src = tile_in(dve, "cmp", b, "kv"[kv], hh)
                        if b >= 2:
                            acc_done(dve, ACC["mean", b - 2])
                        dve.tensor_reduce(subs[:, n % 8, :], src.rearrange("p (r c) -> p c r", r=SUB), AXX,
                                          ALU.add).then_inc(S("sub_ready"), 1)
                if b < 4:
                    acc_emptied(dve, ACC["in", b])
                    dve.tensor_copy(ext[:, b, 16:16 + TP], big[:, b, 0:TP])
                    dve.tensor_copy(sample(ext[:, b, 16 + TP:EXT])[:, :, 15:19],
                                    sample(big[:, b, TP:T])).then_inc(S("ext_ready"), 1)
                if 1 <= b <= 4:
                    g = b - 1
                    wsteps += g + 2
                    dve.wait_ge(S("win_step"), wsteps)
                    dve.scalar_tensor_tensor(out=mix[:, 4 + g, 0:TP], in0=bufs[g % 2][:, 16:16 + TP],
                                             scalar=1.0 / POOLW[g], in1=big[:, g, 0:TP], op0=ALU.mult, op1=ALU.subtract)
                    dve.scalar_tensor_tensor(out=sample(mix[:, 4 + g, TP:T]),
                                             in0=sample(bufs[g % 2][:, 16 + TP:EXT])[:, :, 15:19],
                                             scalar=1.0 / POOLW[g], in1=sample(big[:, g, TP:T]),
                                             op0=ALU.mult, op1=ALU.subtract).then_inc(S("pool_d"), 1)

            for k in (VCM, VWI, GT):
                acc_emptied(dve, ACC["in", k])
            for g in range(2):
                rows = slice(64 * g, 64 * g + 64)
                if not g:
                    dve.wait_ge(S("pool_set"), 3)
                for c in range(4):
                    last = dve.tensor_copy(qbd[rows, :].rearrange("p (b g c t) -> p b g c t", g=2, c=4, t=4)[:, :, g, c, :],
                                           sample(big[rows, Q + c, TP:T]))
            last.then_inc(S("qbd_ready"), 1)
            acc_done(dve, ACC["cmp", 7])
            dve.memset(mv4, 0.0)
            dve.memset(vnew, 0.0)
            dve.memset(mp, 0.0)
            for k in range(2):
                last = dve.tensor_reduce(s32[:, k, :], big[:, KCM + k, 0:TP].rearrange("p (s r) -> p s r", r=SUB),
                                         AXX, ALU.add)
            link(last)
            link(dve.tensor_tensor(mp[:, 0:31], s32[:, 0, 0:31], s32[:, 0, 1:32], ALU.add))
            dve.tensor_scalar(mp[:, 0:31], mp[:, 0:31], 1.0 / 32, None, ALU.mult)
            link(dve.tensor_tensor(s32[:, 1, 0:31], s32[:, 1, 0:31], s32[:, 1, 1:32], ALU.add))
            for q in range(4):
                last = dve.tensor_scalar(mv4[:, q, 32 * q:32 * q + 31], s32[:, 1, 0:31], 1.0 / 32, None, ALU.mult)
            last.then_inc(S("means_ready"), 1)
            dve.wait_ge(S("out_pool"), 16)
            dve.memset(pwn, 0.0)
            dve.memset(spn, 0.0)
            dve.memset(pce, 0.0).then_inc(S("zeroed"), 1)
            for hb in range(2):
                dve.wait_ge(S("grow_mm"), 1)
                link(dve.tensor_tensor(grw, ps[:, 0, 64 + 32 * hb:88 + 32 * hb], C("headmask"), ALU.mult))
                link(dve.tensor_reduce(grow[:, hb, :], grw.rearrange("p (h r) -> p r h", r=3), AXX, ALU.add))
            dve.wait_ge(S("pc_sc"), 1)
            for k in range(2):
                last = dve.tensor_tensor(pcm[:, 512 * k:512 * k + 512].rearrange("p (h n) -> p h n", h=4),
                                         ps[:, 6 + k, :].rearrange("p (h n) -> p h n", h=4),
                                         C("cmpbias").unsqueeze(1).to_broadcast([P, 4, P]), ALU.add)
            link(last)
            pc3 = pcm.rearrange("p (u n) -> p u n", n=32)

            def over(col):
                return col.unsqueeze(2).to_broadcast([P, 32, 32])

            link(dve.tensor_reduce(pcs[:, 0, :], pc3, AXX, ALU.max))
            dve.tensor_tensor(pc3, pc3, over(pcs[:, 0, :]), ALU.subtract).then_inc(S("pc_sub"), 1)
            dve.wait_ge(S("pc_exp"), 1)
            link(dve.tensor_reduce(pcs[:, 1, :], pc3, AXX, ALU.add))
            link(dve.reciprocal(pcs[:, 2, :], pcs[:, 1, :]))
            dve.wait_ge(S("gates_ready"), 2)
            r4 = pcs[:, 2, :].rearrange("p (h q) -> p h q", q=4)
            gv = gpr.rearrange("p q (g c r) -> p g c r q", g=2, c=4)
            for c in range(4):
                for g in range(2):
                    last = dve.tensor_tensor(r4[:, 4 * g + c, :], r4[:, 4 * g + c, :], gv[:, g, c, 0, :], ALU.mult)
            link(last)
            link(dve.tensor_scalar(r4[:, :, 0], r4[:, :, 0], C("anyblock"), None, ALU.mult))
            dve.tensor_tensor(pc3, pc3, over(pcs[:, 2, :]), ALU.mult).then_inc(S("pc_norm"), 1)

            def p_max(u):
                qt = u % 4
                n = (qt + 1) * P
                for br in range(2):
                    dve.wait_ge(S("pa_sc"), 2 * u + br + 1)
                    bank = 2 * (u % 2) + br
                    diag = ps[:, bank, qt * P:n]
                    link(dve.tensor_tensor(diag, diag, C("causal"), ALU.add))
                    link(dve.tensor_reduce(pst[:, u % 2, br, 0:1], ps[:, bank, 0:n], AXX, ALU.max))
                    dve.tensor_scalar(pst[:, u % 2, br, 1:2], pst[:, u % 2, br, 0:1], -SC, None,
                                      ALU.mult).then_inc(S("pa_max"), 1)

            def p_norm(u):
                c, g, qt = u // 8, u // 4 % 2, u % 4
                n = (qt + 1) * P
                for br in range(2):
                    dve.wait_ge(S("pa_exp"), 2 * u + br + 1)
                    link(dve.reciprocal(pst[:, u % 2, br, 3:4], pst[:, u % 2, br, 2:3]))
                    gate = gpr[:, qt, 3 * (4 * g + c) + 1 + br:3 * (4 * g + c) + 2 + br]
                    dve.tensor_scalar(pp[:, u % 2, br, 0:n], pp[:, u % 2, br, 0:n], pst[:, u % 2, br, 3:4], gate,
                                      ALU.mult, ALU.mult).then_inc(S("pa_norm"), 1)

            for u in range(33):
                if u:
                    p_norm(u - 1)
                if u < 32:
                    p_max(u)

            def s_max(sbuf, k):
                link(dve.tensor_reduce(sst[:, k, 0:1], sbuf, AXX, ALU.max))
                dve.tensor_scalar(sst[:, k, 1:2], sst[:, k, 0:1], -SC, None, ALU.mult).then_inc(S("sm_max"), 1)

            def s_inv(k, n):
                dve.wait_ge(S("sm_exp"), n)
                link(dve.reciprocal(sst[:, k, 3:4], sst[:, k, 2:3]))

            dve.wait_ge(S("pa_pv"), 32)
            for hb in range(2):
                dve.wait_ge(S("sc_sc"), hb + 1)
                if hb:
                    dve.wait_ge(S("sc_tr"), 1)
                link(dve.tensor_copy(pce[:, 1:256], ps[:, 4, 0:255]))
                s_max(pce[:, 1:256], 3 * hb)
                s_inv(3 * hb, 2 * hb + 1)
                dve.tensor_scalar(pce[:, 1:256], pce[:, 1:256], sst[:, 3 * hb, 3:4], None,
                                  ALU.mult).then_inc(S("sc_norm"), 1)
                dve.wait_ge(S("sc_imp"), hb + 1)
                imp = sel[:, 0:65]
                link(dve.tensor_copy(imp, ps[:, 5, 0:257:4]))
                for k in range(1, 5):
                    link(dve.tensor_tensor(imp, imp, ps[:, 5, k:k + 257:4], ALU.add))
                dve.memset(sel[:, 0:1], FORCE)
                link(dve.memset(sel[:, 63:65], FORCE))
                for _ in range(2):
                    link(dve.max(m8, imp))
                    link(dve.match_replace(imp, m8, imp, -2.0))
                dve.tensor_scalar(maskb[:, 0:65], imp, -1.0, NEG, ALU.is_gt, ALU.mult)
                dve.tensor_scalar(pce[:, 1:256], pce[:, 1:256], grow[:, hb, 0:1], None,
                                  ALU.mult).then_inc(S("sc_gate"), 1)
                dve.wait_ge(S("sw_cp"), hb + 1)
                dve.tensor_tensor(swin[:, 0:4], swin[:, 0:4], C("oldbias"), ALU.add)
                if hb:
                    dve.wait_ge(S("sw_tr"), 1)
                dve.tensor_tensor(swin[:, 512:544], ps[:, 3, 0:TS], C(f"newbias{hb}"), ALU.add).then_inc(S("sw_new"), 1)
                dve.wait_ge(S("sw_new"), hb + 1)
                s_max(swin, 3 * hb + 1)
                if hb:
                    dve.wait_ge(S("sp_tr"), 8)
                    dve.wait_ge(S("spn_tr"), 1)
                for k in range(33):
                    if k < 32:
                        n = 32 * hb + k
                        j, hh, q = k // 8, k // 4 % 2, k % 4
                        rows = slice(32 * j, 32 * j + 32)
                        at = (16 * hh + 4 * q) * P
                        dve.wait_ge(S("kt_sc"), n + 1)
                        dve.tensor_tensor(
                            sslc[rows, at:at + 512].rearrange("p (r b s) -> p r b s", r=4, s=4),
                            ps[rows, 2 + n % 2, :].rearrange("p (r b s) -> p r b s", r=4, s=4),
                            maskb[rows, 32 * hh:32 * hh + 32].unsqueeze(1).unsqueeze(3).to_broadcast([32, 4, 32, 4]),
                            ALU.add).then_inc(S("sl_ev"), 1)
                    if k > 24:
                        q = k - 25
                        dve.wait_ge(S("sl_ev"), 32 * hb + k)
                        dve.tensor_reduce(smx[:, q:q + 1], sslc[:, 512 * q:512 * q + 512], AXX, ALU.max)
                    if k == 7:
                        s_inv(3 * hb + 1, 2 * hb + 2)
                        dve.tensor_scalar(swin, swin, sst[:, 3 * hb + 1, 3:4], grow[:, hb, 2:3], ALU.mult,
                                          ALU.mult).then_inc(S("sw_norm"), 1)
                dve.wait_ge(S("sl_new"), hb + 1)
                link(dve.tensor_tensor(sslc[:, PAST:PAST + TS], ps[:, 4, 0:TS], C(f"newbias{hb}"), ALU.add))
                link(dve.tensor_reduce(smx[:, 8:9], sslc[:, PAST:PAST + TS], AXX, ALU.max))
                s_max(smx, 3 * hb + 2)
                dve.wait_ge(S("sx_exp"), 9 * (hb + 1))
                link(dve.tensor_reduce(sst[:, 3 * hb + 2, 2:3], sxs, AXX, ALU.add))
                link(dve.reciprocal(sst[:, 3 * hb + 2, 3:4], sst[:, 3 * hb + 2, 2:3]))
                link(dve.tensor_scalar(sfac, sst[:, 3 * hb + 2, 3:4], grow[:, hb, 1:2], None, ALU.mult))
                dve.wait_ge(S("so_rows"), hb + 1)
                link(dve.tensor_scalar(orow, ps[:, 6, 256:384], sfac, None, ALU.mult))
                dve.tensor_tensor(orow, orow, ps[:, 7, 256 + P * hb:384 + P * hb], ALU.add).then_inc(S("so_copied"), 1)

            def layer_end(l):
                name = f"w_out{l}"
                if l == 0:
                    w_lo(WSEG[name][0])
                    w_lo(WSEG[name][0] + 1)
                    mix_lo(0)
                for m in range(AFTER):
                    w_next(name, m)
                inverse(f"mem{l}")
                for c in range(8):
                    dve.scalar_tensor_tensor(out=memn[:, c, :], in0=memn[:, c, :], scalar=G("memgain", 8 * l + c),
                                             in1=rinv[:, 0:NMEM], op0=ALU.mult, op1=ALU.mult).then_inc(S("memn_ready"), 1)
                dve.wait_ge(S("mem_hi"), l + 1)
                dve.tensor_tensor(memlo, memn, F(memhi), ALU.subtract).then_inc(S("mem_lo"), 1)
                for m in range(AFTER, 8):
                    w_next(name, m)
                dve.wait_ge(S("memn_ready"), 8 * (l + 1))
                for m in range(3):
                    w_next(f"mk{l}", m)
                residual(f"pmix{l}", 3 * l, f"mk{l}")
                w_next(f"mk{l}", 7)
                x_lo(3 * l, 0)
                x_lo(3 * l, 1)
                for m in range(8):
                    w_next(f"mv{l}", m)
                    if m < 6:
                        x_lo(3 * l, 2 + m)
                if l == 0:
                    dve.wait_ge(S("out_kv"), 16 * 6)
                for m in range(AFTER):
                    w_next(f"xq{l}", m)
                inverse(f"xat{l}")
                for m in range(8):
                    g = acc_of(f"xq{l}", m)
                    acc_done(dve, g)
                    dve.tensor_tensor(halves(big[:, m, :]), accp[g % 4], halves(rinv[:, :]), ALU.mult).then_inc(drained[g % 4], 1)
                    if m >= AFTER:
                        w_next(f"xq{l}", m)
                dve.wait_ge(S("xq_zero"), l + 1)
                for c in range(8):
                    acc_emptied(dve, acc_of(f"xq{l}", c))
                    for q in range(2):
                        last = dve.tensor_copy(xqd[:, q::2, c, 16 * q + 4 * (c // 2):16 * q + 4 * (c // 2) + 4],
                                               sample(big[:, c, TP:T])[:, q::2, :])
                last.then_inc(S("xq_apart"), 1)

                def x_soft(qt):
                    n = 4 * l + qt
                    dve.wait_ge(S("xp_sc"), n + 1)
                    link(dve.tensor_reduce(xpm[:, 0:4], ps[:, 2:4, :].rearrange("p a (h n) -> p (a h) n", h=2), AXX, ALU.max))
                    dve.tensor_scalar(xpm[:, 4:8], xpm[:, 0:4], -SX, None, ALU.mult).then_inc(S("xp_max"), 1)
                    dve.wait_ge(S("xp_exp"), 4 * (n + 1))
                    link(dve.reciprocal(xpm[:, 12:16], xpm[:, 8:12]))
                    dve.tensor_tensor(xpp, xpp, xpm[:, 12:16].unsqueeze(2).to_broadcast([P, 4, 256]),
                                      ALU.mult).then_inc(S("xp_norm"), 1)

                def s_copy(hb):
                    dve.wait_ge(S("mv_used"), 8 * l + 4 * (hb + 1))
                    dve.tensor_copy(xvr[:, hb, 512:1024], ps[:, 6 * hb + 1, :]).then_inc(S("xv_copied_v"), 1)

                def s_out(hb):
                    dve.wait_ge(S("xv_tr"), 2 * l + hb + 1)
                    for hd in (2, 3):
                        for q in range(2):
                            dst, src = s_places(hb, hd, q)
                            dve.tensor_copy(dst, src).then_inc(S("xv_out_v"), 1)

                x_soft(0)
                dve.wait_ge(S("mk_used"), 8 * (l + 1))
                link(dve.tensor_reduce(xsm[:, 0:1], ps[:, 1, 0:256], AXX, ALU.max))
                dve.tensor_scalar(xsm[:, 1:2], xsm[:, 0:1], -SX, None, ALU.mult).then_inc(S("xs_max"), 1)
                dve.wait_ge(S("xs_exp"), l + 1)
                link(dve.reciprocal(xsm[:, 3:4], xsm[:, 2:3]))
                dve.tensor_scalar(xsp, xsp, xsm[:, 3:4], None, ALU.mult).then_inc(S("xs_norm"), 1)
                x_soft(1)
                s_copy(0)
                x_soft(2)
                s_out(0)
                x_soft(3)
                s_copy(1)
                s_out(1)
                mix_lo(2 * l + 1)
                for m in range(8):
                    w_next(f"xo{l}", m)
                residual(f"pxat{l}", 3 * l + 1)
                sums(f"ffn_{l}")
                dve.wait_ge(S("out_mem"), 32 * (l + 1))
                name = f"ffn{l}"
                for m in range(AFTER):
                    w_next(name, m)
                inverse(f"ffn_{l}")

                def hidden(gs, m, hid, lo, hh, n0, i=0):
                    for j in range(2):
                        g = gs[2 * j]
                        acc_done(dve, g, i)
                        dve.tensor_tensor(halves(hid[j]), accp[g % 4], halves(rinv[:, :]), ALU.mult).then_inc(drained[g % 4], 1)
                        if m + 2 * j >= AFTER:
                            w_next(name, m + 2 * j, i)
                        g = gs[2 * j + 1]
                        acc_done(dve, g, i)
                        dve.tensor_tensor(halves(uprow[:, j, :]), accp[g % 4], halves(rinv[:, :]), ALU.mult).then_inc(drained[g % 4], 1)
                        acc_emptied(dve, g, i)
                        dve.wait_ge(S("silu_ready"), 2 * i + (n0 + j + 1))
                        dve.tensor_tensor(hid[j], hid[j], uprow[:, j, :], ALU.mult).then_inc(S("hidden"), 1)
                        if m + 2 * j + 1 >= AFTER:
                            w_next(name, m + 2 * j + 1, i)
                        dve.wait_ge(S("hid_hi"), 2 * i + (n0 + j + 1))
                        dve.tensor_tensor(lo[j], hid[j], F(hh[j]), ALU.subtract).then_inc(S("hid_lo"), 1)

                hidden([acc_of(name, j) for j in range(4)], 0, [big[:, j, :] for j in range(2)], [big_r[:, j, :] for j in range(2)],
                       [hidhi[:, j, :] for j in range(2)], FC * l)
                with dve.Fori(0, FC // 2 - 1) as i:
                    hidden([acc_of(name, 4 + j) for j in range(4)], 4, [big[:, 2 * i + (2 + j), :] for j in range(2)],
                           [big_r[:, 2 * i + (2 + j), :] for j in range(2)],
                           [hidhi[:, 2 * i + (2 + j), :] for j in range(2)], FC * l + 2, i)
                for m in range(8 * DB):
                    b = WSEG[f"down{l}"][0] + m + 2
                    if b < NBLK:
                        w_lo(b)
                if l == 0:
                    acc_done(dve, ACC["down0"] + 7)
                    dve.memset(cext[:, :, 0:3], 0.0).then_inc(S("conv_zero"), 1)
                residual(f"pffn{l}", 3 * l + 2)

            layer_end(0)

            sums("mix1")
            for m in range(AFTER):
                w_next("w_in1a", m)
            inverse("mix1")
            dve.wait_ge(S("conv_past"), 16)
            n = CEX - 3
            for m in range(8):
                g = acc_of("w_in1a", m)
                pa = 2 * (g % 4)
                acc_done(dve, g)
                dve.tensor_tensor(cext[:, m, 3:3 + H], ps[:, pa, 0:H], rinv[:, 0:H], ALU.mult)
                dve.tensor_tensor(cext[:, m, 3 + H:3 + TP], ps[:, pa + 1, 0:TP - H], rinv[:, H:TP], ALU.mult)
                dve.tensor_tensor(sample(cext[:, m, 3 + TP:CEX])[:, :, 3:7], sample(ps[:, pa + 1, TP - H:H]),
                                  sample(rinv[:, TP:T]), ALU.mult).then_inc(drained[g % 4], 1)
                acc_emptied(dve, g)
                link(dve.tensor_scalar(cv[m % 2][:, 0:n], cext[:, m, 0:n], G("convw", m), G("convb", m), ALU.mult, ALU.add))
                for k in (1, 2):
                    link(dve.scalar_tensor_tensor(out=cv[m % 2][:, 0:n], in0=cext[:, m, k:k + n], scalar=G("convw", 8 * k + m),
                                                  in1=cv[m % 2][:, 0:n], op0=ALU.mult, op1=ALU.add))
                dve.scalar_tensor_tensor(out=mix[:, m, 0:TP], in0=cext[:, m, 3:3 + TP], scalar=G("convw", 24 + m),
                                         in1=cv[m % 2][:, 0:TP], op0=ALU.mult, op1=ALU.add)
                dve.scalar_tensor_tensor(out=sample(mix[:, m, TP:T]), in0=sample(cext[:, m, 3 + TP:CEX])[:, :, 3:7],
                                         scalar=G("convw", 24 + m), in1=sample(cv[m % 2][:, 3 + TP:CEX])[:, :, 0:4],
                                         op0=ALU.mult, op1=ALU.add).then_inc(S("xf_ready"), 1)
                if AFTER + m < 6:
                    w_next("w_in1a", AFTER + m)

            def branch(m):
                g = ACC["w_in1b"] + m
                acc_done(dve, g)
                dve.tensor_tensor(halves(yb[:, m, :]), accp[g % 4], halves(rinv[:, :]), ALU.mult).then_inc(drained[g % 4], 1)

            def col(ap, m0, t):
                return ap[:, m0:m0 + 4, TP:T].rearrange("p c (b t) -> p c b t", t=NT)[:, :, :, t]

            dve.wait_ge(S("xf_ready"), 8)
            for m in range(2):
                w_lo(WSEG["w_in1b"][0] + m)
            for half in range(2):
                m0 = 4 * half
                for m in range(m0, m0 + 4):
                    dve.wait_ge(S("a2_ready"), m + 1)
                    dve.scalar_tensor_tensor(out=th[m % 4], in0=mix[:, m, :], scalar=1.0, in1=th[m % 4],
                                             op0=ALU.add, op1=ALU.mult).then_inc(S("m2_ready"), 1)
                    if m % 2:
                        w_next("w_in1b", m // 2)
                branch(2 * half)
                for m in range(m0, m0 + 4):
                    dve.wait_ge(S("mult_ready"), m + 1)
                    link(dve.memset(th[m % 4][:, 0:1], 1.0))
                    dve.tensor_tensor(big[:, 8 + m, :], big[:, 8 + m, :], th[m % 4],
                                      ALU.mult).then_inc(S("gated_scaled"), 1)
                    dve.wait_ge(S("gated_scaled"), m + 1)
                    link(dve.tensor_tensor_scan(mix[:, m, 0:TP], big[:, m, 0:TP], big[:, 8 + m, 0:TP], 0.0, ALU.mult, ALU.add))
                branch(2 * half + 1)
                if not half:
                    dve.wait_ge(S("h0_loaded"), 16)
                for t in range(NT):
                    prev = lh0[:, m0:m0 + 4, :] if t == 0 else col(mix, m0, t - 1)
                    link(dve.tensor_tensor(tmp8[:, 0:4, :], col(big, m0, t), prev, ALU.mult))
                    link(dve.tensor_tensor(col(mix, m0, t), tmp8[:, 0:4, :], col(big, 8 + m0, t), ALU.add))
                dve.tensor_copy(lh[:, m0:m0 + 4, 0:1], mix[:, m0:m0 + 4, TP - 1:TP])
                dve.tensor_copy(lh[:, m0:m0 + 4, 1:9], col(mix, m0, NT - 1)).then_inc(S("lru_done"), 1)

            def gate(m):
                dve.wait_ge(S("gelu_ready"), m + 1)
                dve.tensor_tensor(mix[:, m, :], mix[:, m, :], yb[:, m, :], ALU.mult).then_inc(S("lmix_ready"), 1)

            for m in range(4, 8):
                w_next("w_in1b", m)
                branch(m)
                if m < 7:
                    gate(m - 4)
            gate(3)
            mix_lo(2, [0])
            gate(4)
            mix_lo(2, [1])
            gate(5)
            mix_lo(2, [2])
            gate(6)
            mix_lo(2, [3])
            gate(7)
            mix_lo(2, range(4, 8))
            layer_end(1)

        @block.tensor
        def _(pe):
            pe.wait_ge(S("const_loaded"), 32)

            def mm(out, lhsT, rhs, start, stop, **kw):
                return pe.matmul(out, lhsT, rhs, start=start, stop=stop, **kw)

            def stats(name):
                g = ACC["s_" + name]
                acc_free(pe, g)
                wd = NMEM if name.startswith("mem") else H
                pe.wait_ge(S("sq_summed"), 6 * (NORM[name] + 1))
                banks = range(1 if name.startswith("mem") else 2)
                for a_ in banks:
                    mm(ps[:, 2 * (g % 4) + a_, 0:wd], C("ones"), ssum[:, a_ * wd:a_ * wd + wd], True, False)
                pe.wait_ge(S("sq_ready"), 8 * (NORM[name] + 1))
                for a_ in banks:
                    last = mm(ps[:, 2 * (g % 4) + a_, 0:wd], C("ones"), sq[:, 1, a_ * wd:a_ * wd + wd], False, True)
                last.then_inc(ready[g % 4], 1)

            def plain(g, b, src, tiles, wt, kn, arrives=None):
                weights_in(pe, b)
                for k in range(kn):
                    if arrives:
                        pe.wait_ge(S(arrives), k + 1)
                    for a_ in range(2):
                        last = mm(accp[g % 4][:, a_, :], wring[:, b % NSLOT, (wt + k) * P:(wt + k) * P + P],
                                  src[:, k, a_ * H:a_ * H + H], k == 0, k == kn - 1, skip_group_check=True)
                return last

            def chunk(g, b, hi, lo, n_i=0, tiles=KB, k0=0, kn=KB, arrives=None):
                pe.wait_ge(S("w_lo"), n_i + (NSPLIT[b] + 1))
                _, wl, wh = block_at(b, tiles)
                last = None
                for k in range(tiles):
                    if arrives:
                        pe.wait_ge(S(arrives[0]), arrives[1] + k0 + k + 1)
                    at = slice(k * P, k * P + P)
                    first, end = k0 + k == 0, k0 + k == kn - 1
                    for wt, src, p_ in ((wh, hi, 0), (wh, lo, 1), (wl, hi, 2)):
                        for a_ in range(2):
                            last = mm(accp[g % 4][:, a_, :], wt[:, at], src[:, k0 + k, a_ * H:a_ * H + H],
                                      first and p_ == 0, end and p_ == 2, skip_group_check=True)
                return last

            def linear(name, hi, lo, arrives=None):
                b0, k, _ = WSEG[name]
                if arrives:
                    his, los, n = arrives
                    for m in range(2):
                        g, (_, wl, wh) = acc_of(name, m), block_at(b0 + m, KB)
                        acc_free(pe, g)
                        pe.wait_ge(S("w_lo"), NSPLIT[b0 + m] + 1)
                        for c in range(KC):
                            if not m:
                                pe.wait_ge(S(his), n + c + 1)
                            for wt in (wh, wl):
                                for a_ in range(2):
                                    mm(accp[g % 4][:, a_, :], wt[:, c * P:c * P + P], hi[:, c, a_ * H:a_ * H + H],
                                       c == 0 and wt is wh, False, skip_group_check=True)
                    for m in range(2):
                        g, (_, wl, wh) = acc_of(name, m), block_at(b0 + m, KB)
                        for c in range(KC):
                            if not m:
                                pe.wait_ge(S(los), n + c + 1)
                            for a_ in range(2):
                                last = mm(accp[g % 4][:, a_, :], wh[:, c * P:c * P + P], lo[:, c, a_ * H:a_ * H + H],
                                          False, c == KC - 1, skip_group_check=True)
                        last.then_inc(ready[g % 4], 1)
                    if name in INNER:
                        stats(INNER[name])
                for m in range(2 if arrives else 0, 4 if k > 8 else 8):
                    g = acc_of(name, m)
                    acc_free(pe, g)
                    chunk(g, b0 + m, hi, lo).then_inc(ready[g % 4], 1)
                if k > 8:
                    with pe.Fori(0, k // 4 - 1) as i:
                        for j in range(4):
                            g = acc_of(name, 4 + j)
                            acc_free(pe, g, i)
                            chunk(g, b0 + 4 + j, hi, lo, 4 * i).then_inc(ready[g % 4], 1)

            stats("mix0")
            for kind, k in FIRST:
                g = ACC[kind, k]
                pa, pb = 2 * (g % 4), 2 * (g % 4) + 1
                acc_free(pe, g)
                if kind == "in":
                    last = plain(g, WSEG["w_in"][0] + k, h, 8, 0, KC, None if k else "h_ready")
                elif kind == "mean":
                    for kv in range(2):
                        for hh in range(2):
                            n = 4 * k + 2 * kv + hh
                            pe.wait_ge(S("sub_ready"), n + 1)
                            last = mm(ps[:, pa + kv, 0:NSUB], subs[:, n % 8, :], C("pair")[:, hh * NSUB:hh * NSUB + NSUB],
                                      hh == 0, hh == 1)
                elif kind == "cmp":
                    if k == 0:
                        pe.wait_ge(S("small_loaded"), 32)
                    acc_emptied(pe, ACC["mean", k])
                    mm(ps[:, pa, 0:NSUB], wcmp_sb[:, 0, :], meant[:, 0, :], True, True)
                    for kt in range(2):
                        last = mm(ps[:, pb, kt * P:kt * P + P], meant[:, 1, kt * P:kt * P + P], wcmp_sb[:, 1, :], True, True)
                else:
                    pe.wait_ge(S("pool_d"), k + 1)
                    for a_ in range(2):
                        last = mm(accp[g % 4][:, a_, :], poolw_sb[:, k, :], mix[:, 4 + k, a_ * H:a_ * H + H], True, True)
                last.then_inc(ready[g % 4], 1)

            for kind, k in FIRST[-4:]:
                acc_emptied(pe, ACC[kind, k])
            pe.wait_ge(S("means_ready"), 1)
            mm(ps[:, 0, 0:32], wcmp_sb[:, 0, :], mp, True, True).then_inc(S("prep_small"), 1)
            for q in range(4):
                last = mm(ps[:, 5, q * P:q * P + P], mv4[:, q, :], wcmp_sb[:, 1, :], True, True)
            last.then_inc(S("prep_small"), 1)
            for v, chunk_ in enumerate((VSL, VWI)):
                for k in range(4):
                    last = pe.transpose(ps[:, 1 + v, k * P:k * P + P], big[:, chunk_, k * P:k * P + P], ident)
                last.then_inc(S("prep_v"), 1)
            for k in range(4):
                pe.transpose(ps[:, 4, k * P:k * P + P], big[:, GT, k * P:k * P + P], ident)
            for v, chunk_ in enumerate((VSL, VWI, GT)):
                last = pe.transpose(ps[0:TS, 3, v * P:v * P + P], big[:, chunk_, TP:T], ident)
            last.then_inc(S("prep_new"), 1)
            pe.wait_ge(S("prep_ready"), 1)
            for u in range(32):
                c, g, qt = u // 8, u // 4 % 2, u % 4
                rows = slice(64 * g, 64 * g + 64)
                at = (4 * c + qt) * 32
                last = mm(ps[:, 6 + g, at:at + 32], big[rows, Q + c, qt * P:qt * P + P],
                          kcp[rows, :], True, True)
            last.then_inc(S("pc_sc"), 1)
            pe.wait_ge(S("gates_ready"), 1)
            for hb in range(2):
                last = mm(ps[:, 0, 64 + 32 * hb:88 + 32 * hb], C(f"rep{hb}")[0:TS, :], gtok[0:TS, :], True, True)
            last.then_inc(S("grow_mm"), 1)
            pe.wait_ge(S("prep_ready"), 5)
            pe.wait_ge(S("pc_norm"), 1)
            for hd in range(8):
                last = pe.transpose(ps[:, hd // 4, (hd % 4) * P:(hd % 4) * P + P], pcm[:, hd * P:hd * P + P], ident)
                if hd % 4 == 3:
                    last.then_inc(S("pc_tr"), 1)

            pe.wait_ge(S("pc_trc"), 2)
            pe.wait_ge(S("gates_ready"), 2)

            def p_scores(u):
                c, g, qt = u // 8, u // 4 % 2, u % 4
                n = (qt + 1) * P
                rows = slice(64 * g, 64 * g + 64)
                if u >= 2:
                    pe.wait_ge(S("pa_exp"), 2 * (u - 1))
                for br, kc in enumerate((KSL, KWI)):
                    mm(ps[:, 2 * (u % 2) + br, 0:n], big[rows, Q + c, qt * P:qt * P + P], big[rows, kc, 0:n],
                       True, True).then_inc(S("pa_sc"), 1)

            def p_turn(u):
                for br in range(2):
                    pe.wait_ge(S("pa_norm"), 2 * u + br + 1)
                    if u:
                        pe.wait_ge(S("pa_trc"), 2 * (u - 1) + br + 1)
                    for k in range(u % 4 + 1):
                        last = pe.transpose(ps[:, 4 + br, k * P:k * P + P], pp[:, u % 2, br, k * P:k * P + P], ident)
                    last.then_inc(S("pa_tr"), 1)

            def p_values(u):
                c, g, qt = u // 8, u // 4 % 2, u % 4
                hd = 4 * g + c
                if u % 8 == 0 and c >= 2:
                    pe.wait_ge(S("pa_out"), c - 1)
                pe.wait_ge(S("pa_trc"), 2 * u + 2)
                out = ps[64 * g:64 * g + 64, 6 + c % 2, qt * P:qt * P + P]
                cols = slice(64 * g, 64 * g + 64)
                mm(out, vcp4[:, qt, cols], pct[:, hd // 4, (hd % 4) * P:(hd % 4) * P + P], True, False)
                for br in range(2):
                    for k in range(qt + 1):
                        last = mm(out, vnat[:, br, k, cols], ppt[:, u % 2, br, k * P:k * P + P], False,
                                  br == 1 and k == qt)
                last.then_inc(S("pa_pv"), 1)

            for u in range(34):
                if u < 32:
                    p_scores(u)
                if 1 <= u <= 32:
                    p_turn(u - 1)
                if u >= 2:
                    p_values(u - 2)

            pe.wait_ge(S("pa_out"), 4)
            pe.wait_ge(S("qbd_ready"), 1)
            opened = set()

            def to_rows(b, probs, values, stop=False, selected=False):
                bank, at = (6, 256) if selected else (7, 256 + P * (b // 4))
                ins = mm(ps[32 * (b % 4):32 * (b % 4) + 32, bank, at:at + P], probs, values, (b, selected) not in opened, stop,
                         skip_group_check=True)
                opened.add((b, selected))
                return ins

            for hb in range(2):
                for j in range(4):
                    b = 4 * hb + j
                    last = mm(ps[32 * j:32 * j + 32, 4, 0:NSUB], qbd[:, 32 * b:32 * b + 32], kstore[:, b, :], True, True)
                last.then_inc(S("sc_sc"), 1)
                wk = tile_in(pe, "win", hb, "k", 0)
                if hb:
                    pe.wait_ge(S("sl_ev"), 32)
                for j in range(4):
                    b = 4 * hb + j
                    mm(ps[32 * j:32 * j + 32, 2, :], qbd[:, 32 * b:32 * b + 32], wk[:, j * 512:j * 512 + 512], True, True)
                rows4 = qbd[:, 128 * hb:128 * hb + 128]
                mm(ps[:, 3, 0:TS], rows4, big[:, KWI, TP:T], True, True).then_inc(S("sw_sc"), 1)
                pe.wait_ge(S("sc_norm"), hb + 1)
                if hb:
                    pe.wait_ge(S("spn_trc"), 1)
                mm(ps[:, 5, 0:264], C("heads"), pce, True, True).then_inc(S("sc_imp"), 1)
                if hb:
                    pe.wait_ge(S("sp_trc"), 8)
                for k in range(33):
                    n = 32 * hb + k
                    if k == 12:
                        pe.wait_ge(S("sc_gate"), hb + 1)
                        for kt in range(2):
                            last = pe.transpose(ps[:, 6, kt * P:kt * P + P], pce[:, 1 + kt * P:1 + kt * P + P], ident)
                        last.then_inc(S("sc_tr"), 1)
                        pe.wait_ge(S("sw_norm"), hb + 1)
                        for kt in range(4):
                            pe.transpose(ps[:, 4, kt * P:kt * P + P], swin[:, kt * P:kt * P + P], ident)
                        pe.transpose(ps[0:TS, 5, 384:512], swin[:, 512:544], ident).then_inc(S("sw_tr"), 1)
                    if k == 14:
                        pe.wait_ge(S("sc_trc"), hb + 1)
                        for j in range(4):
                            b = 4 * hb + j
                            for kt in range(2):
                                to_rows(b, pst2[:, kt * P + 32 * j:kt * P + 32 * j + 32], vstore[:, b, kt * P:kt * P + P])
                        wv = tile_in(pe, "win", hb, "v", 0)
                        pe.wait_ge(S("sw_trc"), 2 * (hb + 1))
                        for j in range(4):
                            b = 4 * hb + j
                            to_rows(b, pwn[:, 32 * j:32 * j + 32], vnew[:, P:2 * P])
                            for kt in range(4):
                                last = to_rows(b, pwt[:, kt * P + 32 * j:kt * P + 32 * j + 32],
                                               wv[:, j * 512 + kt * P:j * 512 + kt * P + P], kt == 3)
                        last.then_inc(S("sw_pv"), 1)
                    if k < 32:
                        if k % 4 == 0:
                            kt_ = tile_in(pe, "slc", 4 * hb + k // 8, "k", k // 4 % 2)
                        if n >= 2:
                            pe.wait_ge(S("kt_trc"), n - 1)
                        for r in range(4):
                            at = (4 * (k % 4) + r) * P
                            last = pe.transpose(ps[:, n % 2, r * P:r * P + P], kt_[:, at:at + P], ident)
                        last.then_inc(S("kt_tr"), 1)
                    if k:
                        n -= 1
                        j = (k - 1) // 8
                        pe.wait_ge(S("kt_trc"), n + 1)
                        if k == 1:
                            pe.wait_ge(S("sw_cp"), hb + 1)
                            pe.wait_ge(S("sw_new"), hb + 1)
                        if n >= 2:
                            pe.wait_ge(S("sl_ev"), n - 1)
                        b = 4 * hb + j
                        mm(ps[32 * j:32 * j + 32, 2 + n % 2, :], qbd[:, 32 * b:32 * b + 32], ktb[:, n % 2, :],
                           True, True).then_inc(S("kt_sc"), 1)
                mm(ps[:, 4, 0:TS], rows4, big[:, KSL, TP:T], True, True).then_inc(S("sl_new"), 1)
                for k in range(8):
                    if k >= 2:
                        pe.wait_ge(S("sp_trc"), 8 * hb + k - 1)
                    pe.wait_ge(S("sx_exp"), 9 * hb + k + 1)
                    for r in range(4):
                        at = (4 * k + r) * P
                        last = pe.transpose(ps[:, k % 2, r * P:r * P + P], sslc[:, at:at + P], ident)
                    last.then_inc(S("sp_tr"), 1)
                pe.wait_ge(S("sx_exp"), 9 * (hb + 1))
                pe.transpose(ps[0:TS, 5, 0:P], sslc[:, PAST:PAST + TS], ident).then_inc(S("spn_tr"), 1)
                pe.wait_ge(S("sp_trc"), 8 * (hb + 1))
                pe.wait_ge(S("spn_trc"), hb + 1)
                for j in range(4):
                    b = 4 * hb + j
                    for hh in range(2):
                        vt = tile_in(pe, "slc", b, "v", hh)
                        for r in range(16):
                            at = (16 * hh + r) * P + 32 * j
                            last = to_rows(b, spt[:, at:at + 32], vt[:, r * P:r * P + P], selected=True)
                        last.then_inc(S("sv_used"), 1)
                    last = to_rows(b, spn[:, 32 * j:32 * j + 32], vnew[:, 0:P], True, True)
                last.then_inc(S("so_rows"), 1)
                pe.wait_ge(S("so_copied"), hb + 1)
                pe.transpose(ps[:, 7, P * hb:P * hb + P], orow, ident).then_inc(S("so_done"), 1)

            def cross(l):
                for m in range(8):
                    acc_emptied(pe, acc_of(f"xq{l}", m))

                def scores(qt):
                    n = 4 * l + qt
                    if n:
                        pe.wait_ge(S("xp_exp"), 4 * n)
                    for hd in range(4):
                        for dc in range(2):
                            c = 2 * hd + dc
                            last = mm(ps[:, 2 + hd // 2, (hd % 2) * 256:(hd % 2) * 256 + 256],
                                      big[:, c, qt * P:qt * P + P], kstore[:, c, :], dc == 0, dc == 1)
                    last.then_inc(S("xp_sc"), 1)

                def turn(qt):
                    n = 4 * l + qt
                    pe.wait_ge(S("xp_norm"), n + 1)
                    if n:
                        pe.wait_ge(S("xp_trc"), 2 * n)
                    for i in range(8):
                        last = pe.transpose(ps[:, 4 + i // 4, (i % 4) * P:(i % 4) * P + P],
                                            xpp[:, i // 2, (i % 2) * P:(i % 2) * P + P], ident)
                        if i % 4 == 3:
                            last.then_inc(S("xp_tr"), 1)

                def values():
                    pe.wait_ge(S("xp_trc"), 8 * (l + 1))
                    for c in range(8):
                        if 8 * l + c >= 2:
                            pe.wait_ge(S("xo_in"), 8 * l + c - 1)
                        for kt in range(2):
                            last = mm(ps[:, 2 + c % 2, :], vst2[:, kt, c * P:c * P + P], xpt[:, 2 * (c // 2) + kt, :],
                                      kt == 0, kt == 1)
                        last.then_inc(S("xp_pv"), 1)

                def s_values(hb):
                    for j in range(4):
                        b = 4 * hb + j
                        mv = tile_in(pe, f"mem{l}", b, "v", 0)
                        for f in range(2):
                            for kt in range(2):
                                at = kt * P + 32 * (b // 2)
                                last = mm(ps[32 * j:32 * j + 32, 6 * hb + f, :], xst[:, at:at + 32],
                                          mv[:, kt * 1024 + 512 * f:kt * 1024 + 512 * f + 512], kt == 0, kt == 1)
                        last.then_inc(S("mv_used"), 1)

                def s_turn(hb):
                    pe.wait_ge(S("xv_copied_a"), 2 * l + hb + 1)
                    pe.wait_ge(S("xv_copied_v"), 2 * l + hb + 1)
                    for c in range(8):
                        last = pe.transpose(ps[:, 6 * hb + c // 4, (c % 4) * P:(c % 4) * P + P],
                                            xvr[:, hb, c * P:c * P + P], ident)
                    last.then_inc(S("xv_tr"), 1)

                scores(0)
                pe.wait_ge(S("xq_apart"), l + 1)
                for b in range(NB):
                    mk = tile_in(pe, f"mem{l}", b, "k", 0)
                    rows = slice(32 * (b // 2), 32 * (b // 2) + 32)
                    for c in range(8):
                        last = mm(ps[rows, 1, 0:256], xqd[:, b, c, :], mk[:, c * 256:c * 256 + 256],
                                  b % 2 == 0 and c == 0, b % 2 == 1 and c == 7)
                    last.then_inc(S("mk_used"), 1)
                scores(1)
                turn(0)
                pe.wait_ge(S("xs_norm"), l + 1)
                for kt in range(2):
                    last = pe.transpose(ps[:, 0, 256 + kt * P:256 + kt * P + P], xsp[:, kt * P:kt * P + P], ident)
                last.then_inc(S("xs_tr"), 1)
                pe.wait_ge(S("xs_trc"), l + 1)
                s_values(0)
                scores(2)
                turn(1)
                s_turn(0)
                scores(3)
                turn(2)
                s_values(1)
                turn(3)
                s_turn(1)
                pe.wait_ge(S("xp_exp"), 16 * (l + 1))
                values()
                pe.wait_ge(S("xo_in"), 8 * (l + 1))

            def layer_end(l):
                linear(f"w_out{l}", hr, mixr, ("mix_hi", "mix_lo", 16 * l))
                stats(f"pmix{l}")
                pe.wait_ge(S("mem_lo"), l + 1)
                b0, g0 = WSEG[f"mk{l}"][0], ACC[f"mk{l}"]
                with pe.Fori(0, 2) as i:
                    for j in range(4):
                        acc_free(pe, g0 + j, i)
                        pe.wait_ge(S("w_lo"), 4 * i + (NSPLIT[b0 + j] + 1))
                        _, wl, wh = block_at(b0 + j, KB)
                        for k in range(8):
                            for wt, src, p_ in ((wh, memhi, 0), (wh, memlo, 1), (wl, memhi, 2)):
                                last = mm(ps[:, 2 * ((g0 + j) % 4), 0:NMEM], wt[:, k * P:k * P + P], src[:, k, :],
                                          k == 0 and p_ == 0, k == 7 and p_ == 2)
                        last.then_inc(ready[(g0 + j) % 4], 1)
                b0, g0 = WSEG[f"mv{l}"][0], ACC[f"mv{l}"]
                for m in range(8):
                    g = g0 + m // 4
                    if m % 4 == 0:
                        acc_free(pe, g)
                    pe.wait_ge(S("w_lo"), NSPLIT[b0 + m] + 1)
                    _, wl, wh = block_at(b0 + m, KB)
                    for k in (2 * (m % 4), 2 * (m % 4) + 1):
                        at = slice((k % 2) * 512, (k % 2) * 512 + 512)
                        for kt in range(2):
                            for wt, src, p_ in ((wh, memhi, 0), (wl, memhi, 1), (wh, memlo, 2)):
                                last = mm(ps[:, 2 * (g % 4) + kt, :], src[:, k, kt * P:kt * P + P], wt[:, at],
                                          k == 0 and p_ == 0, k == 7 and p_ == 2, skip_group_check=True)
                    last.then_inc(*((ready[g % 4], 1) if m % 4 == 3 else (S("part_used"), 1)))
                linear(f"xq{l}", hr, yr, ("xg_ready", "x_lo", 8 * 3 * l))
                cross(l)
                linear(f"xo{l}", hr, mixr, ("mix_hi", "mix_lo", 16 * l + 8))
                stats(f"pxat{l}")
                linear(f"ffn{l}", hr, yr, ("xg_ready", "x_lo", 8 * (3 * l + 1)))
                b0, g0 = WSEG[f"down{l}"][0], ACC[f"down{l}"]
                for m in range(8):
                    acc_free(pe, g0 + m)
                    for q in range(DB):
                        b = b0 + DB * m + q
                        last = chunk(g0 + m, b, hidhi, big_r, 0, tiles_of(b), KB * q, FC, None if m else ("hid_lo", FC * l))
                        last.then_inc(*((ready[(g0 + m) % 4], 1) if q == DB - 1 else (S("part_used"), 1)))
                stats(f"pffn{l}")

            pe.wait_ge(S("so_out"), 8)
            layer_end(0)

            linear("w_in1a", hr, yr, ("xg_ready", "x_lo", 16))
            for m in range(8):
                pe.wait_ge(S("xf_ready"), 2 * (m // 2) + 2)
                for k in range(2):
                    g = ACC["lru"] + 2 * m + k
                    b = WSEG["lru"][0] + m // 2
                    acc_free(pe, g)
                    plain(g, b, mix[:, m // 2 * 2:m // 2 * 2 + 2, :], 2, (2 * m + k) * 2 % 8, 2).then_inc(ready[g % 4], 1)
            linear("w_in1b", hr, yr)
            layer_end(1)


def _chunks(x):
    return np.ascontiguousarray(x.T.reshape(-1, P, x.shape[0]).transpose(1, 0, 2))


def _blocks(w, tiles):
    k, n = w.shape
    t = w.reshape(k // P, P, n // P, P).transpose(2, 0, 1, 3).reshape(-1, tiles, P, P)
    return np.ascontiguousarray(t.transpose(0, 2, 1, 3).reshape(-1, P, tiles * P))


def kernel(**inputs):
    import concourse.bacc as bacc
    from concourse.bass_utils import run_bass_kernel_spmd

    v = {k: np.asarray(t) for k, t in inputs.items()}
    arr = {}
    arr["xp"] = _chunks(v["x_prompt"][0])
    arr["xs"] = _chunks(v["x_sample"].reshape(TS, D))
    arr["mem"] = _chunks(v["mem_prompt"][0])
    past = v["state_pool"][0].transpose(2, 0, 1)
    past = np.pad(past, ((0, 0), (0, 0), (0, 4))).reshape(4, P, NB * 19)
    arr["poolold"] = np.ascontiguousarray(v["state_pool"][0, :, NT:]).reshape(P, -1)
    arr["poolpast"] = np.ascontiguousarray(past.transpose(1, 0, 2))
    for n, k in (("cmpk", "cache_cmp_k"), ("cmpv", "cache_cmp_v"), ("slck", "cache_slc_k"), ("slcv", "cache_slc_v")):
        arr[n] = np.ascontiguousarray(v[k]).reshape(-1, SUB * P)
    wk = v["cache_win_k"][0].reshape(NB, 512, P)
    wv = v["cache_win_v"][0].reshape(NB, 512, P)
    arr["winold_k"] = np.ascontiguousarray(wk[:, 4:]).reshape(P, -1)
    arr["winold_v"] = np.ascontiguousarray(wv[:, 4:]).reshape(P, -1)
    arr["wink"] = np.ascontiguousarray(wk.transpose(2, 0, 1).reshape(P, 2, 4 * 512).transpose(1, 0, 2))
    arr["winv"] = np.ascontiguousarray(
        wv.reshape(2, 4, 4, P, P).transpose(0, 3, 1, 2, 4).reshape(2, P, 4 * 512))
    arr["memk"] = np.ascontiguousarray(
        v["cache_mem_k"].reshape(2, NB, NMEM, 8, P).transpose(0, 1, 4, 3, 2).reshape(2, NB, P, 2048))
    arr["memv"] = np.ascontiguousarray(
        v["cache_mem_v"].reshape(2, NB, 2, P, D).transpose(0, 1, 3, 2, 4).reshape(2, NB, P, 2048))
    pt = v["page_table"].reshape(NB, 2, 16).astype(np.int32)
    arr["pages"] = np.ascontiguousarray(np.repeat(pt, 8, axis=2).transpose(2, 0, 1).reshape(P, 16))
    arr["const"] = CONSTANTS
    cols = [v["norm_gain"].reshape(96, P), v["mem_norm_gain"].reshape(16, P), v["pool_scale"].reshape(4, P),
            v["conv_w"].reshape(32, P), v["conv_b"].reshape(8, P), v["lru_ba"].reshape(8, P),
            v["lru_bx"].reshape(8, P), v["lru_lambda"].reshape(8, P)]
    arr["param"] = np.ascontiguousarray(np.concatenate(cols, axis=0).T)
    arr["poolw"] = np.ascontiguousarray(v["pool_w"][0].transpose(1, 0, 2))
    bd = np.zeros((P, 2, P), np.float32)
    for g in range(2):
        bd[64 * g:64 * g + 64, 0, 64 * g:64 * g + 64] = v["w_cmp_k"][0, g]
        bd[64 * g:64 * g + 64, 1, 64 * g:64 * g + 64] = v["w_cmp_v"][0, g]
    arr["wcmp"] = bd
    arr["lruh"] = np.ascontiguousarray(v["state_lru_h"][0].reshape(NB, 8, P).transpose(2, 1, 0))
    lc = np.pad(v["state_lru_conv"][0].transpose(2, 0, 1), ((0, 0), (0, 0), (0, 4)))
    arr["lruconv"] = np.ascontiguousarray(lc.reshape(8, P, NB * 7).transpose(1, 0, 2))
    wi = v["w_in_even"][0]
    q = wi[:, 512:1024].reshape(D, 2, 4, 64).transpose(0, 2, 1, 3).reshape(D, 512)
    wi = np.pad(np.concatenate([wi[:, :512], q, wi[:, 1024:]], axis=1), ((0, 0), (0, NIN * P - wi.shape[1])))
    wo = v["w_out_even"][0]
    wo = np.concatenate([wo[:512], wo[512:].reshape(2, 4, 64, D).transpose(1, 0, 2, 3).reshape(512, D)], axis=0)
    wts = {"w_in": _blocks(wi, 8), "w_out0": _blocks(wo, 8), "w_in1a": _blocks(v["w_in_odd"][0][:, :D], 8),
           "w_in1b": _blocks(v["w_in_odd"][0][:, D:], 8), "w_out1": _blocks(v["w_out_odd"][0], 8)}
    for l in range(2):
        for n, k in (("xq", "w_xq"), ("mk", "w_xk"), ("xo", "w_xo")):
            wts[f"{n}{l}"] = _blocks(v[k][l], 8)
        xv = v["w_xv"][l].reshape(4, 2, P, 2, 512).transpose(3, 0, 2, 1, 4)
        wts[f"mv{l}"] = np.ascontiguousarray(xv).reshape(8, P, 1024)
        gu = np.stack([v["w_ffn_gate"][l].reshape(D, FC, P), v["w_ffn_up"][l].reshape(D, FC, P)], axis=2)
        wts[f"ffn{l}"] = _blocks(gu.reshape(D, 2 * DFF), 8)
        dn = np.pad(v["w_ffn_down"][l], ((0, DB * KB * P - DFF), (0, 0)))
        wts[f"down{l}"] = _blocks(dn, KB)
    ax = np.stack([v["lru_wa"][0], v["lru_wx"][0]], axis=0).reshape(2, 4, 2, P, 2, P)
    ax = ax.transpose(1, 4, 0, 2, 3, 5).reshape(4, 8, P, P)
    wts["lru"] = np.ascontiguousarray(ax.transpose(0, 2, 1, 3).reshape(4, P, 8 * P))
    outs = {
        "yp": [P, KC, TP], "ys": [P, KC, TS], "pool": [P, 4, 15 + TS], "poolold": [P, NB * 11 * 4], "kv": [6, P, T],
        "wink_s": [P, NB * 508], "winv_s": [P, NB * 508], "memk": [2, P, 8, NMEM], "memv": [2, P, 8, 256],
        "conv_p": [P, 8, 3], "conv_s": [P, 8, NB, 3], "lru_h": [P, 8, 9],
    }
    nc = bacc.Bacc("TRN2", target_bir_lowering=False, num_devices=1)
    feed = {f"in_{n}": t for n, t in arr.items()} | {f"w_{n}": t for n, t in wts.items()}
    a = {n: nc.dram_tensor(f"in_{n}", t.shape, mybir.dt.from_np(t.dtype), kind="ExternalInput").ap() for n, t in arr.items()}
    w = {n: nc.dram_tensor(f"w_{n}", t.shape, F32, kind="ExternalInput").ap() for n, t in wts.items()}
    o = {n: nc.dram_tensor(f"out_{n}", s, F32, kind="ExternalOutput").ap() for n, s in outs.items()}
    decoder_step(nc, a, w, o)
    r = run_bass_kernel_spmd(nc, [feed], core_ids=[0]).results[0]
    r = {n: np.asarray(r[f"out_{n}"]) for n in outs}

    def rows(t):
        return t.transpose(2, 1, 0).reshape(t.shape[2], -1)

    yp = rows(r["yp"]).reshape(1, TP, D)
    ys = rows(r["ys"]).reshape(NB, NT, D)
    pool = rows(r["pool"])
    pool_p = pool[:15].reshape(1, 1, 15, 512)
    pool_new = pool[15:].reshape(1, NB, NT, 512)
    past_rows = r["poolold"].reshape(1, NB, 11, 512)
    pool_s = np.concatenate([past_rows, pool_new], axis=2)
    kv = [rows(r["kv"][i][:, None, :]) for i in range(6)]
    kvp = [t[:TP].reshape(1, 1, TP, 2, 64) for t in kv]
    kvs = [t[TP:].reshape(NB, 1, NT, 2, 64) for t in kv]
    win = []
    for i, n in ((4, "wink_s"), (5, "winv_s")):
        win.append(kv[i][:TP].reshape(1, 1, TP, 2, 64))
        old = r[n].reshape(1, NB, 508, 2, 64)
        win.append(np.concatenate([old, kv[i][TP:].reshape(1, NB, NT, 2, 64)], axis=2))
    lh = r["lru_h"].transpose(2, 1, 0).reshape(9, D)
    conv_p = r["conv_p"].transpose(2, 1, 0).reshape(1, 1, 3, D)
    conv_s = r["conv_s"].transpose(2, 3, 1, 0).reshape(1, NB, 3, D)
    mk = r["memk"].transpose(0, 3, 2, 1).reshape(2, 1, NMEM, 4, 256)
    mv = r["memv"].reshape(2, P, 2, D).transpose(0, 2, 1, 3).reshape(2, 1, NMEM, 4, 256)
    return (yp, ys, pool_p, pool_s, kvp[0], kvs[0], kvp[1], kvs[1], kvp[2], kvs[2], kvp[3], kvs[3],
            win[0], win[1], win[2], win[3], lh[:1].reshape(1, 1, D), lh[1:].reshape(1, NB, D), conv_p, conv_s, mk, mv)
```
